# Optimizing a Trainium2 kernel written in Bass

```python
import jax, jax.numpy as jnp
from jax import lax
import numpy as np

D_MODEL = 1024
BATCH = 1
SEQ = 512
DEPTH = 2

GRID_W = 64
CTX_LEN = 256
HEAD_DIM = 64
N_Q_HEADS = 8
N_KV_HEADS = 2
Q_GROUP = N_Q_HEADS // N_KV_HEADS
ATTN_W = N_Q_HEADS * HEAD_DIM
KV_W = N_KV_HEADS * HEAD_DIM
POOL_WINDOWS = (2, 4, 8, 16)
N_POOL_GROUPS = len(POOL_WINDOWS)
POOL_W = D_MODEL // 2
POOL_GROUP_W = POOL_W // N_POOL_GROUPS
CONV_W = D_MODEL // 2
CONV_K = 31
N_BRANCHES = 3
Q_END = ATTN_W
K_END = Q_END + KV_W
V_END = K_END + KV_W
P_END = V_END + POOL_W
C_END = P_END + 2 * CONV_W
IN_W = C_END + N_BRANCHES * D_MODEL
D_FF = -(-8 * D_MODEL // (3 * 256)) * 256
Q_BLOCK = 128
ROPE_THETA = 10000.0
EPS = 1e-6

kernel_name = 'hybrid_gqa_pool_conformer_prefix_dit'

def rmsnorm(x, g):
    xf = x.astype(jnp.float32)
    y = xf * lax.rsqrt(jnp.mean(xf * xf, axis=-1, keepdims=True) + EPS)
    return (y * g.astype(jnp.float32)).astype(x.dtype)

def layernorm(x, g, b):
    xf = x.astype(jnp.float32)
    mu = jnp.mean(xf, axis=-1, keepdims=True)
    var = jnp.mean(jnp.square(xf - mu), axis=-1, keepdims=True)
    y = (xf - mu) * lax.rsqrt(var + EPS)
    return (y * g.astype(jnp.float32) + b.astype(jnp.float32)).astype(x.dtype)

def axial_rope_tables(n_tokens):
    rows = n_tokens // GRID_W
    row = jnp.repeat(jnp.arange(rows), GRID_W).astype(jnp.float32)
    col = jnp.tile(jnp.arange(GRID_W), rows).astype(jnp.float32)
    n_freq = HEAD_DIM // 4
    inv = 1.0 / (ROPE_THETA ** (jnp.arange(n_freq, dtype=jnp.float32) / n_freq))
    ang_r = row[:, None] * inv[None, :]
    ang_c = col[:, None] * inv[None, :]
    return (jnp.cos(ang_r), jnp.sin(ang_r), jnp.cos(ang_c), jnp.sin(ang_c))

def _rotate(u, cos, sin):
    half = u.shape[-1] // 2
    u1, u2 = u[..., :half], u[..., half:]
    cos = cos[None, :, None, :]
    sin = sin[None, :, None, :]
    return jnp.concatenate([u1 * cos - u2 * sin, u2 * cos + u1 * sin], axis=-1)

def apply_axial_rope(x, tabs):
    cos_r, sin_r, cos_c, sin_c = tabs
    xf = x.astype(jnp.float32)
    half = HEAD_DIM // 2
    out = jnp.concatenate([_rotate(xf[..., :half], cos_r, sin_r),
                           _rotate(xf[..., half:], cos_c, sin_c)], axis=-1)
    return out.astype(x.dtype)

def split_heads(u, n_heads):
    return u.reshape(u.shape[:-1] + (n_heads, HEAD_DIM))

def kv_heads(u_kv, k_norm, rope):
    k = rmsnorm(split_heads(u_kv[..., :KV_W], N_KV_HEADS), k_norm)
    v = split_heads(u_kv[..., KV_W:], N_KV_HEADS)
    if rope is not None:
        k = apply_axial_rope(k, rope)
    return k, v

def attention(q, k, v):
    B, L = q.shape[0], q.shape[1]
    nblk = L // Q_BLOCK
    qb = (q * HEAD_DIM ** -0.5).reshape(B, nblk, Q_BLOCK, N_KV_HEADS, Q_GROUP, HEAD_DIM)
    qb = qb.transpose(1, 0, 2, 3, 4, 5)

    def one_block(qi):
        s = jnp.einsum('bqhgd,bshd->bhgqs', qi, k).astype(jnp.float32)
        p = jax.nn.softmax(s, axis=-1).astype(v.dtype)
        return jnp.einsum('bhgqs,bshd->bqhgd', p, v)

    o = lax.map(one_block, qb)
    return o.transpose(1, 0, 2, 3, 4, 5).reshape(B, L, ATTN_W)

def multiscale_pool(u, pool_w, pool_scale):
    B, L, _ = u.shape
    uf = u.astype(jnp.float32)
    cs = jnp.concatenate([jnp.zeros((B, 1, POOL_W), jnp.float32), jnp.cumsum(uf, axis=1)], axis=1)
    t = jnp.arange(L)
    means = []
    for gi, w in enumerate(POOL_WINDOWS):
        lo = jnp.clip(t - w // 2, 0, L)
        hi = jnp.clip(t + w // 2, 0, L)
        seg = cs[:, :, gi * POOL_GROUP_W:(gi + 1) * POOL_GROUP_W]
        cnt = (hi - lo).astype(jnp.float32)[None, :, None]
        means.append((seg[:, hi] - seg[:, lo]) / cnt)
    d = (jnp.concatenate(means, axis=-1) - uf).astype(u.dtype)
    d = d.reshape(B, L, N_POOL_GROUPS, POOL_GROUP_W)
    y = jnp.einsum('blgc,gcd->blgd', d, pool_w).reshape(B, L, POOL_W)
    return y * pool_scale

def conformer_conv(u, conv_dw, conv_b, ln_g, ln_b, w_o):
    a, gt = u[..., :CONV_W], u[..., CONV_W:]
    g = a * jax.nn.sigmoid(gt)
    y = lax.conv_general_dilated(g, conv_dw[:, None, :], window_strides=(1,),
                                 padding=[(CONV_K // 2, CONV_K // 2)],
                                 dimension_numbers=('NWC', 'WIO', 'NWC'),
                                 feature_group_count=CONV_W) + conv_b
    y = jax.nn.silu(layernorm(y, ln_g, ln_b))
    return y @ w_o

def mixer_out(q, k, v, u_pool, u_conv, u_gate, lp):
    ya = attention(q, k, v) @ lp['w_attn_o']
    yb = multiscale_pool(u_pool, lp['pool_w'], lp['pool_scale']) @ lp['w_pool_o']
    yc = conformer_conv(u_conv, lp['conv_dw'], lp['conv_b'], lp['conv_ln_g'], lp['conv_ln_b'], lp['w_conv_o'])
    g = jax.nn.sigmoid(u_gate.reshape(u_gate.shape[:-1] + (N_BRANCHES, D_MODEL)))
    merged = g[..., 0, :] * ya + g[..., 1, :] * yb + g[..., 2, :] * yc
    return merged @ lp['w_out']

def swiglu(h, w_ffn_in, w_ffn_out):
    u = h @ w_ffn_in
    return (jax.nn.silu(u[..., :D_FF]) * u[..., D_FF:]) @ w_ffn_out

def setup_inputs(seed: int = 0) -> dict:
    key = jax.random.key(seed)
    ks = jax.random.split(key, 32)
    f32 = jnp.float32
    D = D_MODEL

    def nrm(k, shape, scale):
        return jax.random.normal(k, shape, f32) * scale

    return {
        'x': nrm(ks[0], (BATCH, SEQ, D), 1.0),
        'c': nrm(ks[1], (BATCH, D), 1.0),
        'ctx': nrm(ks[2], (BATCH, CTX_LEN, D), 1.0),
        'c_ctx': nrm(ks[3], (D,), 1.0),
        'w_ada': nrm(ks[4], (DEPTH, D, 6 * D), 0.5 * D ** -0.5),
        'b_ada': nrm(ks[5], (DEPTH, 6 * D), 0.01),
        'g_pre1': 1.0 + nrm(ks[6], (DEPTH, D), 0.05),
        'g_post1': 1.0 + nrm(ks[7], (DEPTH, D), 0.05),
        'g_pre2': 1.0 + nrm(ks[8], (DEPTH, D), 0.05),
        'g_post2': 1.0 + nrm(ks[9], (DEPTH, D), 0.05),
        'w_in': nrm(ks[10], (DEPTH, D, IN_W), D ** -0.5),
        'q_norm': 1.0 + nrm(ks[11], (DEPTH, HEAD_DIM), 0.05),
        'k_norm': 1.0 + nrm(ks[12], (DEPTH, HEAD_DIM), 0.05),
        'w_attn_o': nrm(ks[13], (DEPTH, ATTN_W, D), ATTN_W ** -0.5),
        'pool_w': nrm(ks[14], (DEPTH, N_POOL_GROUPS, POOL_GROUP_W, POOL_GROUP_W), POOL_GROUP_W ** -0.5),
        'pool_scale': 1.0 + nrm(ks[15], (DEPTH, POOL_W), 0.05),
        'w_pool_o': nrm(ks[16], (DEPTH, POOL_W, D), POOL_W ** -0.5),
        'conv_dw': nrm(ks[17], (DEPTH, CONV_K, CONV_W), CONV_K ** -0.5),
        'conv_b': nrm(ks[18], (DEPTH, CONV_W), 0.01),
        'conv_ln_g': 1.0 + nrm(ks[19], (DEPTH, CONV_W), 0.05),
        'conv_ln_b': nrm(ks[20], (DEPTH, CONV_W), 0.01),
        'w_conv_o': nrm(ks[21], (DEPTH, CONV_W, D), CONV_W ** -0.5),
        'w_out': nrm(ks[22], (DEPTH, D, D), D ** -0.5),
        'w_ffn_in': nrm(ks[23], (DEPTH, D, 2 * D_FF), D ** -0.5),
        'w_ffn_out': nrm(ks[24], (DEPTH, D_FF, D), D_FF ** -0.5),
    }

def reference(x, c, ctx, c_ctx, w_ada, b_ada, g_pre1, g_post1, g_pre2, g_post2, w_in, q_norm, k_norm,
              w_attn_o, pool_w, pool_scale, w_pool_o, conv_dw, conv_b, conv_ln_g, conv_ln_b, w_conv_o,
              w_out, w_ffn_in, w_ffn_out):
    n_lat = x.shape[1]
    rope = axial_rope_tables(n_lat)
    e = ctx
    for i in range(DEPTH):
        last = i == DEPTH - 1
        lp = {'w_attn_o': w_attn_o[i], 'pool_w': pool_w[i], 'pool_scale': pool_scale[i],
              'w_pool_o': w_pool_o[i], 'conv_dw': conv_dw[i], 'conv_b': conv_b[i],
              'conv_ln_g': conv_ln_g[i], 'conv_ln_b': conv_ln_b[i], 'w_conv_o': w_conv_o[i],
              'w_out': w_out[i]}
        mod_x = (jax.nn.silu(c) @ w_ada[i] + b_ada[i])[:, None, :]
        mod_c = (jax.nn.silu(c_ctx) @ w_ada[i] + b_ada[i])[None, None, :]
        sh1, sc1, gt1, sh2, sc2, gt2 = jnp.split(mod_x, 6, axis=-1)
        csh1, csc1, cgt1, csh2, csc2, cgt2 = jnp.split(mod_c, 6, axis=-1)

        hx = rmsnorm(x, g_pre1[i]) * (1.0 + sc1) + sh1
        hc = rmsnorm(e, g_pre1[i]) * (1.0 + csc1) + csh1
        ux = hx @ w_in[i]
        qx = apply_axial_rope(rmsnorm(split_heads(ux[..., :Q_END], N_Q_HEADS), q_norm[i]), rope)
        kx, vx = kv_heads(ux[..., Q_END:V_END], k_norm[i], rope)
        if last:
            uc_kv = hc @ w_in[i][:, Q_END:V_END]
        else:
            uc = hc @ w_in[i]
            uc_kv = uc[..., Q_END:V_END]
        kc, vc = kv_heads(uc_kv, k_norm[i], None)
        k_all = jnp.concatenate([kc, kx], axis=1)
        v_all = jnp.concatenate([vc, vx], axis=1)
        yx = mixer_out(qx, k_all, v_all, ux[..., V_END:P_END], ux[..., P_END:C_END], ux[..., C_END:], lp)
        x_new = x + gt1 * rmsnorm(yx, g_post1[i])
        if not last:
            qc = rmsnorm(split_heads(uc[..., :Q_END], N_Q_HEADS), q_norm[i])
            yc = mixer_out(qc, kc, vc, uc[..., V_END:P_END], uc[..., P_END:C_END], uc[..., C_END:], lp)
            e = e + cgt1 * rmsnorm(yc, g_post1[i])
        x = x_new

        hx2 = rmsnorm(x, g_pre2[i]) * (1.0 + sc2) + sh2
        x = x + gt2 * rmsnorm(swiglu(hx2, w_ffn_in[i], w_ffn_out[i]), g_post2[i])
        if not last:
            hc2 = rmsnorm(e, g_pre2[i]) * (1.0 + csc2) + csh2
            e = e + cgt2 * rmsnorm(swiglu(hc2, w_ffn_in[i], w_ffn_out[i]), g_post2[i])
    return x


_drawn_inputs = setup_inputs


def setup_inputs(seed=0):
    import zlib

    import numpy as np

    out = dict(_drawn_inputs(seed))
    spreads = {}
    factors = {'ctx': 4.27,
     'b_ada': 2.752,
     'g_post1': 2.727,
     'g_post2': 2.798,
     'q_norm': 8.0,
     'k_norm': 8.0,
     'pool_scale': 3.311,
     'conv_b': 8.0,
     'conv_ln_g': 4.166,
     'conv_ln_b': 28.013}
    for name, (base, spread) in spreads.items():
        noise = np.random.default_rng([zlib.crc32(name.encode()), seed]).standard_normal(out[name].shape)
        drawn = base * np.exp(spread * noise) if base else spread * noise
        out[name] = __import__('jax').numpy.asarray(drawn.astype(out[name].dtype))
    for name, factor in factors.items():
        out[name] = (out[name] * factor).astype(out[name].dtype)
    return out
```

```python
from contextlib import ExitStack, contextmanager

import numpy as np
import concourse.bass as bass
from concourse import mybir

F32 = mybir.dt.float32
F32R = mybir.dt.float32r
ACT = mybir.ActivationFunctionType
ALU = mybir.AluOpType
AX = mybir.AxisListType

P = 128
D = 1024
KT = D // P
CTX, LAT = 256, 512
T = CTX + LAT
LAYERS = 2
HD = 64
HEADS = 8
KV = 2
EPS = 1e-6
BR = 4
TAPS = 31
HALF = TAPS // 2
WIN = (2, 4, 8, 16)
D_FF = 2816
FT = D_FF // P
GROUPS = (8, 8, 6)
RING = 4
RAW = 2
ADA = 48

S_K, S_V, S_Q, S_CONV, S_P0, S_POOL, S_P1, S_P2, S_OUT, S_FF = 0, 2, 4, 8, 16, 32, 40, 56, 72, 80
FF_IN, FF_OUT = [], []
_s = S_FF
for _n in GROUPS:
    FF_IN.append(_s)
    FF_OUT.append(_s + 2 * _n)
    _s += 2 * _n + KT
SLABS = _s
POOL_ORDER = (("u", 0), ("u", 1), ("w", 0), ("u", 2), ("w", 1), ("u", 3), ("w", 2), ("w", 3))

ADA_PLAN = [(0, 0, 0), (0, 1, 0), (0, 2, S_Q + 1), (0, 3, S_Q + 2), (0, 4, S_Q + 3), (0, 5, S_Q + 4),
            (1, 0, S_FF), (1, 1, S_FF), (1, 2, SLABS), (1, 3, SLABS), (1, 4, SLABS + S_Q + 1),
            (1, 5, SLABS + S_FF)]

V_BADA, V_GPRE1, V_GPOST1, V_GPRE2, V_GPOST2 = 0, 48, 56, 64, 72
V_QN, V_KN, V_PS, V_DW = 80, 81, 82, 86
V_CB = V_DW + BR * TAPS
V_LG, V_LB = V_CB + BR, V_CB + 2 * BR
NV = V_LB + BR
C_ID, C_ONE, C_BLK, C_ROT, C_EDGE, C_COS, C_SIN = 0, 128, 256, 384, 512, 576, 576 + T
NC = C_SIN + T

GC, GL = HALF, HALF + CTX + HALF
GW = GL + LAT + HALF
CW = GW - 2 * HALF
UC, UL = 8, 8 + CTX + 8
UW = UL + LAT + 8


def slab_blocks(s):
    if S_P0 <= s < S_POOL or S_P1 <= s < S_OUT:
        return 4 if s % 2 else 8
    if S_POOL <= s < S_P1:
        return 1 if POOL_ORDER[s - S_POOL][0] == "w" else 8
    for g, n in enumerate(GROUPS):
        if FF_OUT[g] <= s < FF_OUT[g] + KT:
            return n
    return 8


def build(nc, io, known):
    noted, strides = {}, {}
    old_marks, old_strides = known

    class Tally:

        def __init__(self, name):
            self.name, self.sem, self.n = name, ctx.enter_context(nc.semaphore(name)), 0
            self.start, self.key, self.i = None, None, None
            tallies[name] = self

        def up(self, *name):
            self.n += 1
            if name:
                assert name not in noted, name
                noted[name] = (self.name, self.n, self.key)
            return self.sem, 1

        def ago(self, back=0):
            v = self.n - back
            if self.key is None:
                return self.sem, max(v, 1)
            return self.sem, self.i * old_strides.get((self.key, self.name), 0) + max(v, 1)

    tallies = {}

    def seen(*name, i=None, back=0):
        if name not in old_marks:
            assert not old_marks, name
            return tallies["rounded"].sem, 1
        tally, value, key = old_marks[name]
        if key is None or i is None:
            assert key is None or back == 0, name
            return tallies[tally].sem, value
        stride = old_strides[(key, tally)]
        return tallies[tally].sem, i * stride + (value - back * stride)

    @contextmanager
    def repeat(eng, count, *key):
        with eng.Fori(0, count) as i:
            for t in tallies.values():
                t.start = t.n
            mine = (eng_name[id(eng)],) + key
            for t in tallies.values():
                t.key, t.i = mine, i
            yield i
            for t in tallies.values():
                d = t.n - t.start
                strides[(mine, t.name)] = d
                t.n += d * (count - 1)
                t.key = t.i = None

    eng_name = {}

    ctx = ExitStack()
    with ctx:
        def sb(name, shape, dt=F32):
            return ctx.enter_context(nc.sbuf_tensor(name, [P] + shape, dt))

        def overlay(name, size, *layouts):
            out = []
            for layout in layouts:
                with ExitStack() as open_:
                    for n, shape, dt in layout:
                        out.append(open_.enter_context(nc.sbuf_tensor(n, [P] + shape, dt)))
            sb(name, [size // 4])
            return out

        x, pt0h, pt0l, cg, cacc, ct, ml = overlay(
            "region_x", 4 * BR * (GW + CW) + 32,
            [("x", [KT, T], F32)],
            [("pt0h", [6, LAT], F32R), ("pt0l", [6, LAT], F32R)],
            [("conv_in", [BR, GW], F32), ("conv_acc", [BR, CW], F32)],
            [("conv_norm", [BR, T], F32)],
            [("merged_l", [KT, T], F32R)])
        pt1h, pt1l, acc = overlay(
            "region_acc", 4 * KT * T,
            [("pt1h", [6, LAT], F32R), ("pt1l", [6, LAT], F32R)],
            [("acc", [KT, T], F32)])
        half = 4 * KT * T
        (qs, kk, vh, vl, pr, o_raw, pad1, oh, ol, yph, ypl, dh, dl, pad2, ych, ycl, mh, midh, midl,
         ns) = overlay(
            "region_m", 2 * half,
            [("q_split", [HEADS, T], F32R), ("k_split", [2 * KV, T], F32R), ("v_h", [6, P], F32R),
             ("v_l", [6, P], F32R), ("probs", [2, T], F32)],
            [("o_raw", [BR, 2 * T], F32)],
            [("pad1", [half // 4], F32), ("o_h", [BR, T], F32R), ("o_l", [BR, T], F32R)],
            [("pool_h", [BR, T], F32R), ("pool_l", [BR, T], F32R), ("dev_h", [T], F32R),
             ("dev_l", [T], F32R)],
            [("pad2", [half // 4], F32), ("conv_h", [BR, T], F32R), ("conv_l", [BR, T], F32R)],
            [("merged_h", [KT, T], F32R)],
            [("mid_h", [KT, T], F32R), ("mid_l", [KT, T], F32R)],
            [("norm_tmp", [7, T], F32)])
        hh, hl = sb("h_h", [KT, T], F32R), sb("h_l", [KT, T], F32R)
        raw = sb("w_raw", [RAW, KT * P])
        wh, wl = sb("w_h", [RING, KT * P], F32R), sb("w_l", [RING, KT * P], F32R)
        ada_raw = sb("ada_raw", [2, KT * P])
        t1, t2, t3 = (sb(n, [800]) for n in ("t1", "t2", "t3"))
        const = sb("const", [NC])
        vec = sb("vec", [LAYERS, NV])
        cvec, silu_c = sb("cvec", [KT, 2]), sb("silu_c", [KT, 2])
        mod = sb("mod", [LAYERS, ADA, 2])
        gain = sb("gain", [LAYERS, 4, KT, 2])
        ust = sb("unit_stats", [4, 8])
        ps = ctx.enter_context(nc.psum_tensor("ps", [P, 8, 512], F32))
        psf = ps[:].rearrange("p b n -> p (b n)")
        A = [psf[:, 0:1024], psf[:, 1024:2048]]
        B = psf[:, 2048:3072]
        O = psf[:, 3072:3584]
        DD = psf[:, 3584:4096]

        ident, ones = const[:, C_ID:C_ID + P], const[:, C_ONE:C_ONE + P]
        blk, rot = const[:, C_BLK:C_BLK + P], const[:, C_ROT:C_ROT + P]
        cos, sin = const[:, C_COS:C_COS + T], const[:, C_SIN:C_SIN + T]

        def sem(name):
            return ctx.enter_context(nc.semaphore(name))

        w_loaded = [sem(f"w_loaded{k}") for k in range(RAW)]
        ada_loaded = [sem(f"ada_loaded{k}") for k in range(2)]
        const_loaded, x_loaded, x_stored, out_stored = (
            sem(n) for n in ("const_loaded", "x_loaded", "x_stored", "out_stored"))
        rounded, split, used = Tally("rounded"), sem("split"), sem("used")
        ada_used = Tally("ada_used")
        pe_done = Tally("pe_done")
        act_tmp = Tally("act_tmp")
        act_hi = Tally("act_hi")
        act_out = Tally("act_out")
        dve_tmp = Tally("dve_tmp")
        dve_lo = Tally("dve_lo")
        dve_out = Tally("dve_out")
        dve_tap = Tally("dve_tap")

        def lo_of(ly):
            return 0 if ly == 0 else CTX

        def chunks(lo):
            return ([(0, CTX, 1)] if lo == 0 else []) + [(CTX, T, 0)]

        def at(w, c0, c1):
            return w[:, 256 + c0:256 + c1]

        def units(ly):
            out, b = [], 0
            for h in range(HEADS):
                for q0, nq, nk in ([(CTX, 4, T)] + ([(0, 2, CTX)] if ly == 0 else [])):
                    out += [(h, q0, nk, q, nq, b) for q in range(nq)]
                    b += 1
            return out

        block = ctx.enter_context(nc.Block())

        @block.sync
        def _(sp):
            eng_name[id(sp)] = "sp"
            total = LAYERS * SLABS
            ada_n = [0]

            def load(s, blocks, i=None):
                if s >= RAW or i is not None:
                    sp.wait_ge(split, s - RAW + 1 if i is None else i * RING + (s - RAW + 1))
                src = io["w"][s] if i is None else io["w"][bass.ds(i * RING + s, 1)].rearrange(
                    "a p n -> (a p) n")
                sp.dma_start(raw[:, s % RAW, 0:blocks * P], src[:, 0:blocks * P]).then_inc(
                    w_loaded[s % RAW], 16)

            def load_ada(ly, g):
                for n in range(8 * g, 8 * g + 8):
                    k = ada_n[0]
                    if k >= 2:
                        sp.wait_ge(*seen("ada", k - 2))
                    sp.dma_start(ada_raw[:, k % 2, :], io["ada"][ly, n]).then_inc(ada_loaded[k % 2], 16)
                    ada_n[0] += 1

            def load_run(a, b):
                s = a
                while s < b:
                    pat = [slab_blocks((s + k) % SLABS) for k in range(RING)]
                    n = 0
                    while s % RING == 0 and s + RING * (n + 1) <= b and pat == [
                            slab_blocks((s + RING * n + k) % SLABS) for k in range(RING)]:
                        n += 1
                    if n >= 2 and s >= RAW:
                        with sp.Fori(0, n) as i:
                            for k in range(RING):
                                load(s + k, pat[k], i)
                        s += RING * n
                    else:
                        load(s, pat[0])
                        s += 1

            at_s = 0
            for ly, g, before in ADA_PLAN:
                stop = 0 if before == 0 else min(before + RING - 1, total)
                load_run(at_s, stop)
                at_s = stop
                load_ada(ly, g)
            load_run(at_s, total)

        @block.gpsimd
        def _(pool):
            with pool.Fori(0, LAYERS * SLABS // RING) as i:
                for k in range(RING):
                    pool.wait_ge(rounded.sem, i * RING + (k + 1))
                    nc.gpsimd.tensor_tensor(wl[:, k, :], raw[:, k % RAW, :], wh[:, k, :],
                                            ALU.subtract).then_inc(split, 1)

        @block.tensor
        def _(pe):
            eng_name[id(pe)] = "pe"
            last_use = {}
            ada_n = [0]

            def take(w, *name):
                if w in last_use:
                    pe.wait_ge(*seen("free", *last_use[w]))
                last_use[w] = name

            def gemm(out, slabs, xh, xl, cols, i=None, k_ready=None, start_k=0, n_k=None):
                kt = 0
                n_k = sum(nb for _, nb in slabs)
                for s, nb in slabs:
                    pe.wait_ge(split, s + 1 if i is None else i * RING + (s + 1))
                    for b in range(nb):
                        if k_ready is not None:
                            pe.wait_ge(*k_ready(kt))
                        for n, (w, m) in enumerate(((wh, xh), (wh, xl), (wl, xh))):
                            for c0, c1, _ in cols:
                                ins = nc.tensor.matmul(
                                    at(out, c0, c1), w[:, s % RING, b * P:(b + 1) * P], m[:, kt, c0:c1],
                                    start=(kt == 0 and n == 0), stop=(kt == n_k - 1 and n == 2))
                        kt += 1
                    ins.then_inc(used, 1)

            def ada(ly, g):
                take("D", "ada", ly, g)
                for t in range(8):
                    k = ada_n[0]
                    pe.wait_ge(ada_loaded[k % 2], 16 * (k // 2 + 1))
                    for b in range(KT):
                        ins = nc.tensor.matmul(DD[:, 2 * t:2 * t + 2], ada_raw[:, k % 2, b * P:(b + 1) * P],
                                               silu_c[:, b, :], start=(b == 0), stop=(b == KT - 1))
                    ins.then_inc(*ada_used.up("ada", k))
                    ada_n[0] += 1

            def sums(mat, src, cols, need, *name):
                take("B", *name)
                pe.wait_ge(*seen(*need))
                for c0, c1, _ in cols:
                    ins = nc.tensor.matmul(at(B, c0, c1), mat, src(c0, c1), start=True, stop=True)
                ins.then_inc(*pe_done.up(*name))

            def t_cols(t):
                return lambda c0, c1: t[:, c0:c1]

            def n_cols(k):
                return lambda c0, c1: ns[:, k, c0:c1]

            pe.wait_ge(const_loaded, 16 * 3)
            pe.wait_ge(*seen("silu"))
            ada(0, 0)
            ada(0, 1)
            for ly in range(LAYERS):
                s0 = ly * SLABS
                lo = lo_of(ly)
                cols, full = chunks(lo), chunks(0)

                def pre_ready(k):
                    return seen("hl", ly, "pre1", k)

                sums(ones, n_cols(6), full, ("sqadd", ly, "pre1", KT - 1), "stat", ly, "pre1")
                if ly == 1:
                    ada(1, 3)

                tiles = ["k", "v", "q0", "q1", "q2", "q3"]

                def finish(n):
                    c = full if n in "kv" else cols
                    if n == "v":
                        take("B", "vt", ly)
                        pe.wait_ge(*seen("vcopy", ly))
                        for k in range(6):
                            ins = nc.tensor.transpose(at(B, k * P, (k + 1) * P), t1[:, k * P:(k + 1) * P], ident)
                        ins.then_inc(*pe_done.up("vt", ly))
                    else:
                        sums(blk, t_cols(t1), c, ("tsq", ly, n), "stat", ly, n)
                        sums(rot, t_cols(t2), c, ("free", "gemm", ly, n), "rot", ly, n)

                for n, name in enumerate(tiles):
                    w = n % 2
                    take(w, "gemm", ly, name)
                    if name in "kv":
                        s = s0 + (S_K if name == "k" else S_V)
                        gemm(A[w], [(s, 4), (s + 1, 4)], hh, hl, full,
                             k_ready=pre_ready if name == "k" else None)
                    else:
                        gemm(A[w], [(s0 + S_Q + n - 2, 8)], hh, hl, cols)
                        if ly == 0:
                            ada(0, n)
                        elif n == 2:
                            ada(1, 4)
                    if n:
                        finish(tiles[n - 1])
                finish(tiles[-1])

                us = units(ly)

                def scores(u):
                    h, q0, nk, q, nq, b = us[u]
                    take(u % 2, "scores", ly, u)
                    if u == 0:
                        pe.wait_ge(*seen("tile", ly, "k"))
                    if q == 0:
                        pe.wait_ge(*seen("tile", ly, f"q{h // 2}"))
                    ks = [(0, CTX), (CTX, T)] if nk == T else [(0, CTX)]
                    for part in range(2):
                        for c0, c1 in ks:
                            ins = nc.tensor.matmul(
                                at(A[u % 2], c0, c1), qs[:, h, q0 + q * P:q0 + (q + 1) * P],
                                kk[:, 2 * (h // 4) + part, c0:c1], start=(part == 0), stop=(part == 1))
                    ins.then_inc(*pe_done.up("scores", ly, u))

                def transposes(u):
                    h, q0, nk, q, nq, b = us[u]
                    take("B", "pt", ly, u)
                    pe.wait_ge(*seen("normed", ly, u))
                    for k in range(nk // P):
                        ins = nc.tensor.transpose(at(B, k * P, (k + 1) * P), pr[:, u % 2, k * P:(k + 1) * P], ident)
                    ins.then_inc(*pe_done.up("pt", ly, u))

                def values(u):
                    h, q0, nk, q, nq, b = us[u]
                    take("O", "pv", ly, b)
                    if u < 6:
                        pe.wait_ge(*seen("tile", ly, "v"))
                    pe.wait_ge(*seen("free", "pt", ly, u))
                    ph, pl = ((pt0h, pt0l), (pt1h, pt1l))[b % 2]
                    d0 = HD * (h // 4)
                    for k in range(nk // P):
                        for n, (v, p) in enumerate(((vh, ph), (vh, pl), (vl, ph))):
                            ins = nc.tensor.matmul(O[0:HD, 0:nq * P], v[:, k, d0:d0 + HD], p[:, k, 0:nq * P],
                                                   start=(k == 0 and n == 0), stop=(k == nk // P - 1 and n == 2))
                    ins.then_inc(*pe_done.up("pv", ly, b))

                for u in range(len(us) + 2):
                    if u < len(us):
                        scores(u)
                    if 1 <= u <= len(us):
                        transposes(u - 1)
                    if u >= 2 and us[u - 2][3] == us[u - 2][4] - 1:
                        values(u - 2)

                for j in range(BR):
                    s = s0 + S_CONV + 2 * j
                    take(0, "cgate", ly, j)
                    gemm(A[0], [(s, 8)], hh, hl, cols)
                    take(1, "cval", ly, j)
                    gemm(A[1], [(s + 1, 8)], hh, hl, cols)

                def branch(b, xh, xl, j, i=None, parity=0, ready=None):
                    s = s0 + (S_P0, S_P1, S_P2)[b] + (2 * j if i is None else 2 * parity)
                    gemm(A[0], [(s, 8)], hh, hl, cols, i)
                    if i is None:
                        take(1, "value", ly, b, j)
                    else:
                        pe.wait_ge(*seen("free", "value", ly, b, 1 - parity, i=i, back=1 - parity))
                    gemm(A[1], [(s + 1, 4)], xh, xl, cols, i, ready)

                def branch_loop(b, xh, xl, ready):
                    for w in range(2):
                        take(w, "gate" if w == 0 else "value", ly, b, 1)
                    pe.wait_ge(*ready)
                    with repeat(pe, KT // 2, ly, "branch", b) as i:
                        for c in range(2):
                            pe.wait_ge(*seen("free", "gate", ly, b, 1 - c, i=i, back=1 - c))
                            branch(b, xh, xl, None, i, c)

                branch_loop(0, oh, ol, ("rounded",) if False else seen("ol", ly, BR - 1))
                last_use[0], last_use[1] = ("gateend", ly, 0), ("valueend", ly, 0)
                pe.wait_ge(*seen("free", "gate", ly, 0, 1, i=KT // 2 - 1))
                pe.wait_ge(*seen("free", "value", ly, 0, 1, i=KT // 2 - 1))
                del last_use[0], last_use[1]

                for n, (kind, g) in enumerate(POOL_ORDER):
                    s = s0 + S_POOL + n
                    if kind == "u":
                        take(0, "pin", ly, g)
                        gemm(A[0], [(s, 8)], hh, hl, cols)
                    else:
                        take(1, "pout", ly, g)
                        gemm(A[1], [(s, 1)], dh[:].rearrange("p (a t) -> p a t", a=1),
                             dl[:].rearrange("p (a t) -> p a t", a=1), cols,
                             k_ready=lambda k: seen("dl", ly, g))

                for j in range(KT):
                    if j == 2:
                        sums(ones, lambda c0, c1: cacc[:, 0, c0:c1], cols, ("cysum", ly), "cmu", ly)
                    if j == 5:
                        sums(ones, lambda c0, c1: cacc[:, 0, c0:c1], cols, ("cqsum", ly), "cvar", ly)
                    take(0, "gate", ly, 1, j)
                    branch(1, yph, ypl, j, ready=(lambda k: seen("ypl", ly, k)) if j == 0 else None)

                branch_loop(2, ych, ycl, seen("ycl", ly, BR - 1))
                pe.wait_ge(*seen("free", "gate", ly, 2, 1, i=KT // 2 - 1))
                pe.wait_ge(*seen("free", "value", ly, 2, 1, i=KT // 2 - 1))
                del last_use[0], last_use[1]

                for j in range(KT):
                    take(j % 2, "out", ly, j)
                    gemm(A[j % 2], [(s0 + S_OUT + j, 8)], mh, ml, cols,
                         k_ready=(lambda k: seen("ml", ly, k // 2 * 0 + k % 2, i=k // 2)) if j == 0 else None)
                sums(ones, t_cols(t3), cols, ("ysum", ly, "post1"), "stat", ly, "post1")
                ada(1, 0) if ly == 0 else ada(1, 5)
                sums(ones, n_cols(6), cols, ("sqadd", ly, "pre2", KT - 1), "stat", ly, "pre2")
                if ly == 0:
                    ada(1, 1)

                for k in range(2):
                    if k in last_use:
                        pe.wait_ge(*seen("free", *last_use.pop(k)))
                for g, nf in enumerate(GROUPS):
                    if g == 0:
                        for k in range(KT):
                            pe.wait_ge(*seen("hl", ly, "pre2", k))
                    s = s0 + FF_IN[g]
                    with repeat(pe, nf // 2, ly, "ffin", g) as i:
                        for c in range(2):
                            pe.wait_ge(*seen("free", "ffa", ly, g, 1 - c, i=i, back=1 - c))
                            gemm(A[0], [(s + 2 * c, 8)], hh, hl, cols, i)
                            pe.wait_ge(*seen("free", "ffb", ly, g, 1 - c, i=i, back=1 - c))
                            gemm(A[1], [(s + 2 * c + 1, 8)], hh, hl, cols, i)
                    pe.wait_ge(*seen("free", "ffa", ly, g, 1, i=nf // 2 - 1))
                    pe.wait_ge(*seen("free", "ffb", ly, g, 1, i=nf // 2 - 1))
                    s = s0 + FF_OUT[g]
                    for j in range(KT):
                        take(j % 2, "ffo", ly, g, j)
                        gemm(A[j % 2], [(s + j, nf)], midh, midl, cols,
                             k_ready=(lambda k: seen("midl", ly, g, k % 2, i=k // 2)) if j == 0 else None)
                    for k in range(2):
                        pe.wait_ge(*seen("free", *last_use.pop(k)))
                sums(ones, t_cols(t3), cols, ("ysum", ly, "post2"), "stat", ly, "post2")
                if ly == 0:
                    ada(1, 2)

        @block.scalar
        def _(act):
            eng_name[id(act)] = "act"
            nxt = [0]
            total = LAYERS * SLABS

            def round_slab(s, i=None):
                nb = slab_blocks(s % SLABS) if s >= RING else 8
                if i is None:
                    act.wait_ge(w_loaded[s % RAW], 16 * (s // RAW + 1))
                    if s >= RING:
                        act.wait_ge(used, s - RING + 1)
                else:
                    act.wait_ge(w_loaded[s % RAW], i * (16 * RING // RAW) + 16 * (s // RAW + 1))
                    act.wait_ge(used, i * RING + (s - RING + 1))
                nc.scalar.activation(wh[:, s % RING, 0:nb * P], raw[:, s % RAW, 0:nb * P],
                                     ACT.Copy).then_inc(*rounded.up())

            def rounds(s):
                while nxt[0] <= min(s, total - 1):
                    round_slab(nxt[0])
                    nxt[0] += 1

            def result_of(s, i=None):
                if i is None:
                    rounds(s + RING - 1)
                else:
                    round_slab(s + RING - 1, i)
                act.wait_ge(used, s + 1 if i is None else i * RING + (s + 1))

            def sq_in(st, lo, x_ready):
                for k in range(KT):
                    act.wait_ge(*x_ready(k))
                    if k >= 2:
                        act.wait_ge(*seen("sqadd", *st, k - 2))
                    nc.scalar.activation(ns[:, 4 + k % 2, lo:T], x[:, k, lo:T],
                                         ACT.Square).then_inc(*act_tmp.up("sq", *st, k))

            def root(buf, *name):
                act.wait_ge(*seen("var", *name))
                nc.scalar.activation(buf, buf, ACT.Sqrt).then_inc(*act_tmp.up("rs", *name))

            def h_high(ly, st, lo, shift):
                for k in range(KT):
                    act.wait_ge(*seen("t", ly, st, k))
                    for c0, c1, s in chunks(lo):
                        ins = nc.scalar.activation(hh[:, k, c0:c1], ns[:, 2 + k % 2, c0:c1], ACT.Identity,
                                                   bias=mod[:, ly, shift + k, s:s + 1])
                    ins.then_inc(*act_hi.up("hh", ly, st, k))

            act.dma_start(cvec[:], io["c"]).then_inc(const_loaded, 16)
            act.dma_start(vec[:], io["vec"]).then_inc(const_loaded, 16)
            act.dma_start(const[:], io["const"]).then_inc(const_loaded, 16)
            for k in range(KT):
                act.dma_start(x[:, k, :], io["x"][:, k, :]).then_inc(x_loaded, 16)
            act.wait_ge(const_loaded, 16 * 3)
            nc.scalar.activation(silu_c[:], cvec[:], ACT.Tanh, scale=0.5).then_inc(*act_tmp.up("ctanh"))

            for ly in range(LAYERS):
                s0 = ly * SLABS
                lo = lo_of(ly)
                cols, full = chunks(lo), chunks(0)

                if ly == 0:
                    sq_in((0, "pre1"), 0, lambda k: (x_loaded, 16 * KT))
                root(ns[:, 1, 0:T], ly, "pre1")
                rounds(s0 + RING - 1)
                h_high(ly, "pre1", 0, 0)

                prev = None
                for n, name in enumerate(["k", "v", "q0", "q1", "q2", "q3"]):
                    w, l0 = A[n % 2], (0 if name in "kv" else lo)
                    result_of(s0 + (S_K + 1, S_V + 1, S_Q, S_Q + 1, S_Q + 2, S_Q + 3)[n])
                    if prev:
                        act.wait_ge(*seen("tile", ly, prev))
                    if name == "v":
                        nc.scalar.activation(t1[:, 0:T], at(w, 0, T), ACT.Copy).then_inc(
                            *act_out.up("free", "gemm", ly, name))
                        noted[("vcopy", ly)] = noted[("free", "gemm", ly, name)]
                        act.wait_ge(*seen("vt", ly))
                        nc.scalar.activation(vh[:].rearrange("p a b -> p (a b)"), at(B, 0, T),
                                             ACT.Copy).then_inc(*act_hi.up("vh", ly))
                    else:
                        nc.scalar.activation(t1[:, l0:T], at(w, l0, T), ACT.Square).then_inc(
                            *act_tmp.up("tsq", ly, name))
                        gcol = V_KN if name == "k" else V_QN
                        nc.scalar.activation(t2[:, l0:T], at(w, l0, T), ACT.Copy,
                                             scale=vec[:, ly, gcol:gcol + 1]).then_inc(
                            *act_out.up("free", "gemm", ly, name))
                        root(t1[:, l0:T], ly, name)
                        act.wait_ge(*seen("roped", ly, name))
                        if name == "k":
                            for kv in range(KV):
                                for p in range(2):
                                    ins = nc.scalar.activation(kk[64 * p:64 * p + 64, 2 * kv, :],
                                                               t2[64 * kv:64 * kv + 64, 0:T], ACT.Copy)
                        else:
                            j = int(name[1])
                            for p in range(2):
                                ins = nc.scalar.activation(qs[64 * p:64 * p + 64, 2 * j + p, l0:T],
                                                           t2[64 * p:64 * p + 64, l0:T], ACT.Copy)
                        ins.then_inc(*act_hi.up("hi", ly, name))
                    prev = name

                us = units(ly)
                act.wait_ge(*seen("tile", ly, "q3"))
                if ly:
                    act.wait_ge(x_stored, 16 * KT)

                def o_out(b, h, q0, nq):
                    act.wait_ge(*seen("pv", ly, b))
                    p = 64 * (h % 2)
                    nc.scalar.activation(o_raw[p:p + 64, h // 2, q0:q0 + nq * P], O[0:HD, 0:nq * P],
                                         ACT.Copy).then_inc(*act_out.up("free", "pv", ly, b))

                for u in range(len(us) + 3):
                    if u < len(us):
                        h, q0, nk, q, nq, b = us[u]
                        act.wait_ge(*seen("negmax", ly, u))
                        if u >= 2:
                            act.wait_ge(*seen("pt", ly, u - 2))
                        nc.scalar.activation(pr[:, u % 2, 0:nk], at(A[u % 2], 0, nk), ACT.Exp,
                                             bias=ust[:, 1, u % 8:u % 8 + 1], scale=HD ** -0.5,
                                             accum_out=ust[:, 2, u % 8:u % 8 + 1]).then_inc(
                            *act_out.up("free", "scores", ly, u))
                    if 1 <= u <= len(us):
                        h, q0, nk, q, nq, b = us[u - 1]
                        act.wait_ge(*seen("pt", ly, u - 1))
                        if q == 0 and b >= 2:
                            act.wait_ge(*seen("pv", ly, b - 2))
                        ph = (pt0h, pt1h)[b % 2]
                        nc.scalar.activation(ph[:, 0:nk // P, q * P:(q + 1) * P],
                                             at(B, 0, nk).rearrange("p (k q) -> p k q", q=P),
                                             ACT.Copy).then_inc(*act_hi.up("pth", ly, u - 1))
                    if u >= 3 and us[u - 3][3] == us[u - 3][4] - 1:
                        h, q0, nk, q, nq, b = us[u - 3]
                        o_out(b, h, q0, nq)
                act.wait_ge(*act_out.ago())
                for j in range(BR):
                    nc.scalar.activation(oh[:, j, lo:T], o_raw[:, j, lo:T], ACT.Copy).then_inc(
                        *act_hi.up("oh", ly, j))

                for j in range(BR):
                    result_of(s0 + S_CONV + 2 * j)
                    if j:
                        act.wait_ge(*seen("free", "cval", ly, j - 1))
                    nc.scalar.activation(t1[:, lo:T], at(A[0], lo, T), ACT.Tanh, scale=0.5).then_inc(
                        *act_out.up("free", "cgate", ly, j))
                    result_of(s0 + S_CONV + 2 * j + 1)

                def branch_loop(b):
                    s = s0 + (S_P0, S_P2)[b // 2]
                    for c in range(2):
                        pass
                    with repeat(act, KT // 2, ly, "branch", b) as i:
                        for c in range(2):
                            result_of(s + 2 * c, i)
                            act.wait_ge(*seen("free", "value", ly, b, c, i=i, back=1))
                            tt = (t1, t3)[c]
                            nc.scalar.activation(tt[:, lo:T], at(A[0], lo, T), ACT.Tanh, scale=0.5).then_inc(
                                *act_out.up("free", "gate", ly, b, c))
                            round_slab(s + 2 * c + 1 + RING - 1, i)
                            if b == 2:
                                act.wait_ge(*seen("macc", ly, c, i=i))
                                nc.scalar.activation(mh[:, bass.ds(i * 2 + c, 1), lo:T].rearrange("p a t -> p (a t)"),
                                                     acc[:, bass.ds(i * 2 + c, 1), lo:T].rearrange("p a t -> p (a t)"),
                                                     ACT.Copy).then_inc(*act_hi.up("mh", ly, c))
                    nxt[0] += RING * (KT // 2)

                act.wait_ge(*seen("free", "cval", ly, BR - 1))
                branch_loop(0)

                for n, (kind, g) in enumerate(POOL_ORDER):
                    result_of(s0 + S_POOL + n)
                    if kind == "u":
                        act.wait_ge(*(seen("dev", ly, g - 1) if g else seen("pads", ly)))
                        for c0, c1, s in cols:
                            u0 = UC if s else UL
                            ins = nc.scalar.activation(t1[:, u0:u0 + c1 - c0], at(A[0], c0, c1), ACT.Copy)
                        ins.then_inc(*act_out.up("free", "pin", ly, g))
                        if g:
                            act.wait_ge(used, s0 + S_POOL + POOL_ORDER.index(("w", g - 1)) + 1)
                        act.wait_ge(*seen("dev", ly, g))
                        d = (t3, t2)[g % 2]
                        for c0, c1, s in cols:
                            u0 = UC if s else UL
                            ins = nc.scalar.activation(dh[:, c0:c1], d[:, u0:u0 + c1 - c0], ACT.Copy)
                        ins.then_inc(*act_hi.up("dh", ly, g))
                    else:
                        nc.scalar.activation(yph[:, g, lo:T], at(A[1], lo, T), ACT.Copy,
                                             scale=vec[:, ly, V_PS + g:V_PS + g + 1]).then_inc(
                            *act_hi.up("yph", ly, g))

                def ln_y():
                    act.wait_ge(*seen("taps", ly))
                    for j in range(BR):
                        for c0, c1, s in cols:
                            src = 0 if s else GL - GC
                            ins = nc.scalar.activation(ct[:, j, c0:c1], cacc[:, j, src:src + c1 - c0],
                                                       ACT.Identity, scale=0.5,
                                                       bias=vec[:, ly, V_CB + j:V_CB + j + 1])
                        ins.then_inc(*act_tmp.up("cy", ly, j))

                def ln_sq():
                    for j in range(BR):
                        act.wait_ge(*seen("cc", ly, j))
                        if j >= 2:
                            act.wait_ge(*seen("cqadd", ly, j - 2))
                        nc.scalar.activation(cacc[:, 2 + j % 2, lo:T], ct[:, j, lo:T], ACT.Square).then_inc(
                            *act_tmp.up("csq", ly, j))

                def ln_act(j):
                    act.wait_ge(*seen("cn", ly, j))
                    if j >= 2:
                        act.wait_ge(*seen("cm", ly, j - 2))
                    nc.scalar.activation(ct[:, j, lo:T], ct[:, j, lo:T], ACT.Identity,
                                         scale=vec[:, ly, V_LG + j:V_LG + j + 1],
                                         bias=vec[:, ly, V_LB + j:V_LB + j + 1]).then_inc(*act_tmp.up())
                    act.wait_ge(*act_tmp.ago())
                    nc.scalar.activation(cacc[:, 2 + j % 2, lo:T], ct[:, j, lo:T], ACT.Tanh,
                                         scale=0.5).then_inc(*act_tmp.up("cth", ly, j))
                    act.wait_ge(*seen("cm", ly, j))
                    nc.scalar.activation(ych[:, j, lo:T], ct[:, j, lo:T], ACT.Copy, scale=0.5).then_inc(
                        *act_hi.up("ych", ly, j))

                for j in range(KT):
                    result_of(s0 + S_P1 + 2 * j)
                    if j >= 2:
                        act.wait_ge(*seen("free", "value", ly, 1, j - 2))
                    tt = (t1, t3)[j % 2]
                    nc.scalar.activation(tt[:, lo:T], at(A[0], lo, T), ACT.Tanh, scale=0.5).then_inc(
                        *act_out.up("free", "gate", ly, 1, j))
                    result_of(s0 + S_P1 + 2 * j + 1)
                    if j == 0:
                        ln_y()
                    elif j == 3:
                        ln_sq()
                    elif j == 5:
                        root(cacc[:, 1, lo:T], ly, "conv")
                    elif j >= 6:
                        ln_act(2 * (j - 6))
                        ln_act(2 * (j - 6) + 1)

                branch_loop(2)

                def y_out(j, w, scale, st):
                    if j >= 2:
                        act.wait_ge(*seen("yadd", ly, st, j - 2))
                    nc.scalar.activation((t1, t2)[j % 2][:, lo:T], at(w, lo, T), ACT.Square,
                                         scale=scale).then_inc(*act_tmp.up("ysq", ly, st, j))
                    nc.scalar.activation(acc[:, j, lo:T], at(w, lo, T), ACT.Copy, scale=scale).then_inc(
                        *act_out.up("free", "out", ly, j))

                for j in range(KT):
                    result_of(s0 + S_OUT + j)
                    if j == 0:
                        act.wait_ge(*seen("ml", ly, 1, i=KT // 2 - 1))
                    y_out(j, A[j % 2], 0.5, "post1")
                for k in range(KT):
                    act.dma_start(x[:, k, lo:T], (io["x"] if ly == 0 else io["xs"])[:, k, lo:T]).then_inc(x_loaded, 16)
                root(ns[:, 0, lo:T], ly, "post1")
                sq_in((ly, "pre2"), lo, lambda k: seen("x", ly, "post1", k))
                root(ns[:, 1, lo:T], ly, "pre2")
                h_high(ly, "pre2", lo, 3 * KT)

                for g, nf in enumerate(GROUPS):
                    s = s0 + FF_IN[g]
                    with repeat(act, nf // 2, ly, "ffin", g) as i:
                        for c in range(2):
                            f = bass.ds(i * 2 + c, 1)
                            result_of(s + 2 * c, i)
                            act.wait_ge(*seen("free", "ffa", ly, g, 1 - c, i=i, back=1 - c))
                            nc.scalar.activation(t1[:, lo:T], at(A[0], lo, T), ACT.Tanh, scale=0.5).then_inc(
                                *act_tmp.up("fth", ly, g, c))
                            round_slab(s + 2 * c + 1 + RING - 1, i)
                            act.wait_ge(*seen("free", "ffb", ly, g, c, i=i))
                            nc.scalar.activation(midh[:, f, lo:T].rearrange("p a t -> p (a t)"), t3[:, lo:T],
                                                 ACT.Copy).then_inc(*act_hi.up("midh", ly, g, c))
                    nxt[0] += RING * (nf // 2)
                    for j in range(KT):
                        result_of(s0 + FF_OUT[g] + j)
                        if g == 0:
                            nc.scalar.activation(acc[:, j, lo:T], at(A[j % 2], lo, T), ACT.Copy).then_inc(
                                *act_out.up("free", "ffo", ly, g, j))
                        elif g == 2:
                            act.wait_ge(*seen("free", "ffo", ly, g, j))
                            if j >= 2:
                                act.wait_ge(*seen("yadd", ly, "post2", j - 2))
                            nc.scalar.activation((t1, t2)[j % 2][:, lo:T], acc[:, j, lo:T], ACT.Square).then_inc(
                                *act_tmp.up("ysq", ly, "post2", j))
                root(ns[:, 0, lo:T], ly, "post2")
                if ly == 0:
                    for k in range(KT):
                        act.wait_ge(*seen("x", ly, "post2", k))
                        act.dma_start(io["xs"][:, k, :], x[:, k, :]).then_inc(x_stored, 16)
                    sq_in((1, "pre1"), 0, lambda k: seen("x", 0, "post2", k))
                else:
                    for k in range(KT):
                        act.wait_ge(*seen("x", ly, "post2", k))
                        act.dma_start(io["out"][:, k, :], x[:, k, CTX:T]).then_inc(out_stored, 16)
                    act.wait_ge(out_stored, 16 * KT)

        @block.vector
        def _(dve):
            eng_name[id(dve)] = "dve"
            v = nc.vector

            def link(ins, tally, *name):
                ins.then_inc(*tally.up(*name))
                dve.wait_ge(*tally.ago())

            def sq_add(st, lo):
                for k in range(KT):
                    dve.wait_ge(*seen("sq", *st, k))
                    if k == 0:
                        ins = v.tensor_copy(ns[:, 6, lo:T], ns[:, 4, lo:T])
                    else:
                        ins = v.tensor_tensor(ns[:, 6, lo:T], ns[:, 6, lo:T], ns[:, 4 + k % 2, lo:T], ALU.add)
                    link(ins, dve_tmp, "sqadd", *st, k)

            def variance(buf, lo, n, *name, stat=None):
                dve.wait_ge(*seen(*(stat or ("stat",) + name)))
                link(v.tensor_scalar(buf, at(B, lo, T), 1.0 / n, EPS, ALU.mult, ALU.add), dve_out,
                     "free", *(stat or ("stat",) + name))
                link(v.reciprocal(buf, buf), dve_tmp, "var", *name)

            def normalise(ly, st, lo, which, shift):
                dve.wait_ge(*seen("rs", ly, st))

                def low(k):
                    dve.wait_ge(*seen("hh", ly, st, k))
                    for c0, c1, s in chunks(lo):
                        ins = v.scalar_tensor_tensor(
                            out=hl[:, k, c0:c1], in0=ns[:, 2 + k % 2, c0:c1],
                            scalar=mod[:, ly, shift + k, s:s + 1], in1=hh[:, k, c0:c1],
                            op0=ALU.add, op1=ALU.subtract)
                        last = (c0, c1, s) == chunks(lo)[-1]
                        ins.then_inc(*(dve_lo.up("hl", ly, st, k) if last else dve_lo.up()))

                for k in range(KT):
                    if k >= 2:
                        dve.wait_ge(*dve_lo.ago())
                    for c0, c1, s in chunks(lo):
                        ins = v.scalar_tensor_tensor(
                            out=ns[:, 2 + k % 2, c0:c1], in0=x[:, k, c0:c1],
                            scalar=gain[:, ly, which, k, s:s + 1], in1=ns[:, 1, c0:c1],
                            op0=ALU.mult, op1=ALU.mult)
                        last = (c0, c1, s) == chunks(lo)[-1]
                        ins.then_inc(*(dve_tmp.up("t", ly, st, k) if last else dve_tmp.up()))
                    if k:
                        low(k - 1)
                low(KT - 1)

            def residual(ly, st, lo, which):
                dve.wait_ge(*seen("rs", ly, st))
                for k in range(KT):
                    for c0, c1, s in chunks(lo):
                        ins = v.scalar_tensor_tensor(
                            out=ns[:, 2 + k % 2, c0:c1], in0=acc[:, k, c0:c1],
                            scalar=gain[:, ly, which, k, s:s + 1], in1=ns[:, 0, c0:c1],
                            op0=ALU.mult, op1=ALU.mult)
                        ins.then_inc(*dve_tmp.up())
                    dve.wait_ge(*dve_tmp.ago())
                    link(v.tensor_tensor(x[:, k, lo:T], x[:, k, lo:T], ns[:, 2 + k % 2, lo:T], ALU.add),
                         dve_tmp, "x", ly, st, k)

            def modulation(ly, g):
                dve.wait_ge(*seen("ada", ada_k[(ly, g)]))
                m = mod[:, ly, 8 * g:8 * g + 8, :]
                d = DD[:, 0:16].rearrange("p (t s) -> p t s", s=2)
                b = vec[:, ly, V_BADA + 8 * g:V_BADA + 8 * g + 8]
                for s in range(2):
                    ins = v.tensor_tensor(m[:, :, s], d[:, :, s], b, ALU.add)
                    ins.then_inc(*(dve_out.up("free", "ada", ly, g) if s else dve_out.up()))
                dve.wait_ge(*dve_out.ago())
                if g in (0, 3):
                    return
                which, col = {1: (0, V_GPRE1), 2: (1, V_GPOST1), 4: (2, V_GPRE2), 5: (3, V_GPOST2)}[g]
                for s in range(2):
                    gv = vec[:, ly, col:col + KT]
                    if g in (1, 4):
                        ins = v.scalar_tensor_tensor(out=gain[:, ly, which, :, s], in0=m[:, :, s], scalar=1.0,
                                                     in1=gv, op0=ALU.add, op1=ALU.mult)
                    else:
                        ins = v.tensor_tensor(gain[:, ly, which, :, s], m[:, :, s], gv, ALU.mult)
                    ins.then_inc(*dve_tmp.up())
                dve.wait_ge(*dve_tmp.ago())

            ada_k = {(ly, g): 8 * n + 7 for n, (ly, g, _) in enumerate(ADA_PLAN)}

            dve.wait_ge(*seen("ctanh"))
            link(v.scalar_tensor_tensor(out=silu_c[:].rearrange("p a b -> p (a b)"),
                                        in0=silu_c[:].rearrange("p a b -> p (a b)"), scalar=1.0,
                                        in1=cvec[:].rearrange("p a b -> p (a b)"), op0=ALU.add, op1=ALU.mult),
                 dve_tmp)
            link(v.tensor_scalar(silu_c[:].rearrange("p a b -> p (a b)"),
                                 silu_c[:].rearrange("p a b -> p (a b)"), 0.5, None, ALU.mult), dve_tmp, "silu")
            sq_add((0, "pre1"), 0)
            modulation(0, 0)
            modulation(0, 1)
            variance(ns[:, 1, 0:T], 0, D, 0, "pre1")

            for ly in range(LAYERS):
                s0 = ly * SLABS
                lo = lo_of(ly)
                cols, full = chunks(lo), chunks(0)
                normalise(ly, "pre1", 0, 0, 0)
                if ly == 1:
                    modulation(1, 3)

                for n, name in enumerate(["k", "v", "q0", "q1", "q2", "q3"]):
                    l0 = 0 if name in "kv" else lo
                    if name == "v":
                        dve.wait_ge(*seen("vh", ly))
                        v.tensor_tensor(vl[:].rearrange("p a b -> p (a b)"), at(B, 0, T),
                                        vh[:].rearrange("p a b -> p (a b)"), ALU.subtract).then_inc(
                            *dve_lo.up("free", "vt", ly))
                        noted[("tile", ly, "v")] = noted[("free", "vt", ly)]
                        continue
                    if ly == 0 and n >= 2:
                        modulation(0, n)
                    if ly == 1 and n == 2:
                        modulation(1, 4)
                    variance(t1[:, l0:T], l0, HD, ly, name)
                    dve.wait_ge(*seen("rot", ly, name))
                    v.tensor_tensor(t3[:, l0:T], at(B, l0, T), sin[:, l0:T], ALU.mult).then_inc(
                        *dve_out.up("free", "rot", ly, name))
                    link(v.tensor_tensor(t2[:, l0:T], t2[:, l0:T], cos[:, l0:T], ALU.mult), dve_tmp)
                    dve.wait_ge(*dve_out.ago())
                    link(v.tensor_tensor(t2[:, l0:T], t2[:, l0:T], t3[:, l0:T], ALU.add), dve_tmp)
                    dve.wait_ge(*seen("rs", ly, name))
                    link(v.tensor_tensor(t2[:, l0:T], t2[:, l0:T], t1[:, l0:T], ALU.mult), dve_tmp,
                         "roped", ly, name)
                    dve.wait_ge(*seen("hi", ly, name))
                    for a in range(2):
                        if name == "k":
                            for p in range(2):
                                ins = v.tensor_tensor(kk[64 * p:64 * p + 64, 2 * a + 1, :], t2[64 * a:64 * a + 64, 0:T],
                                                      kk[64 * a:64 * a + 64, 2 * a, :], ALU.subtract)
                                ins.then_inc(*(dve_lo.up("tile", ly, name) if a and p else dve_lo.up()))
                        else:
                            j = int(name[1])
                            ins = v.tensor_tensor(qs[64 - 64 * a:128 - 64 * a, 2 * j + a, l0:T],
                                                  t2[64 * a:64 * a + 64, l0:T],
                                                  qs[64 * a:64 * a + 64, 2 * j + a, l0:T], ALU.subtract)
                            ins.then_inc(*(dve_lo.up("tile", ly, name) if a else dve_lo.up()))

                us = units(ly)
                for u in range(len(us) + 2):
                    if u < len(us):
                        h, q0, nk, q, nq, b = us[u]
                        c = u % 8
                        dve.wait_ge(*seen("scores", ly, u))
                        link(v.reduce_max(ust[:, 0, c:c + 1], at(A[u % 2], 0, nk), AX.X), dve_tmp)
                        v.tensor_scalar(ust[:, 1, c:c + 1], ust[:, 0, c:c + 1], -(HD ** -0.5), None,
                                        ALU.mult).then_inc(*dve_tmp.up("negmax", ly, u))
                    if 1 <= u <= len(us):
                        h, q0, nk, q, nq, b = us[u - 1]
                        c = (u - 1) % 8
                        dve.wait_ge(*seen("free", "scores", ly, u - 1))
                        link(v.reciprocal(ust[:, 3, c:c + 1], ust[:, 2, c:c + 1]), dve_tmp)
                        v.tensor_scalar(pr[:, (u - 1) % 2, 0:nk], pr[:, (u - 1) % 2, 0:nk], ust[:, 3, c:c + 1],
                                        None, ALU.mult).then_inc(*dve_tmp.up("normed", ly, u - 1))
                    if u >= 2:
                        h, q0, nk, q, nq, b = us[u - 2]
                        dve.wait_ge(*seen("pth", ly, u - 2))
                        ph, pl = ((pt0h, pt0l), (pt1h, pt1l))[b % 2]
                        v.tensor_tensor(pl[:, 0:nk // P, q * P:(q + 1) * P],
                                        at(B, 0, nk).rearrange("p (k q) -> p k q", q=P),
                                        ph[:, 0:nk // P, q * P:(q + 1) * P], ALU.subtract).then_inc(
                            *dve_lo.up("free", "pt", ly, u - 2))
                for j in range(BR):
                    dve.wait_ge(*seen("oh", ly, j))
                    v.tensor_tensor(ol[:, j, lo:T], o_raw[:, j, lo:T], oh[:, j, lo:T], ALU.subtract).then_inc(
                        *dve_lo.up("ol", ly, j))

                a0 = 0 if lo == 0 else GL - HALF
                for p0, p1 in ([(0, GC)] if lo == 0 else []) + [(GL - HALF, GL), (GL + LAT, GW)]:
                    v.memset(cg[:, :, p0:p1], 0.0).then_inc(*dve_tmp.up())
                dve.wait_ge(*dve_tmp.ago())

                def tap(j, t, shift):
                    w = vec[:, ly, bass.ds(V_DW + j * TAPS + t, 1)]
                    src = cg[:, j, bass.ds(shift + a0, CW - a0)]
                    return v.scalar_tensor_tensor(out=cacc[:, j, a0:CW], in0=src, scalar=w,
                                                  in1=cacc[:, j, a0:CW], op0=ALU.mult, op1=ALU.add)

                FIRST = TAPS - 6 * (KT // 2)
                for j in range(BR):
                    dve.wait_ge(*seen("free", "cgate", ly, j))
                    dve.wait_ge(used, s0 + S_CONV + 2 * j + 2)
                    for c0, c1, s in cols:
                        g0 = GC if s else GL
                        ins = v.scalar_tensor_tensor(out=cg[:, j, g0:g0 + c1 - c0], in0=t1[:, c0:c1], scalar=1.0,
                                                     in1=at(A[1], c0, c1), op0=ALU.add, op1=ALU.mult)
                        ins.then_inc(*(dve_out.up() if s else dve_out.up("free", "cval", ly, j)))
                    dve.wait_ge(*dve_out.ago())
                    link(v.tensor_scalar(cacc[:, j, a0:CW], cg[:, j, a0:CW], vec[:, ly, V_DW + j * TAPS:V_DW + j * TAPS + 1],
                                         None, ALU.mult), dve_tap)
                    for t in range(1, FIRST):
                        link(tap(j, t, t), dve_tap)

                def merge(b, c, i):
                    dve.wait_ge(*(seen("free", "gate", ly, b, c, i=i) if b != 1 else seen("free", "gate", ly, b, i)))
                    s = s0 + (S_P0, S_P1, S_P2)[b]
                    dve.wait_ge(used, s + 2 * i + 2 if b == 1 else i * RING + (s + 2 * c + 2))
                    tt = (t1, t3)[c]
                    dst = acc[:, i, lo:T] if b == 1 else acc[:, bass.ds(i * 2 + c, 1), lo:T].rearrange(
                        "p a t -> p (a t)")
                    name = ("free", "value", ly, b) + ((i,) if b == 1 else (c,))
                    if b == 0:
                        v.scalar_tensor_tensor(out=dst, in0=tt[:, lo:T], scalar=1.0, in1=at(A[1], lo, T),
                                               op0=ALU.add, op1=ALU.mult).then_inc(*dve_out.up(*name))
                        return
                    link(v.scalar_tensor_tensor(out=t2[:, lo:T], in0=tt[:, lo:T], scalar=1.0, in1=at(A[1], lo, T),
                                                op0=ALU.add, op1=ALU.mult), dve_out, *name)
                    link(v.tensor_tensor(dst, dst, t2[:, lo:T], ALU.add), dve_tmp,
                         *(("macc", ly, c) if b == 2 else ()))
                    if b == 2:
                        dve.wait_ge(*seen("mh", ly, c, i=i))
                        f = bass.ds(i * 2 + c, 1)
                        v.tensor_tensor(ml[:, f, lo:T].rearrange("p a t -> p (a t)"), dst,
                                        mh[:, f, lo:T].rearrange("p a t -> p (a t)"), ALU.subtract).then_inc(
                            *dve_lo.up("ml", ly, c))

                with repeat(dve, KT // 2, ly, "branch", 0) as i:
                    for c in range(2):
                        merge(0, c, i)
                        for t in range(3):
                            for j in range(BR):
                                dve.wait_ge(*dve_tap.ago(BR - 1))
                                shift = i * 6 + (FIRST + 3 * c + t)
                                tap(j, shift, shift).then_inc(*dve_tap.up())
                dve.wait_ge(*dve_tap.ago())
                dve.wait_ge(*dve_out.ago())
                link(v.memset(t1[:, UC + CTX:UL], 0.0), dve_tmp, "taps", ly)

                if lo == 0:
                    v.memset(t1[:, 0:UC], 0.0).then_inc(*dve_tmp.up())
                link(v.memset(t1[:, UL + LAT:UW], 0.0), dve_tmp, "pads", ly)
                b0 = 0 if lo == 0 else UL - 8
                for n, (kind, g) in enumerate(POOL_ORDER):
                    if kind == "w":
                        dve.wait_ge(*seen("yph", ly, g))
                        v.scalar_tensor_tensor(out=ypl[:, g, lo:T], in0=at(A[1], lo, T),
                                               scalar=vec[:, ly, V_PS + g:V_PS + g + 1], in1=yph[:, g, lo:T],
                                               op0=ALU.mult, op1=ALU.subtract).then_inc(
                            *dve_lo.up("free", "pout", ly, g))
                        noted[("ypl", ly, g)] = noted[("free", "pout", ly, g)]
                        continue
                    dve.wait_ge(*seen("free", "pin", ly, g))
                    link(v.tensor_tensor(t2[:, b0 + 1:UW], t1[:, b0:UW - 1], t1[:, b0 + 1:UW], ALU.add), dve_tmp)
                    src, e = t2, 1
                    for m in range(g):
                        sh = 1 << m
                        dst = (t3, t2)[m % 2]
                        e += sh
                        link(v.tensor_tensor(dst[:, b0 + e:UW - e + 1], src[:, b0 + e - sh:UW - e + 1 - sh],
                                             src[:, b0 + e + sh:UW - e + 1 + sh], ALU.add), dve_tmp)
                        src = dst
                    for c0, c1, s in cols:
                        u0 = UC if s else UL
                        for off, ecol in ((u0, 0), (u0 + c1 - c0 - 8, 8)):
                            e0 = C_EDGE + 16 * g + ecol
                            v.tensor_tensor(src[:, off:off + 8], src[:, off:off + 8], const[:, e0:e0 + 8],
                                            ALU.mult).then_inc(*dve_tmp.up())
                    dve.wait_ge(*dve_tmp.ago())
                    d = (t3, t2)[g % 2]
                    link(v.scalar_tensor_tensor(out=d[:, b0 + 8:UW - 8], in0=src[:, b0 + 8:UW - 8],
                                                scalar=1.0 / WIN[g], in1=t1[:, b0 + 8:UW - 8], op0=ALU.mult,
                                                op1=ALU.subtract), dve_tmp, "dev", ly, g)
                    dve.wait_ge(*seen("dh", ly, g))
                    for c0, c1, s in cols:
                        u0 = UC if s else UL
                        ins = v.tensor_tensor(dl[:, c0:c1], d[:, u0:u0 + c1 - c0], dh[:, c0:c1], ALU.subtract)
                        ins.then_inc(*(dve_lo.up() if s else dve_lo.up("dl", ly, g)))
                    dve.wait_ge(*dve_lo.ago())

                cy = [ct[:, j, lo:T] for j in range(BR)]
                ca = [cacc[:, j, lo:T] for j in range(BR)]

                def ln_sum():
                    dve.wait_ge(*seen("cy", ly, BR - 1))
                    link(v.tensor_tensor(ca[0], cy[0], cy[1], ALU.add), dve_tmp)
                    link(v.tensor_tensor(ca[0], ca[0], cy[2], ALU.add), dve_tmp)
                    link(v.tensor_tensor(ca[0], ca[0], cy[3], ALU.add), dve_tmp, "cysum", ly)

                def ln_centre():
                    dve.wait_ge(*seen("cmu", ly))
                    link(v.tensor_scalar(ca[1], at(B, lo, T), 1.0 / (BR * P), None, ALU.mult), dve_out,
                         "free", "cmu", ly)
                    for j in range(BR):
                        v.tensor_tensor(cy[j], cy[j], ca[1], ALU.subtract).then_inc(*dve_tmp.up("cc", ly, j))

                def ln_squares():
                    for j in range(BR):
                        dve.wait_ge(*seen("csq", ly, j))
                        ins = (v.tensor_copy(ca[0], ca[2]) if j == 0 else
                               v.tensor_tensor(ca[0], ca[0], ca[2 + j % 2], ALU.add))
                        link(ins, dve_tmp, "cqadd", ly, j)
                    noted[("cqsum", ly)] = noted[("cqadd", ly, BR - 1)]

                def ln_scale():
                    dve.wait_ge(*seen("rs", ly, "conv"))
                    for j in range(BR):
                        v.tensor_tensor(cy[j], cy[j], ca[1], ALU.mult).then_inc(*dve_tmp.up("cn", ly, j))

                def ln_silu(j):
                    dve.wait_ge(*seen("cth", ly, j))
                    link(v.scalar_tensor_tensor(out=cy[j], in0=ca[2 + j % 2], scalar=1.0, in1=cy[j], op0=ALU.add,
                                                op1=ALU.mult), dve_tmp, "cm", ly, j)
                    dve.wait_ge(*seen("ych", ly, j))
                    v.scalar_tensor_tensor(out=ycl[:, j, lo:T], in0=cy[j], scalar=0.5, in1=ych[:, j, lo:T],
                                           op0=ALU.mult, op1=ALU.subtract).then_inc(*dve_lo.up("ycl", ly, j))

                for j in range(KT):
                    merge(1, j % 2, j)
                    if j == 0:
                        ln_sum()
                    elif j == 2:
                        ln_centre()
                    elif j == 3:
                        ln_squares()
                    elif j == 5:
                        variance(ca[1], lo, BR * P, ly, "conv", stat=("cvar", ly))
                        ln_scale()
                    elif j >= 6:
                        ln_silu(2 * (j - 6))
                        ln_silu(2 * (j - 6) + 1)
                with repeat(dve, KT // 2, ly, "branch", 2) as i:
                    for c in range(2):
                        merge(2, c, i)

                def y_add(st, j):
                    dve.wait_ge(*seen("ysq", ly, st, j))
                    ins = (v.tensor_copy(t3[:, lo:T], t1[:, lo:T]) if j == 0 else
                           v.tensor_tensor(t3[:, lo:T], t3[:, lo:T], (t1, t2)[j % 2][:, lo:T], ALU.add))
                    link(ins, dve_tmp, "yadd", ly, st, j)
                    if j == KT - 1:
                        noted[("ysum", ly, st)] = noted[("yadd", ly, st, j)]

                for j in range(KT):
                    y_add("post1", j)
                variance(ns[:, 0, lo:T], lo, D, ly, "post1")
                dve.wait_ge(x_loaded, 16 * KT * (ly + 2))
                residual(ly, "post1", lo, 1)
                sq_add((ly, "pre2"), lo)
                modulation(1, 0 if ly == 0 else 5)
                variance(ns[:, 1, lo:T], lo, D, ly, "pre2")
                normalise(ly, "pre2", lo, 2, 3 * KT)
                if ly == 0:
                    modulation(1, 1)

                for g, nf in enumerate(GROUPS):
                    s = s0 + FF_IN[g]
                    with repeat(dve, nf // 2, ly, "ffin", g) as i:
                        for c in range(2):
                            f = bass.ds(i * 2 + c, 1)
                            dve.wait_ge(*seen("fth", ly, g, c, i=i))
                            link(v.scalar_tensor_tensor(out=t2[:, lo:T], in0=t1[:, lo:T], scalar=1.0,
                                                        in1=at(A[0], lo, T), op0=ALU.add, op1=ALU.mult),
                                 dve_out, "free", "ffa", ly, g, c)
                            dve.wait_ge(used, i * RING + (s + 2 * c + 2))
                            link(v.scalar_tensor_tensor(out=t3[:, lo:T], in0=t2[:, lo:T], scalar=0.5,
                                                        in1=at(A[1], lo, T), op0=ALU.mult, op1=ALU.mult),
                                 dve_out, "free", "ffb", ly, g, c)
                            dve.wait_ge(*seen("midh", ly, g, c, i=i))
                            v.tensor_tensor(midl[:, f, lo:T].rearrange("p a t -> p (a t)"), t3[:, lo:T],
                                            midh[:, f, lo:T].rearrange("p a t -> p (a t)"), ALU.subtract).then_inc(
                                *dve_lo.up("midl", ly, g, c))
                            dve.wait_ge(*dve_lo.ago())
                    for j in range(KT):
                        if g:
                            dve.wait_ge(used, s0 + FF_OUT[g] + j + 1)
                            link(v.tensor_tensor(acc[:, j, lo:T], acc[:, j, lo:T], at(A[j % 2], lo, T), ALU.add),
                                 dve_out, "free", "ffo", ly, g, j)
                        if g == 2:
                            y_add("post2", j)
                variance(ns[:, 0, lo:T], lo, D, ly, "post2")
                residual(ly, "post2", lo, 3)
                if ly == 0:
                    sq_add((1, "pre1"), 0)
                    modulation(1, 2)
                    variance(ns[:, 1, 0:T], 0, D, 1, "pre1")

    return noted, strides


def program(nc, scratch, io):
    known = build(scratch[0], scratch[1], ({}, {}))
    build(nc, io, known)


def slabs_of(l, w_in, w_attn_o, pool_w, w_pool_o, w_conv_o, w_out, w_ffn_in, w_ffn_out, out):
    q_end, v_end = HEADS * HD, HEADS * HD + 2 * KV * HD
    p_end = v_end + BR * P
    g_end = p_end + 2 * BR * P

    def put(s, w, cols, k0=0, k1=KT):
        n = k1 - k0
        out[s, :, 0:n * P] = w[k0 * P:k1 * P, cols:cols + P].reshape(n, P, P).transpose(1, 0, 2).reshape(P, n * P)

    for n, c in ((S_K, q_end), (S_V, q_end + KV * HD)):
        put(n, w_in, c, 0, 4)
        put(n + 1, w_in, c, 4, 8)
    for j in range(BR):
        put(S_Q + j, w_in, j * P)
        put(S_CONV + 2 * j, w_in, p_end + (BR + j) * P)
        put(S_CONV + 2 * j + 1, w_in, p_end + j * P)
    for n, (kind, g) in enumerate(POOL_ORDER):
        if kind == "u":
            put(S_POOL + n, w_in, v_end + g * P)
        else:
            out[S_POOL + n, :, 0:P] = pool_w[g]
    for b, (s, w) in enumerate(((S_P0, w_attn_o), (S_P1, w_pool_o), (S_P2, w_conv_o))):
        for j in range(KT):
            put(s + 2 * j, w_in, g_end + b * D + j * P)
            put(s + 2 * j + 1, w, j * P, 0, BR)
    for j in range(KT):
        put(S_OUT + j, w_out, j * P)
    f0 = 0
    for g, nf in enumerate(GROUPS):
        for f in range(nf):
            put(FF_IN[g] + 2 * f, w_ffn_in, (f0 + f) * P)
            put(FF_IN[g] + 2 * f + 1, w_ffn_in, D_FF + (f0 + f) * P)
        for j in range(KT):
            put(FF_OUT[g] + j, w_ffn_out, j * P, f0, f0 + nf)
        f0 += nf


def constants():
    c = np.zeros((P, NC), np.float32)
    c[:, C_ID:C_ID + P] = np.eye(P)
    c[:, C_ONE:C_ONE + P] = 1
    for h in range(P // HD):
        c[h * HD:(h + 1) * HD, C_BLK + h * HD:C_BLK + (h + 1) * HD] = 1
    for m in range(P):
        if m % 32 < 16:
            c[m + 16, C_ROT + m] = -1
        else:
            c[m - 16, C_ROT + m] = 1
    for g, w in enumerate(WIN):
        for t in range(8):
            c[:, C_EDGE + 16 * g + t] = w / min(w, t + w // 2)
            c[:, C_EDGE + 16 * g + 8 + t] = w / min(w, (8 - t) + w // 2)
    n_freq = HD // 4
    inv = (1.0 / (np.float32(10000.0) ** (np.arange(n_freq, dtype=np.float32) / np.float32(n_freq)))).astype(np.float32)
    pos = np.arange(LAT)
    row, col = (pos // 64).astype(np.float32), (pos % 64).astype(np.float32)
    c[:, C_COS:C_COS + T] = 1
    for p in range(P):
        d = p % HD
        ang = (row if d < HD // 2 else col) * inv[d % n_freq]
        c[p, C_COS + CTX:C_COS + T] = np.cos(ang)
        c[p, C_SIN + CTX:C_SIN + T] = np.sin(ang)
    return c


def kernel(**inputs):
    from concourse.bacc import Bacc
    from concourse.bass_utils import run_bass_kernel_spmd

    a = {k: np.asarray(v) for k, v in inputs.items()}

    def fm(v):
        return v.T.reshape(-1, P, v.shape[0]).transpose(1, 0, 2)

    def fv(v):
        return v.reshape(-1, P).T

    w = np.zeros((LAYERS * SLABS, P, KT * P), np.float32)
    vec = np.zeros((P, LAYERS, NV), np.float32)
    ada = np.empty((LAYERS, ADA, P, KT * P), np.float32)
    for l in range(LAYERS):
        slabs_of(l, *(a[k][l] for k in ("w_in", "w_attn_o", "pool_w", "w_pool_o", "w_conv_o", "w_out",
                                        "w_ffn_in", "w_ffn_out")), w[l * SLABS:(l + 1) * SLABS])
        ada[l] = a["w_ada"][l].reshape(KT, P, ADA, P).transpose(2, 1, 0, 3).reshape(ADA, P, KT * P)
        vec[:, l, V_BADA:V_BADA + ADA] = fv(a["b_ada"][l])
        for col, k in ((V_GPRE1, "g_pre1"), (V_GPOST1, "g_post1"), (V_GPRE2, "g_pre2"), (V_GPOST2, "g_post2"),
                       (V_PS, "pool_scale"), (V_CB, "conv_b"), (V_LG, "conv_ln_g"), (V_LB, "conv_ln_b")):
            m = fv(a[k][l])
            vec[:, l, col:col + m.shape[1]] = m
        for col, k in ((V_QN, "q_norm"), (V_KN, "k_norm")):
            for h in range(P // HD):
                vec[h * HD:(h + 1) * HD, l, col] = a[k][l]
        vec[:, l, V_DW:V_DW + BR * TAPS] = a["conv_dw"][l].T.reshape(BR, P, TAPS).transpose(1, 0, 2).reshape(P, -1)
    arrays = {
        "x": np.ascontiguousarray(fm(np.concatenate([a["ctx"][0], a["x"][0]], 0))),
        "c": np.ascontiguousarray(fm(np.stack([a["c"][0], a["c_ctx"]], 0))),
        "w": w, "ada": ada, "vec": vec, "const": constants(),
    }

    def core():
        nc = Bacc("TRN2", target_bir_lowering=False, num_devices=1, dynamic_dma_scratch_size=1024)
        io = {k: nc.dram_tensor(f"in_{k}", v.shape, F32, kind="ExternalInput").ap() for k, v in arrays.items()}
        io["xs"] = nc.dram_tensor("x_between", (P, KT, T), F32).ap()
        io["out"] = nc.dram_tensor("out", (P, KT, LAT), F32, kind="ExternalOutput").ap()
        return nc, io

    nc, io = core()
    program(nc, core(), io)
    r = run_bass_kernel_spmd(nc, [{f"in_{k}": v for k, v in arrays.items()}], core_ids=[0])
    out = r.results[0]["out"]
    return out.transpose(1, 0, 2).reshape(D, LAT).T.reshape(1, LAT, D)
```

```python
from contextlib import ExitStack, contextmanager

import numpy as np
import concourse.bass as bass
from concourse import mybir

F32 = mybir.dt.float32
F32R = mybir.dt.float32r
ACT = mybir.ActivationFunctionType
ALU = mybir.AluOpType
AX = mybir.AxisListType

P = 128
D = 1024
KT = D // P
CTX, LAT = 256, 512
T = CTX + LAT
LAYERS = 2
HD = 64
HEADS = 8
KV = 2
EPS = 1e-6
BR = 4
TAPS = 31
HALF = TAPS // 2
WIN = (2, 4, 8, 16)
D_FF = 2816
FT = D_FF // P
GROUPS = (8, 8, 6)
RING = 4
RAW = 2
ADA = 48

S_K, S_V, S_Q, S_CONV, S_P0, S_POOL, S_P1, S_P2, S_OUT, S_FF = 0, 2, 4, 8, 16, 32, 40, 56, 72, 80
FF_IN, FF_OUT = [], []
_s = S_FF
for _n in GROUPS:
    FF_IN.append(_s)
    FF_OUT.append(_s + 2 * _n)
    _s += 2 * _n + KT
SLABS = _s
POOL_ORDER = (("u", 0), ("u", 1), ("w", 0), ("u", 2), ("w", 1), ("u", 3), ("w", 2), ("w", 3))

ADA_PE = 2 * KT
ADA_STEPS = {}
for _ly, _phase, _first, _width in ((0, "p1", S_P1, 2), (0, "out", S_OUT, 1), (0, "ffo0", FF_OUT[0], 1),
                                    (0, "ffo1", FF_OUT[1], 1), (1, "p1", SLABS + S_P1, 2)):
    for _j in range(KT):
        ADA_STEPS[(_ly, _phase, _j)] = (ADA_PE + 2 * len(ADA_STEPS), _first + _width * _j)
assert ADA_PE + 2 * len(ADA_STEPS) == LAYERS * ADA

V_BADA, V_GPRE1, V_GPOST1, V_GPRE2, V_GPOST2 = 0, 48, 56, 64, 72
V_QN, V_KN, V_PS, V_DW = 80, 81, 82, 86
V_CB = V_DW + BR * TAPS
V_LG, V_LB = V_CB + BR, V_CB + 2 * BR
NV = V_LB + BR
C_ID, C_ONE, C_BLK, C_ROT, C_EDGE, C_COS, C_SIN = 0, 128, 256, 384, 512, 576, 576 + T
NC = C_SIN + T

TT = T // P
TOK = {"post1": 0, "post2": 0, "pre1": TT, "pre2": TT, "conv": 2 * TT, "k": 3 * TT, "q": 5 * TT}
NTOK = 5 * TT + TT * HEADS

GC, GL = HALF, HALF + CTX + HALF
GW = GL + LAT + HALF
CW = GW - 2 * HALF
UC, UL = 8, 8 + CTX + 8
UW = UL + LAT + 8


def slab_blocks(s):
    if S_P0 <= s < S_POOL or S_P1 <= s < S_OUT:
        return 4 if s % 2 else 8
    if S_POOL <= s < S_P1:
        return 1 if POOL_ORDER[s - S_POOL][0] == "w" else 8
    for g, n in enumerate(GROUPS):
        if FF_OUT[g] <= s < FF_OUT[g] + KT:
            return n
    return 8


def build(nc, io, known):
    noted, strides = {}, {}
    old_marks, old_strides = known

    class Tally:

        def __init__(self, name):
            self.name, self.sem, self.n = name, ctx.enter_context(nc.semaphore(name)), 0
            self.start, self.key, self.i = None, None, None
            tallies[name] = self

        def up(self, *name):
            self.n += 1
            if name:
                assert name not in noted, name
                noted[name] = (self.name, self.n, self.key)
            return self.sem, 1

        def ago(self, back=0):
            v = self.n - back
            if self.key is None:
                return self.sem, max(v, 1)
            return self.sem, self.i * old_strides.get((self.key, self.name), 0) + max(v, 1)

    tallies = {}

    def seen(*name, i=None, back=0):
        if name not in old_marks:
            assert not old_marks, name
            return tallies["rounded"].sem, 1
        tally, value, key = old_marks[name]
        if key is None or i is None:
            assert key is None or back == 0, name
            return tallies[tally].sem, value
        stride = old_strides[(key, tally)]
        return tallies[tally].sem, i * stride + (value - back * stride)

    @contextmanager
    def repeat(eng, count, *key):
        with eng.Fori(0, count) as i:
            for t in tallies.values():
                t.start = t.n
            mine = (eng_name[id(eng)],) + key
            for t in tallies.values():
                t.key, t.i = mine, i
            yield i
            for t in tallies.values():
                d = t.n - t.start
                strides[(mine, t.name)] = d
                t.n += d * (count - 1)
                t.key = t.i = None

    eng_name = {}

    ctx = ExitStack()
    with ctx:
        def sb(name, shape, dt=F32):
            return ctx.enter_context(nc.sbuf_tensor(name, [P] + shape, dt))

        def overlay(name, size, *layouts):
            out = []
            for layout in layouts:
                with ExitStack() as open_:
                    for n, shape, dt in layout:
                        out.append(open_.enter_context(nc.sbuf_tensor(n, [P] + shape, dt)))
            sb(name, [size // 4])
            return out

        x, pt0h, pt0l, cg, cacc, ct, ml = overlay(
            "region_x", 4 * BR * (GW + CW) + 32,
            [("x", [KT, T], F32)],
            [("pt0h", [6, LAT], F32R), ("pt0l", [6, LAT], F32R)],
            [("conv_in", [BR, GW], F32), ("conv_acc", [BR, CW], F32)],
            [("conv_norm", [BR, T], F32)],
            [("merged_l", [KT, T], F32R)])
        pt1h, pt1l, acc = overlay(
            "region_acc", 4 * KT * T,
            [("pt1h", [6, LAT], F32R), ("pt1l", [6, LAT], F32R)],
            [("acc", [KT, T], F32)])
        half = 4 * KT * T
        (qs, kk, vh, vl, pr, o_raw, pad1, oh, ol, yph, ypl, dh, dl, pad2, ych, ycl, mh, midh, midl,
         ns) = overlay(
            "region_m", 2 * half,
            [("q_split", [HEADS, T], F32R), ("k_split", [2 * KV, T], F32R), ("v_h", [6, P], F32R),
             ("v_l", [6, P], F32R), ("probs", [2, T], F32)],
            [("o_raw", [BR, 2 * T], F32)],
            [("pad1", [half // 4], F32), ("o_h", [BR, T], F32R), ("o_l", [BR, T], F32R)],
            [("pool_h", [BR, T], F32R), ("pool_l", [BR, T], F32R), ("dev_h", [T], F32R),
             ("dev_l", [T], F32R)],
            [("pad2", [half // 4], F32), ("conv_h", [BR, T], F32R), ("conv_l", [BR, T], F32R)],
            [("merged_h", [KT, T], F32R)],
            [("mid_h", [KT, T], F32R), ("mid_l", [KT, T], F32R)],
            [("norm_tmp", [7, T], F32)])
        hh, hl = sb("h_h", [KT, T], F32R), sb("h_l", [KT, T], F32R)
        raw = sb("w_raw", [RAW, KT * P])
        wh, wl = sb("w_h", [RING, KT * P], F32R), sb("w_l", [RING, KT * P], F32R)
        ada_raw = sb("ada_raw", [2, KT * P])
        t1, t2, t3 = (sb(n, [800]) for n in ("t1", "t2", "t3"))
        const = sb("const", [NC])
        vec = sb("vec", [LAYERS, NV])
        cvec, silu_c = sb("cvec", [KT, 2]), sb("silu_c", [KT, 2])
        c_row = sb("c_row", [2, D])
        mod = sb("mod", [LAYERS, ADA, 2])
        gain = sb("gain", [LAYERS, 4, KT, 2])
        ust = sb("unit_stats", [4, 8])
        token_rs = sb("token_rs", [NTOK])
        ps = ctx.enter_context(nc.psum_tensor("ps", [P, 8, 512], F32))
        psf = ps[:].rearrange("p b n -> p (b n)")
        A = [psf[:, 0:1024], psf[:, 1024:2048]]
        B = psf[:, 2048:3072]
        O = psf[:, 3072:3584]
        DD = psf[:, 3584:4096]
        OD = psf[:, 3072:4096]

        def token_sum(kind, c, n):
            c += 2048 if kind in ("post1", "post2", "conv") else 3072
            return psf[:, c:c + n]

        ident, ones = const[:, C_ID:C_ID + P], const[:, C_ONE:C_ONE + P]
        blk, rot = const[:, C_BLK:C_BLK + P], const[:, C_ROT:C_ROT + P]
        cos, sin = const[:, C_COS:C_COS + T], const[:, C_SIN:C_SIN + T]

        def sem(name):
            return ctx.enter_context(nc.semaphore(name))

        w_loaded = [sem(f"w_loaded{k}") for k in range(RAW)]
        ada_loaded = [sem(f"ada_loaded{k}") for k in range(2)]
        const_loaded, c_row_loaded, x_stored, out_stored = (
            sem(n) for n in ("const_loaded", "c_row_loaded", "x_stored", "out_stored"))
        x_loaded = [sem(f"x_loaded{k}") for k in range(KT)]
        rounded, split, used = Tally("rounded"), sem("split"), sem("used")
        ada_sum = Tally("ada_sum")
        ada_dot = Tally("ada_dot")
        pe_done = Tally("pe_done")
        act_tmp = Tally("act_tmp")
        act_hi = Tally("act_hi")
        act_out = Tally("act_out")
        dve_tmp = Tally("dve_tmp")
        dve_lo = Tally("dve_lo")
        dve_out = Tally("dve_out")
        pool_norm = Tally("pool_norm")
        dve_tap = Tally("dve_tap")

        def lo_of(ly):
            return 0 if ly == 0 else CTX

        def chunks(lo):
            return ([(0, CTX, 1)] if lo == 0 else []) + [(CTX, T, 0)]

        def at(w, c0, c1):
            return w[:, 256 + c0:256 + c1]

        def units(ly):
            out, b = [], 0
            for h in range(HEADS):
                for q0, nq, nk in ([(CTX, 4, T)] + ([(0, 2, CTX)] if ly == 0 else [])):
                    out += [(h, q0, nk, q, nq, b) for q in range(nq)]
                    b += 1
            return out

        def value_steps(us):
            todo, out = [], {}
            for u in range(2, len(us) + 2):
                if us[u - 2][3] == us[u - 2][4] - 1:
                    parts = 1 if us[u - 2][2] == CTX else 3
                    todo += [(u - 2, part, parts) for part in range(parts)]
                n = 1 if u < len(us) + 1 else len(todo)
                out[u], todo = todo[:n], todo[n:]
            return out

        def q_scale(unit):
            h, q0, nk, q, nq, b = unit
            c = TOK["q"] + (q0 // P + q) * HEADS + h
            return token_rs[:, c:c + 1]

        pool_adds, pool_lows = (0, 2, 4, 6), (1, 3, 5)

        def norm_tile(n):
            return ns[:, (2, 3, 6)[n % 3]]

        block = ctx.enter_context(nc.Block())

        @block.sync
        def _(sp):
            eng_name[id(sp)] = "sp"
            total = LAYERS * SLABS

            def load(s, blocks, i=None):
                if s >= RAW or i is not None:
                    sp.wait_ge(split, s - RAW + 1 if i is None else i * RING + (s - RAW + 1))
                src = io["w"][s] if i is None else io["w"][bass.ds(i * RING + s, 1)].rearrange(
                    "a p n -> (a p) n")
                sp.dma_start(raw[:, s % RAW, 0:blocks * P], src[:, 0:blocks * P]).then_inc(
                    w_loaded[s % RAW], 16)

            def load_ada(k):
                if k >= 2:
                    sp.wait_ge(*seen("ada", k - 2))
                sp.dma_start(ada_raw[:, k % 2, :], io["ada"][k // ADA, k % ADA]).then_inc(ada_loaded[k % 2], 16)

            def load_run(a, b):
                s = a
                while s < b:
                    pat = [slab_blocks((s + k) % SLABS) for k in range(RING)]
                    n = 0
                    while s % RING == 0 and s + RING * (n + 1) <= b and pat == [
                            slab_blocks((s + RING * n + k) % SLABS) for k in range(RING)]:
                        n += 1
                    if n >= 2 and s >= RAW:
                        with sp.Fori(0, n) as i:
                            for k in range(RING):
                                load(s + k, pat[k], i)
                        s += RING * n
                    else:
                        load(s, pat[0])
                        s += 1

            for k in range(ADA_PE):
                load_ada(k)
            sp.dma_start(c_row[:], io["c_row"]).then_inc(c_row_loaded, 16)
            at_s = 0
            for k, slab in ADA_STEPS.values():
                stop = min(slab + RING + 1, total)
                load_run(at_s, stop)
                at_s = stop
                load_ada(k)
                load_ada(k + 1)
            load_run(at_s, total)

        @block.gpsimd
        def _(pool):
            eng_name[id(pool)] = "pool"

            def split_slab(s, i=None):
                pool.wait_ge(rounded.sem, s + 1 if i is None else i * RING + (s + 1))
                nc.gpsimd.tensor_tensor(wl[:, s % RING, :], raw[:, s % RAW, :], wh[:, s % RING, :],
                                        ALU.subtract).then_inc(split, 1)

            def split_run(a, b):
                n = (b - a) // RING
                if n:
                    with pool.Fori(0, n) as i:
                        for k in range(RING):
                            split_slab(a + k, i)
                for s in range(a + RING * n, b):
                    split_slab(s)

            def residual(ly, st, lo, reload):
                for k in range(KT):
                    if k in pool_adds:
                        if reload:
                            pool.wait_ge(x_loaded[k], reload)
                        pool.wait_ge(*seen("rt", ly, st, k))
                        nc.gpsimd.tensor_tensor(x[:, k, lo:T], x[:, k, lo:T], norm_tile(k)[:, lo:T], ALU.add).then_inc(
                            *pool_norm.up("x", ly, st, k))

            def lows(ly, st, lo):
                for k in pool_lows:
                    pool.wait_ge(*seen("hh", ly, st, k))
                    nc.gpsimd.tensor_tensor(hl[:, k, lo:T], norm_tile(k)[:, lo:T], hh[:, k, lo:T],
                                            ALU.subtract).then_inc(*pool_norm.up("hl", ly, st, k))

            at_s = RING - 1
            split_run(0, at_s)
            lows(0, "pre1", 0)
            for ly in range(LAYERS):
                lo = lo_of(ly)
                stop = ly * SLABS + S_FF + RING - 1
                split_run(at_s, stop)
                residual(ly, "post1", lo, 16 * (ly + 2))
                lows(ly, "pre2", lo)
                at_s = min((ly + 1) * SLABS + RING - 1, LAYERS * SLABS)
                split_run(stop, at_s)
                residual(ly, "post2", lo, None)
                if ly == 0:
                    lows(1, "pre1", 0)

        @block.tensor
        def _(pe):
            eng_name[id(pe)] = "pe"
            last_use = {}

            def take(w, *name):
                if w in last_use:
                    pe.wait_ge(*seen("free", *last_use[w]))
                last_use[w] = name

            def gemm(out, slabs, xh, xl, cols, i=None, k_ready=None, start_k=0, n_k=None):
                kt = 0
                n_k = sum(nb for _, nb in slabs)
                for s, nb in slabs:
                    pe.wait_ge(split, s + 1 if i is None else i * RING + (s + 1))
                    for b in range(nb):
                        if k_ready is not None:
                            pe.wait_ge(*k_ready(kt))
                        for n, (w, m) in enumerate(((wh, xh), (wh, xl), (wl, xh))):
                            for c0, c1, _ in cols:
                                ins = nc.tensor.matmul(
                                    at(out, c0, c1), w[:, s % RING, b * P:(b + 1) * P], m[:, kt, c0:c1],
                                    start=(kt == 0 and n == 0), stop=(kt == n_k - 1 and n == 2))
                        kt += 1
                    ins.then_inc(used, 1)

            def ada(g):
                take("D", "ada", 0, g)
                for k in range(KT * g, KT * (g + 1)):
                    pe.wait_ge(ada_loaded[k % 2], 16 * (k // 2 + 1))
                    t = k % KT
                    for b in range(KT):
                        ins = nc.tensor.matmul(DD[:, 2 * t:2 * t + 2], ada_raw[:, k % 2, b * P:(b + 1) * P],
                                               silu_c[:, b, :], start=(b == 0), stop=(b == KT - 1))
                    ins.then_inc(*ada_sum.up("ada", k))

            def sums(mat, src, cols, need, *name, w="B"):
                take(w, *name)
                pe.wait_ge(*seen(*need))
                for c0, c1, _ in cols:
                    ins = nc.tensor.matmul(at(B if w == "B" else OD, c0, c1), mat, src(c0, c1), start=True, stop=True)
                ins.then_inc(*pe_done.up(*name))

            def token_sums(src, lo, kind, start=True, stop=True):
                for t in range(lo // P, TT):
                    first, last = t == lo // P, t == TT - 1
                    ins = nc.tensor.matmul(token_sum(kind, TOK[kind] + t, 1), src[:, t * P:(t + 1) * P], ones[:, 0:1],
                                           start=start and first, stop=stop and last)
                return ins

            def head_sums(src, lo, col, per_tile):
                for t in range(lo // P, TT):
                    c = col + t * per_tile
                    ins = nc.tensor.matmul(token_sum("q", c, 2), src[:, t * P:(t + 1) * P],
                                           blk[:, 0:P:HD], start=True, stop=True)
                return ins

            def spread(lo, kind, *name, heads=1):
                take("B", "spread", *name)
                pe.wait_ge(*seen("rs", *name))
                rows = P // heads
                for t in range(lo // P, TT):
                    for h in range(heads):
                        c = TOK[kind] + t * heads + h
                        ins = nc.tensor.matmul(at(B, t * P, (t + 1) * P)[h * rows:(h + 1) * rows],
                                               token_rs[:, c:c + 1].to_broadcast([P, rows]), ident,
                                               start=True, stop=True)
                ins.then_inc(*pe_done.up("spread", *name))

            def square_sums(ly, st, lo):
                for k in range(KT):
                    pe.wait_ge(*seen("sq", ly, st, k))
                    token_sums(ns[:, 4 + k % 2, :], lo, st, start=(k == 0), stop=(k == KT - 1)).then_inc(
                        *pe_done.up("sqsum", ly, st, k))
                noted[("stat", ly, st)] = noted[("sqsum", ly, st, KT - 1)]

            def t_cols(t):
                return lambda c0, c1: t[:, c0:c1]

            pe.wait_ge(const_loaded, 16 * 3)
            pe.wait_ge(*seen("silu"))
            ada(0)
            ada(1)
            take("D", "end")
            del last_use["D"]
            for ly in range(LAYERS):
                s0 = ly * SLABS
                lo = lo_of(ly)
                cols, full = chunks(lo), chunks(0)

                def pre_ready(k):
                    return seen("hl", ly, "pre1", k)

                square_sums(ly, "pre1", 0)
                spread(0, "pre1", ly, "pre1")

                tiles = ["k", "v", "q0", "q1", "q2", "q3"]

                def finish(n):
                    c = full if n in "kv" else cols
                    if n == "v":
                        take("B", "vt", ly)
                        pe.wait_ge(*seen("vcopy", ly))
                        for k in range(6):
                            ins = nc.tensor.transpose(at(B, k * P, (k + 1) * P), t1[:, k * P:(k + 1) * P], ident)
                        ins.then_inc(*pe_done.up("vt", ly))
                    else:
                        pe.wait_ge(*seen("tsq", ly, n))
                        if "OD" in last_use:
                            pe.wait_ge(*seen("free", *last_use["OD"]))
                        col, per = (TOK["k"], 2) if n == "k" else (TOK["q"] + 2 * int(n[1]), HEADS)
                        head_sums(t1, c[0][0], col, per).then_inc(*pe_done.up("stat", ly, n))
                        sums(rot, t_cols(t2), c, ("free", "gemm", ly, n), "rot", ly, n, w="OD")
                        if n == "k":
                            spread(0, "k", ly, "k", heads=KV)

                for n, name in enumerate(tiles):
                    w = n % 2
                    take(w, "gemm", ly, name)
                    if name in "kv":
                        s = s0 + (S_K if name == "k" else S_V)
                        gemm(A[w], [(s, 4), (s + 1, 4)], hh, hl, full,
                             k_ready=pre_ready if name == "k" else None)
                    else:
                        gemm(A[w], [(s0 + S_Q + n - 2, 8)], hh, hl, cols)
                    if n:
                        finish(tiles[n - 1])
                finish(tiles[-1])

                us = units(ly)

                def scores(u):
                    h, q0, nk, q, nq, b = us[u]
                    take(u % 2, "scores", ly, u)
                    if u == 0:
                        pe.wait_ge(*seen("tile", ly, "k"))
                    if q == 0:
                        pe.wait_ge(*seen("tile", ly, f"q{h // 2}"))
                    ks = [(0, CTX), (CTX, T)] if nk == T else [(0, CTX)]
                    for part in range(2):
                        for c0, c1 in ks:
                            ins = nc.tensor.matmul(
                                at(A[u % 2], c0, c1), qs[:, h, q0 + q * P:q0 + (q + 1) * P],
                                kk[:, 2 * (h // 4) + part, c0:c1], start=(part == 0), stop=(part == 1))
                    ins.then_inc(*pe_done.up("scores", ly, u))

                def transposes(u):
                    h, q0, nk, q, nq, b = us[u]
                    take("B", "pt", ly, u)
                    pe.wait_ge(*seen("normed", ly, u))
                    for k in range(nk // P):
                        ins = nc.tensor.transpose(at(B, k * P, (k + 1) * P), pr[:, u % 2, k * P:(k + 1) * P], ident)
                    ins.then_inc(*pe_done.up("pt", ly, u))

                def values(u, part, parts):
                    h, q0, nk, q, nq, b = us[u]
                    if b == 0 and part == 0:
                        take("OD", "pvs", ly)
                        del last_use["OD"]
                    if part == 0:
                        take("O", "pv", ly, b)
                        if b == 0:
                            pe.wait_ge(*seen("tile", ly, "v"))
                        pe.wait_ge(*seen("free", "pt", ly, u))
                    ph, pl = ((pt0h, pt0l), (pt1h, pt1l))[b % 2]
                    d0 = HD * (h // 4)
                    share = nk // P // parts
                    for k in range(part * share, (part + 1) * share):
                        for n, (v, p) in enumerate(((vh, ph), (vh, pl), (vl, ph))):
                            ins = nc.tensor.matmul(O[0:HD, 0:nq * P], v[:, k, d0:d0 + HD], p[:, k, 0:nq * P],
                                                   start=(k == 0 and n == 0), stop=(k == nk // P - 1 and n == 2))
                    if part == parts - 1:
                        ins.then_inc(*pe_done.up("pv", ly, b))

                scores(0)
                plan = value_steps(us)
                for u in range(len(us) + 2):
                    if u + 1 < len(us):
                        scores(u + 1)
                    if 1 <= u <= len(us):
                        transposes(u - 1)
                    for step in plan.get(u, ()):
                        values(*step)

                for j in range(BR):
                    s = s0 + S_CONV + 2 * j
                    take(0, "cgate", ly, j)
                    gemm(A[0], [(s, 8)], hh, hl, cols)
                    take(1, "cval", ly, j)
                    gemm(A[1], [(s + 1, 8)], hh, hl, cols)

                def branch(b, xh, xl, j, i=None, parity=0, ready=None):
                    s = s0 + (S_P0, S_P1, S_P2)[b] + (2 * j if i is None else 2 * parity)
                    gemm(A[0], [(s, 8)], hh, hl, cols, i)
                    if i is None:
                        take(1, "value", ly, b, j)
                    else:
                        pe.wait_ge(*seen("free", "value", ly, b, 1 - parity, i=i, back=1 - parity))
                    gemm(A[1], [(s + 1, 4)], xh, xl, cols, i, ready)

                def branch_loop(b, xh, xl, ready):
                    for w in range(2):
                        take(w, "gate" if w == 0 else "value", ly, b, 1)
                    pe.wait_ge(*ready)
                    with repeat(pe, KT // 2, ly, "branch", b) as i:
                        for c in range(2):
                            pe.wait_ge(*seen("free", "gate", ly, b, 1 - c, i=i, back=1 - c))
                            branch(b, xh, xl, None, i, c)

                branch_loop(0, oh, ol, seen("ol", ly, BR - 1))
                last_use[0], last_use[1] = ("gateend", ly, 0), ("valueend", ly, 0)
                pe.wait_ge(*seen("free", "gate", ly, 0, 1, i=KT // 2 - 1))
                pe.wait_ge(*seen("free", "value", ly, 0, 1, i=KT // 2 - 1))
                del last_use[0], last_use[1]

                for n, (kind, g) in enumerate(POOL_ORDER):
                    s = s0 + S_POOL + n
                    if kind == "u":
                        take(0, "pin", ly, g)
                        gemm(A[0], [(s, 8)], hh, hl, cols)
                    else:
                        take(1, "pout", ly, g)
                        gemm(A[1], [(s, 1)], dh[:].rearrange("p (a t) -> p a t", a=1),
                             dl[:].rearrange("p (a t) -> p a t", a=1), cols,
                             k_ready=lambda k: seen("dl", ly, g))

                for j in range(KT):
                    if j == 2:
                        sums(ones, lambda c0, c1: cacc[:, 0, c0:c1], cols, ("cysum", ly), "cmu", ly)
                    if j == 4:
                        pe.wait_ge(*seen("cqsum", ly))
                        token_sums(cacc[:, 0, :], lo, "conv").then_inc(*pe_done.up("stat", ly, "conv"))
                    if j == 5:
                        spread(lo, "conv", ly, "conv")
                    take(0, "gate", ly, 1, j)
                    branch(1, yph, ypl, j, ready=(lambda k: seen("ypl", ly, k)) if j == 0 else None)

                branch_loop(2, ych, ycl, seen("ycl", ly, BR - 1))
                pe.wait_ge(*seen("free", "gate", ly, 2, 1, i=KT // 2 - 1))
                pe.wait_ge(*seen("free", "value", ly, 2, 1, i=KT // 2 - 1))
                del last_use[0], last_use[1]

                for j in range(KT):
                    take(j % 2, "out", ly, j)
                    gemm(A[j % 2], [(s0 + S_OUT + j, 8)], mh, ml, cols,
                         k_ready=(lambda k: seen("ml", ly, k % 2, i=k // 2)) if j == 0 else None)
                pe.wait_ge(*seen("ysum", ly, "post1"))
                token_sums(t3, lo, "post1").then_inc(*pe_done.up("stat", ly, "post1"))
                spread(lo, "post1", ly, "post1")
                square_sums(ly, "pre2", lo)
                spread(lo, "pre2", ly, "pre2")

                for k in range(2):
                    if k in last_use:
                        pe.wait_ge(*seen("free", *last_use.pop(k)))
                for g, nf in enumerate(GROUPS):
                    if g == 0:
                        for k in range(KT):
                            pe.wait_ge(*seen("hl", ly, "pre2", k))
                    s = s0 + FF_IN[g]
                    with repeat(pe, nf // 2, ly, "ffin", g) as i:
                        for c in range(2):
                            pe.wait_ge(*seen("free", "ffa", ly, g, 1 - c, i=i, back=1 - c))
                            gemm(A[0], [(s + 2 * c, 8)], hh, hl, cols, i)
                            pe.wait_ge(*seen("free", "ffb", ly, g, 1 - c, i=i, back=1 - c))
                            gemm(A[1], [(s + 2 * c + 1, 8)], hh, hl, cols, i)
                    pe.wait_ge(*seen("free", "ffa", ly, g, 1, i=nf // 2 - 1))
                    pe.wait_ge(*seen("free", "ffb", ly, g, 1, i=nf // 2 - 1))
                    s = s0 + FF_OUT[g]
                    for j in range(KT):
                        take(j % 2, "ffo", ly, g, j)
                        gemm(A[j % 2], [(s + j, nf)], midh, midl, cols,
                             k_ready=(lambda k: seen("midl", ly, g, k % 2, i=k // 2)) if j == 0 else None)
                    for k in range(2):
                        pe.wait_ge(*seen("free", *last_use.pop(k)))
                pe.wait_ge(*seen("ysum", ly, "post2"))
                token_sums(t3, lo, "post2").then_inc(*pe_done.up("stat", ly, "post2"))
                spread(lo, "post2", ly, "post2")

        @block.scalar
        def _(act):
            eng_name[id(act)] = "act"
            nxt = [0]
            total = LAYERS * SLABS

            def round_slab(s, i=None):
                nb = slab_blocks(s % SLABS) if s >= RING else 8
                if i is None:
                    act.wait_ge(w_loaded[s % RAW], 16 * (s // RAW + 1))
                    if s >= RING:
                        act.wait_ge(used, s - RING + 1)
                else:
                    act.wait_ge(w_loaded[s % RAW], i * (16 * RING // RAW) + 16 * (s // RAW + 1))
                    act.wait_ge(used, i * RING + (s - RING + 1))
                nc.scalar.activation(wh[:, s % RING, 0:nb * P], raw[:, s % RAW, 0:nb * P],
                                     ACT.Copy).then_inc(*rounded.up())

            def rounds(s):
                while nxt[0] <= min(s, total - 1):
                    round_slab(nxt[0])
                    nxt[0] += 1

            def result_of(s, i=None):
                if i is None:
                    rounds(s + RING - 1)
                else:
                    round_slab(s + RING - 1, i)
                act.wait_ge(used, s + 1 if i is None else i * RING + (s + 1))

            def sq_in(st, lo, x_ready):
                for k in range(KT):
                    act.wait_ge(*x_ready(k))
                    if k >= 2:
                        act.wait_ge(*seen("sqsum", *st, k - 2))
                    nc.scalar.activation(ns[:, 4 + k % 2, lo:T], x[:, k, lo:T],
                                         ACT.Square).then_inc(*act_tmp.up("sq", *st, k))

            def root(kind, n, *name, scale=1.0):
                act.wait_ge(*seen("var", *name))
                buf = token_rs[:, TOK[kind]:TOK[kind] + n]
                nc.scalar.activation(buf, buf, ACT.Sqrt, scale=scale).then_inc(*act_tmp.up("rs", *name))

            def h_high(ly, st, lo, shift):
                for k in range(KT):
                    act.wait_ge(*seen("t", ly, st, k))
                    t = norm_tile(k)
                    for c0, c1, s in chunks(lo):
                        ins = nc.scalar.activation(t[:, c0:c1] if k in pool_lows else hh[:, k, c0:c1], t[:, c0:c1],
                                                   ACT.Identity, bias=mod[:, ly, shift + k, s:s + 1])
                        if k in pool_lows:
                            ins.then_inc(*act_tmp.up())
                    if k in pool_lows:
                        act.wait_ge(*act_tmp.ago())
                        ins = nc.scalar.activation(hh[:, k, lo:T], t[:, lo:T], ACT.Copy)
                    ins.then_inc(*act_hi.up("hh", ly, st, k))

            act.dma_start(cvec[:], io["c"]).then_inc(const_loaded, 16)
            act.dma_start(vec[:], io["vec"]).then_inc(const_loaded, 16)
            act.dma_start(const[:], io["const"]).then_inc(const_loaded, 16)
            for k in range(KT):
                act.dma_start(x[:, k, :], io["x"][:, k, :]).then_inc(x_loaded[k], 16)
            act.wait_ge(const_loaded, 16 * 3)
            nc.scalar.activation(silu_c[:], cvec[:], ACT.Tanh, scale=0.5).then_inc(*act_tmp.up("ctanh"))

            for ly in range(LAYERS):
                s0 = ly * SLABS
                lo = lo_of(ly)
                cols, full = chunks(lo), chunks(0)

                if ly == 0:
                    sq_in((0, "pre1"), 0, lambda k: (x_loaded[k], 16))
                root("pre1", TT, ly, "pre1")
                rounds(s0 + RING - 1)
                h_high(ly, "pre1", 0, 0)

                prev = None
                for n, name in enumerate(["k", "v", "q0", "q1", "q2", "q3"]):
                    w, l0 = A[n % 2], (0 if name in "kv" else lo)
                    result_of(s0 + (S_K + 1, S_V + 1, S_Q, S_Q + 1, S_Q + 2, S_Q + 3)[n])
                    if prev:
                        act.wait_ge(*seen("tile", ly, prev))
                    if name == "v":
                        nc.scalar.activation(t1[:, 0:T], at(w, 0, T), ACT.Copy).then_inc(
                            *act_out.up("free", "gemm", ly, name))
                        noted[("vcopy", ly)] = noted[("free", "gemm", ly, name)]
                        act.wait_ge(*seen("vt", ly))
                        nc.scalar.activation(vh[:].rearrange("p a b -> p (a b)"), at(B, 0, T),
                                             ACT.Copy).then_inc(*act_hi.up("vh", ly))
                    else:
                        nc.scalar.activation(t1[:, l0:T], at(w, l0, T), ACT.Square).then_inc(
                            *act_tmp.up("tsq", ly, name))
                        gcol = V_KN if name == "k" else V_QN
                        nc.scalar.activation(t2[:, l0:T], at(w, l0, T), ACT.Copy,
                                             scale=vec[:, ly, gcol:gcol + 1]).then_inc(
                            *act_out.up("free", "gemm", ly, name))
                        if name == "k":
                            root("k", 2 * TT, ly, "k")
                        act.wait_ge(*seen("roped", ly, name))
                        if name == "k":
                            for kv in range(KV):
                                for p in range(2):
                                    ins = nc.scalar.activation(kk[64 * p:64 * p + 64, 2 * kv, :],
                                                               t2[64 * kv:64 * kv + 64, 0:T], ACT.Copy)
                        else:
                            j = int(name[1])
                            for p in range(2):
                                ins = nc.scalar.activation(qs[64 * p:64 * p + 64, 2 * j + p, l0:T],
                                                           t2[64 * p:64 * p + 64, l0:T], ACT.Copy)
                        ins.then_inc(*act_hi.up("hi", ly, name))
                    prev = name
                root("q", HEADS * TT, ly, "q", scale=1.0 / HD)

                us = units(ly)
                act.wait_ge(*seen("tile", ly, "q3"))
                if ly:
                    act.wait_ge(x_stored, 16 * KT)

                def o_out(b, h, q0, nq):
                    act.wait_ge(*seen("pv", ly, b))
                    p = 64 * (h % 2)
                    nc.scalar.activation(o_raw[p:p + 64, h // 2, q0:q0 + nq * P], O[0:HD, 0:nq * P],
                                         ACT.Copy).then_inc(*act_out.up("free", "pv", ly, b))

                plan = value_steps(us)
                for u in range(len(us) + 3):
                    if u < len(us):
                        h, q0, nk, q, nq, b = us[u]
                        act.wait_ge(*seen("negmax", ly, u))
                        if u >= 2:
                            act.wait_ge(*seen("pt", ly, u - 2))
                        nc.scalar.activation(pr[:, u % 2, 0:nk], at(A[u % 2], 0, nk), ACT.Exp,
                                             bias=ust[:, 1, u % 8:u % 8 + 1], scale=q_scale(us[u]),
                                             accum_out=ust[:, 2, u % 8:u % 8 + 1]).then_inc(
                            *act_out.up("free", "scores", ly, u))
                    if 1 <= u <= len(us):
                        h, q0, nk, q, nq, b = us[u - 1]
                        act.wait_ge(*seen("pt", ly, u - 1))
                        if q == 0 and b >= 2:
                            act.wait_ge(*seen("pv", ly, b - 2))
                        ph = (pt0h, pt1h)[b % 2]
                        nc.scalar.activation(ph[:, 0:nk // P, q * P:(q + 1) * P],
                                             at(B, 0, nk).rearrange("p (k q) -> p k q", q=P),
                                             ACT.Copy).then_inc(*act_hi.up("pth", ly, u - 1))
                    for v, part, parts in plan.get(u - 1, ()):
                        if part == parts - 1:
                            h, q0, nk, q, nq, b = us[v]
                            o_out(b, h, q0, nq)
                act.wait_ge(*act_out.ago())
                for j in range(BR):
                    nc.scalar.activation(oh[:, j, lo:T], o_raw[:, j, lo:T], ACT.Copy).then_inc(
                        *act_hi.up("oh", ly, j))

                for j in range(BR):
                    result_of(s0 + S_CONV + 2 * j)
                    if j:
                        act.wait_ge(*seen("free", "cval", ly, j - 1))
                    nc.scalar.activation(t1[:, lo:T], at(A[0], lo, T), ACT.Tanh, scale=0.5).then_inc(
                        *act_out.up("free", "cgate", ly, j))
                    result_of(s0 + S_CONV + 2 * j + 1)

                def branch_loop(b):
                    s = s0 + (S_P0, S_P2)[b // 2]
                    with repeat(act, KT // 2, ly, "branch", b) as i:
                        for c in range(2):
                            result_of(s + 2 * c, i)
                            act.wait_ge(*seen("free", "value", ly, b, c, i=i, back=1))
                            tt = (t1, t3)[c]
                            nc.scalar.activation(tt[:, lo:T], at(A[0], lo, T), ACT.Tanh, scale=0.5).then_inc(
                                *act_out.up("free", "gate", ly, b, c))
                            round_slab(s + 2 * c + 1 + RING - 1, i)
                            if b == 2:
                                act.wait_ge(*seen("macc", ly, c, i=i))
                                nc.scalar.activation(mh[:, bass.ds(i * 2 + c, 1), lo:T].rearrange("p a t -> p (a t)"),
                                                     acc[:, bass.ds(i * 2 + c, 1), lo:T].rearrange("p a t -> p (a t)"),
                                                     ACT.Copy).then_inc(*act_hi.up("mh", ly, c))
                    nxt[0] += RING * (KT // 2)

                act.wait_ge(*seen("free", "cval", ly, BR - 1))
                branch_loop(0)

                if ly == 0:
                    act.wait_ge(c_row_loaded, 16)
                    for n in range(2):
                        if n:
                            act.wait_ge(*seen("c_silu", n - 1))
                        nc.scalar.activation(OD, c_row[:, n, :], ACT.Tanh, scale=0.5).then_inc(
                            *act_tmp.up("c_tanh", n))

                for n, (kind, g) in enumerate(POOL_ORDER):
                    result_of(s0 + S_POOL + n)
                    if kind == "u":
                        act.wait_ge(*(seen("dev", ly, g - 1) if g else seen("pads", ly)))
                        for c0, c1, s in cols:
                            u0 = UC if s else UL
                            ins = nc.scalar.activation(t1[:, u0:u0 + c1 - c0], at(A[0], c0, c1), ACT.Copy)
                        ins.then_inc(*act_out.up("free", "pin", ly, g))
                        if g:
                            act.wait_ge(used, s0 + S_POOL + POOL_ORDER.index(("w", g - 1)) + 1)
                        act.wait_ge(*seen("dev", ly, g))
                        d = (t3, t2)[g % 2]
                        for c0, c1, s in cols:
                            u0 = UC if s else UL
                            ins = nc.scalar.activation(dh[:, c0:c1], d[:, u0:u0 + c1 - c0], ACT.Copy)
                        ins.then_inc(*act_hi.up("dh", ly, g))
                    else:
                        nc.scalar.activation(yph[:, g, lo:T], at(A[1], lo, T), ACT.Copy,
                                             scale=vec[:, ly, V_PS + g:V_PS + g + 1]).then_inc(
                            *act_hi.up("yph", ly, g))

                def ln_y():
                    act.wait_ge(*seen("taps", ly))
                    for j in range(BR):
                        for c0, c1, s in cols:
                            src = 0 if s else GL - GC
                            ins = nc.scalar.activation(ct[:, j, c0:c1], cacc[:, j, src:src + c1 - c0],
                                                       ACT.Identity, scale=0.5,
                                                       bias=vec[:, ly, V_CB + j:V_CB + j + 1])
                        ins.then_inc(*act_tmp.up("cy", ly, j))

                def ln_sq():
                    for j in range(BR):
                        act.wait_ge(*seen("cc", ly, j))
                        if j >= 2:
                            act.wait_ge(*seen("cqadd", ly, j - 2))
                        nc.scalar.activation(cacc[:, 2 + j % 2, lo:T], ct[:, j, lo:T], ACT.Square).then_inc(
                            *act_tmp.up("csq", ly, j))

                def ln_act(j):
                    act.wait_ge(*seen("cn", ly, j))
                    if j >= 2:
                        act.wait_ge(*seen("cm", ly, j - 2))
                    nc.scalar.activation(ct[:, j, lo:T], ct[:, j, lo:T], ACT.Identity,
                                         scale=vec[:, ly, V_LG + j:V_LG + j + 1],
                                         bias=vec[:, ly, V_LB + j:V_LB + j + 1]).then_inc(*act_tmp.up())
                    act.wait_ge(*act_tmp.ago())
                    nc.scalar.activation(cacc[:, 2 + j % 2, lo:T], ct[:, j, lo:T], ACT.Tanh,
                                         scale=0.5).then_inc(*act_tmp.up("cth", ly, j))
                    act.wait_ge(*seen("cm", ly, j))
                    nc.scalar.activation(ych[:, j, lo:T], ct[:, j, lo:T], ACT.Copy, scale=0.5).then_inc(
                        *act_hi.up("ych", ly, j))

                for j in range(KT):
                    result_of(s0 + S_P1 + 2 * j)
                    if j >= 2:
                        act.wait_ge(*seen("free", "value", ly, 1, j - 2))
                    tt = (t1, t3)[j % 2]
                    nc.scalar.activation(tt[:, lo:T], at(A[0], lo, T), ACT.Tanh, scale=0.5).then_inc(
                        *act_out.up("free", "gate", ly, 1, j))
                    result_of(s0 + S_P1 + 2 * j + 1)
                    if j == 0:
                        ln_y()
                    elif j == 2:
                        ln_sq()
                    elif j == 3:
                        root("conv", TT, ly, "conv")
                    elif j in (5, 6):
                        ln_act(2 * (j - 5))
                        ln_act(2 * (j - 5) + 1)

                branch_loop(2)

                def y_out(j, w, scale, st):
                    if j >= 2:
                        act.wait_ge(*seen("yadd", ly, st, j - 2))
                    nc.scalar.activation((t1, t2)[j % 2][:, lo:T], at(w, lo, T), ACT.Square,
                                         scale=scale).then_inc(*act_tmp.up("ysq", ly, st, j))
                    nc.scalar.activation(acc[:, j, lo:T], at(w, lo, T), ACT.Copy, scale=scale).then_inc(
                        *act_out.up("free", "out", ly, j))

                for j in range(KT):
                    result_of(s0 + S_OUT + j)
                    if j == 0:
                        act.wait_ge(*seen("ml", ly, 1, i=KT // 2 - 1))
                    y_out(j, A[j % 2], 0.5, "post1")
                for k in range(KT):
                    act.dma_start(x[:, k, lo:T], (io["x"] if ly == 0 else io["xs"])[:, k, lo:T]).then_inc(
                        x_loaded[k], 16)
                root("post1", TT, ly, "post1")
                sq_in((ly, "pre2"), lo, lambda k: seen("x", ly, "post1", k))
                root("pre2", TT, ly, "pre2")
                h_high(ly, "pre2", lo, 3 * KT)

                for g, nf in enumerate(GROUPS):
                    s = s0 + FF_IN[g]
                    with repeat(act, nf // 2, ly, "ffin", g) as i:
                        for c in range(2):
                            f = bass.ds(i * 2 + c, 1)
                            result_of(s + 2 * c, i)
                            act.wait_ge(*seen("free", "ffa", ly, g, 1 - c, i=i, back=1 - c))
                            nc.scalar.activation(t1[:, lo:T], at(A[0], lo, T), ACT.Tanh, scale=0.5).then_inc(
                                *act_tmp.up("fth", ly, g, c))
                            round_slab(s + 2 * c + 1 + RING - 1, i)
                            act.wait_ge(*seen("free", "ffb", ly, g, c, i=i))
                            nc.scalar.activation(midh[:, f, lo:T].rearrange("p a t -> p (a t)"), t3[:, lo:T],
                                                 ACT.Copy).then_inc(*act_hi.up("midh", ly, g, c))
                    nxt[0] += RING * (nf // 2)
                    for j in range(KT):
                        result_of(s0 + FF_OUT[g] + j)
                        if g == 0:
                            nc.scalar.activation(acc[:, j, lo:T], at(A[j % 2], lo, T), ACT.Copy).then_inc(
                                *act_out.up("free", "ffo", ly, g, j))
                        elif g == 2:
                            act.wait_ge(*seen("free", "ffo", ly, g, j))
                            if j >= 2:
                                act.wait_ge(*seen("yadd", ly, "post2", j - 2))
                            nc.scalar.activation((t1, t2)[j % 2][:, lo:T], acc[:, j, lo:T], ACT.Square).then_inc(
                                *act_tmp.up("ysq", ly, "post2", j))
                root("post2", TT, ly, "post2")
                if ly == 0:
                    for k in range(KT):
                        act.wait_ge(*seen("x", ly, "post2", k))
                        act.dma_start(io["xs"][:, k, :], x[:, k, :]).then_inc(x_stored, 16)
                    sq_in((1, "pre1"), 0, lambda k: seen("x", 0, "post2", k))
                else:
                    for k in range(KT):
                        act.wait_ge(*seen("x", ly, "post2", k))
                        act.dma_start(io["out"][:, k, :], x[:, k, CTX:T]).then_inc(out_stored, 16)
                    act.wait_ge(out_stored, 16 * KT)

        @block.vector
        def _(dve):
            eng_name[id(dve)] = "dve"
            v = nc.vector

            def link(ins, tally, *name):
                ins.then_inc(*tally.up(*name))
                dve.wait_ge(*tally.ago())

            def variance(kind, first, cols, n, *name):
                dve.wait_ge(*seen("stat", *name))
                c = TOK[kind] + first
                buf = token_rs[:, c:c + cols]
                link(v.tensor_scalar(buf, token_sum(kind, c, cols), 1.0 / n, EPS, ALU.mult, ALU.add), dve_tmp)
                link(v.reciprocal(buf, buf), dve_tmp, "var", *name)

            def normalise(ly, st, lo, which, shift):
                dve.wait_ge(*seen("spread", ly, st))

                def low(k):
                    dve.wait_ge(*seen("hh", ly, st, k))
                    for c0, c1, s in chunks(lo):
                        ins = v.scalar_tensor_tensor(out=hl[:, k, c0:c1], in0=norm_tile(k)[:, c0:c1],
                                                     scalar=mod[:, ly, shift + k, s:s + 1], in1=hh[:, k, c0:c1],
                                                     op0=ALU.add, op1=ALU.subtract)
                        ins.then_inc(*(dve_lo.up("hl", ly, st, k) if s == 0 else dve_lo.up()))

                for k in range(KT):
                    if k >= 3:
                        dve.wait_ge(*seen("hl", ly, st, k - 3))
                    for c0, c1, s in chunks(lo):
                        ins = v.scalar_tensor_tensor(
                            out=norm_tile(k)[:, c0:c1], in0=x[:, k, c0:c1],
                            scalar=gain[:, ly, which, k, s:s + 1], in1=at(B, c0, c1),
                            op0=ALU.mult, op1=ALU.mult)
                        ins.then_inc(*(dve_tmp.up("t", ly, st, k) if s == 0 else dve_tmp.up()))
                    if k and k - 1 not in pool_lows:
                        low(k - 1)
                noted[("free", "spread", ly, st)] = noted[("t", ly, st, KT - 1)]
                low(KT - 1)

            def residual(ly, st, lo, which, reload):
                dve.wait_ge(*seen("spread", ly, st))
                for k in range(KT):
                    if k >= 3:
                        dve.wait_ge(*seen("x", ly, st, k - 3))
                    for c0, c1, s in chunks(lo):
                        ins = v.scalar_tensor_tensor(
                            out=norm_tile(k)[:, c0:c1], in0=acc[:, k, c0:c1],
                            scalar=gain[:, ly, which, k, s:s + 1], in1=at(B, c0, c1),
                            op0=ALU.mult, op1=ALU.mult)
                        ins.then_inc(*(dve_tmp.up("rt", ly, st, k) if s == 0 else dve_tmp.up()))
                    if k not in pool_adds:
                        dve.wait_ge(*dve_tmp.ago())
                        if reload:
                            dve.wait_ge(x_loaded[k], reload)
                        v.tensor_tensor(x[:, k, lo:T], x[:, k, lo:T], norm_tile(k)[:, lo:T], ALU.add).then_inc(
                            *dve_tmp.up("x", ly, st, k))
                noted[("free", "spread", ly, st)] = noted[("rt", ly, st, KT - 1)]

            def modulation(ly, g):
                m = mod[:, ly, 8 * g:8 * g + 8, :]
                b = vec[:, ly, V_BADA + 8 * g:V_BADA + 8 * g + 8]
                first = ly == 0 and g < 2
                if first:
                    dve.wait_ge(*seen("ada", 8 * g + 7))
                src = DD[:, 0:16].rearrange("p (t s) -> p t s", s=2) if first else m
                for s in range(2):
                    ins = v.tensor_tensor(m[:, :, s], src[:, :, s], b, ALU.add)
                    ins.then_inc(*(dve_out.up("free", "ada", ly, g) if s else dve_out.up()))
                dve.wait_ge(*dve_out.ago())
                if g in (0, 3):
                    return
                which, col = {1: (0, V_GPRE1), 2: (1, V_GPOST1), 4: (2, V_GPRE2), 5: (3, V_GPOST2)}[g]
                for s in range(2):
                    gv = vec[:, ly, col:col + KT]
                    if g in (1, 4):
                        ins = v.scalar_tensor_tensor(out=gain[:, ly, which, :, s], in0=m[:, :, s], scalar=1.0,
                                                     in1=gv, op0=ALU.add, op1=ALU.mult)
                    else:
                        ins = v.tensor_tensor(gain[:, ly, which, :, s], m[:, :, s], gv, ALU.mult)
                    ins.then_inc(*dve_tmp.up())
                dve.wait_ge(*dve_tmp.ago())

            def ada_step(*step):
                if step not in ADA_STEPS:
                    return
                for k in (ADA_STEPS[step][0], ADA_STEPS[step][0] + 1):
                    dve.wait_ge(ada_loaded[k % 2], 16 * (k // 2 + 1))
                    for s in range(2):
                        link(v.tensor_tensor_reduce(out=OD, in0=ada_raw[:, k % 2, :], in1=c_row[:, s, :],
                                                    scale=1.0, scalar=0.0, op0=ALU.mult, op1=ALU.add,
                                                    accum_out=mod[:, k // ADA, k % ADA, s:s + 1]),
                             ada_dot, *(("ada", k) if s else ()))
                    if k % KT == KT - 1:
                        modulation(k // ADA, k % ADA // KT)

            dve.wait_ge(*seen("ctanh"))
            link(v.scalar_tensor_tensor(out=silu_c[:].rearrange("p a b -> p (a b)"),
                                        in0=silu_c[:].rearrange("p a b -> p (a b)"), scalar=1.0,
                                        in1=cvec[:].rearrange("p a b -> p (a b)"), op0=ALU.add, op1=ALU.mult),
                 dve_tmp)
            link(v.tensor_scalar(silu_c[:].rearrange("p a b -> p (a b)"),
                                 silu_c[:].rearrange("p a b -> p (a b)"), 0.5, None, ALU.mult), dve_tmp, "silu")
            modulation(0, 0)
            modulation(0, 1)
            variance("pre1", 0, TT, D, 0, "pre1")

            for ly in range(LAYERS):
                s0 = ly * SLABS
                lo = lo_of(ly)
                cols, full = chunks(lo), chunks(0)
                normalise(ly, "pre1", 0, 0, 0)

                for n, name in enumerate(["k", "v", "q0", "q1", "q2", "q3"]):
                    l0 = 0 if name in "kv" else lo
                    if name == "v":
                        dve.wait_ge(*seen("vh", ly))
                        v.tensor_tensor(vl[:].rearrange("p a b -> p (a b)"), at(B, 0, T),
                                        vh[:].rearrange("p a b -> p (a b)"), ALU.subtract).then_inc(
                            *dve_lo.up("free", "vt", ly))
                        noted[("tile", ly, "v")] = noted[("free", "vt", ly)]
                        continue
                    dve.wait_ge(*seen("rot", ly, name))
                    if name == "k":
                        variance("k", 0, 2 * TT, HD, ly, "k")
                    v.tensor_tensor(t3[:, l0:T], at(OD, l0, T), sin[:, l0:T], ALU.mult).then_inc(
                        *dve_out.up("free", "rot", ly, name))
                    link(v.tensor_tensor(t2[:, l0:T], t2[:, l0:T], cos[:, l0:T], ALU.mult), dve_tmp)
                    dve.wait_ge(*dve_out.ago())
                    link(v.tensor_tensor(t2[:, l0:T], t2[:, l0:T], t3[:, l0:T], ALU.add), dve_tmp,
                         *(() if name == "k" else ("roped", ly, name)))
                    if name == "k":
                        dve.wait_ge(*seen("spread", ly, name))
                        link(v.tensor_tensor(t2[:, 0:T], t2[:, 0:T], at(B, 0, T), ALU.mult), dve_tmp,
                             "roped", ly, name)
                        noted[("free", "spread", ly, name)] = noted[("roped", ly, name)]
                    dve.wait_ge(*seen("hi", ly, name))
                    for a in range(2):
                        if name == "k":
                            for p in range(2):
                                ins = v.tensor_tensor(kk[64 * p:64 * p + 64, 2 * a + 1, :], t2[64 * a:64 * a + 64, 0:T],
                                                      kk[64 * a:64 * a + 64, 2 * a, :], ALU.subtract)
                                ins.then_inc(*(dve_lo.up("tile", ly, name) if a and p else dve_lo.up()))
                        else:
                            j = int(name[1])
                            ins = v.tensor_tensor(qs[64 - 64 * a:128 - 64 * a, 2 * j + a, l0:T],
                                                  t2[64 * a:64 * a + 64, l0:T],
                                                  qs[64 * a:64 * a + 64, 2 * j + a, l0:T], ALU.subtract)
                            ins.then_inc(*(dve_lo.up("tile", ly, name) if a else dve_lo.up()))

                noted[("stat", ly, "q")] = noted[("stat", ly, "q3")]
                t0 = lo // P
                variance("q", t0 * HEADS, (TT - t0) * HEADS, HD, ly, "q")

                us = units(ly)
                for u in range(len(us) + 2):
                    if u < len(us):
                        h, q0, nk, q, nq, b = us[u]
                        c = u % 8
                        dve.wait_ge(*seen("scores", ly, u))
                        link(v.reduce_max(ust[:, 0, c:c + 1], at(A[u % 2], 0, nk), AX.X), dve_tmp)
                        if u == 0:
                            dve.wait_ge(*seen("rs", ly, "q"))
                        v.tensor_scalar(ust[:, 1, c:c + 1], ust[:, 0, c:c + 1], q_scale(us[u]), -1.0,
                                        ALU.mult, ALU.mult).then_inc(*dve_tmp.up("negmax", ly, u))
                    if 1 <= u <= len(us):
                        h, q0, nk, q, nq, b = us[u - 1]
                        c = (u - 1) % 8
                        dve.wait_ge(*seen("free", "scores", ly, u - 1))
                        link(v.reciprocal(ust[:, 3, c:c + 1], ust[:, 2, c:c + 1]), dve_tmp)
                        v.tensor_scalar(pr[:, (u - 1) % 2, 0:nk], pr[:, (u - 1) % 2, 0:nk], ust[:, 3, c:c + 1],
                                        None, ALU.mult).then_inc(*dve_tmp.up("normed", ly, u - 1))
                    if u >= 2:
                        h, q0, nk, q, nq, b = us[u - 2]
                        dve.wait_ge(*seen("pth", ly, u - 2))
                        ph, pl = ((pt0h, pt0l), (pt1h, pt1l))[b % 2]
                        v.tensor_tensor(pl[:, 0:nk // P, q * P:(q + 1) * P],
                                        at(B, 0, nk).rearrange("p (k q) -> p k q", q=P),
                                        ph[:, 0:nk // P, q * P:(q + 1) * P], ALU.subtract).then_inc(
                            *dve_lo.up("free", "pt", ly, u - 2))
                for j in range(BR):
                    dve.wait_ge(*seen("oh", ly, j))
                    v.tensor_tensor(ol[:, j, lo:T], o_raw[:, j, lo:T], oh[:, j, lo:T], ALU.subtract).then_inc(
                        *dve_lo.up("ol", ly, j))

                a0 = 0 if lo == 0 else GL - HALF
                for p0, p1 in ([(0, GC)] if lo == 0 else []) + [(GL - HALF, GL), (GL + LAT, GW)]:
                    v.memset(cg[:, :, p0:p1], 0.0).then_inc(*dve_tmp.up())
                dve.wait_ge(*dve_tmp.ago())

                def tap(j, t, shift):
                    w = vec[:, ly, bass.ds(V_DW + j * TAPS + t, 1)]
                    src = cg[:, j, bass.ds(shift + a0, CW - a0)]
                    return v.scalar_tensor_tensor(out=cacc[:, j, a0:CW], in0=src, scalar=w,
                                                  in1=cacc[:, j, a0:CW], op0=ALU.mult, op1=ALU.add)

                FIRST = TAPS - 5 * (KT // 2)
                for j in range(BR):
                    dve.wait_ge(*seen("free", "cgate", ly, j))
                    dve.wait_ge(used, s0 + S_CONV + 2 * j + 2)
                    for c0, c1, s in cols:
                        g0 = GC if s else GL
                        ins = v.scalar_tensor_tensor(out=cg[:, j, g0:g0 + c1 - c0], in0=t1[:, c0:c1], scalar=1.0,
                                                     in1=at(A[1], c0, c1), op0=ALU.add, op1=ALU.mult)
                        ins.then_inc(*(dve_out.up() if s else dve_out.up("free", "cval", ly, j)))
                    dve.wait_ge(*dve_out.ago())
                    link(v.tensor_scalar(cacc[:, j, a0:CW], cg[:, j, a0:CW], vec[:, ly, V_DW + j * TAPS:V_DW + j * TAPS + 1],
                                         None, ALU.mult), dve_tap)
                    for t in range(1, FIRST):
                        link(tap(j, t, t), dve_tap)

                def merge(b, c, i):
                    dve.wait_ge(*(seen("free", "gate", ly, b, c, i=i) if b != 1 else seen("free", "gate", ly, b, i)))
                    s = s0 + (S_P0, S_P1, S_P2)[b]
                    dve.wait_ge(used, s + 2 * i + 2 if b == 1 else i * RING + (s + 2 * c + 2))
                    tt = (t1, t3)[c]
                    dst = acc[:, i, lo:T] if b == 1 else acc[:, bass.ds(i * 2 + c, 1), lo:T].rearrange(
                        "p a t -> p (a t)")
                    name = ("free", "value", ly, b) + ((i,) if b == 1 else (c,))
                    if b == 0:
                        v.scalar_tensor_tensor(out=dst, in0=tt[:, lo:T], scalar=1.0, in1=at(A[1], lo, T),
                                               op0=ALU.add, op1=ALU.mult).then_inc(*dve_out.up(*name))
                        return
                    link(v.scalar_tensor_tensor(out=t2[:, lo:T], in0=tt[:, lo:T], scalar=1.0, in1=at(A[1], lo, T),
                                                op0=ALU.add, op1=ALU.mult), dve_out, *name)
                    link(v.tensor_tensor(dst, dst, t2[:, lo:T], ALU.add), dve_tmp,
                         *(("macc", ly, c) if b == 2 else ()))
                    if b == 2:
                        dve.wait_ge(*seen("mh", ly, c, i=i))
                        f = bass.ds(i * 2 + c, 1)
                        v.tensor_tensor(ml[:, f, lo:T].rearrange("p a t -> p (a t)"), dst,
                                        mh[:, f, lo:T].rearrange("p a t -> p (a t)"), ALU.subtract).then_inc(
                            *dve_lo.up("ml", ly, c))

                with repeat(dve, KT // 2, ly, "branch", 0) as i:
                    for c in range(2):
                        merge(0, c, i)
                        for t in range(3 - c):
                            for j in range(BR):
                                dve.wait_ge(*dve_tap.ago(BR - 1))
                                shift = i * 5 + (FIRST + 3 * c + t)
                                tap(j, shift, shift).then_inc(*dve_tap.up())
                dve.wait_ge(*dve_tap.ago())
                dve.wait_ge(*dve_out.ago())
                link(v.memset(t1[:, UC + CTX:UL], 0.0), dve_tmp, "taps", ly)

                if ly == 0:
                    for n in range(2):
                        dve.wait_ge(*seen("c_tanh", n))
                        link(v.scalar_tensor_tensor(out=c_row[:, n, :], in0=OD, scalar=1.0, in1=c_row[:, n, :],
                                                    op0=ALU.add, op1=ALU.mult), dve_tmp, "c_silu", n)
                        link(v.tensor_scalar(c_row[:, n, :], c_row[:, n, :], 0.5, None, ALU.mult), dve_tmp)

                if lo == 0:
                    v.memset(t1[:, 0:UC], 0.0).then_inc(*dve_tmp.up())
                link(v.memset(t1[:, UL + LAT:UW], 0.0), dve_tmp, "pads", ly)
                b0 = 0 if lo == 0 else UL - 8
                for n, (kind, g) in enumerate(POOL_ORDER):
                    if kind == "w":
                        dve.wait_ge(*seen("yph", ly, g))
                        v.scalar_tensor_tensor(out=ypl[:, g, lo:T], in0=at(A[1], lo, T),
                                               scalar=vec[:, ly, V_PS + g:V_PS + g + 1], in1=yph[:, g, lo:T],
                                               op0=ALU.mult, op1=ALU.subtract).then_inc(
                            *dve_lo.up("free", "pout", ly, g))
                        noted[("ypl", ly, g)] = noted[("free", "pout", ly, g)]
                        continue
                    dve.wait_ge(*seen("free", "pin", ly, g))
                    link(v.tensor_tensor(t2[:, b0 + 1:UW], t1[:, b0:UW - 1], t1[:, b0 + 1:UW], ALU.add), dve_tmp)
                    src, e = t2, 1
                    for m in range(g):
                        sh = 1 << m
                        dst = (t3, t2)[m % 2]
                        e += sh
                        link(v.tensor_tensor(dst[:, b0 + e:UW - e + 1], src[:, b0 + e - sh:UW - e + 1 - sh],
                                             src[:, b0 + e + sh:UW - e + 1 + sh], ALU.add), dve_tmp)
                        src = dst
                    for c0, c1, s in cols:
                        u0 = UC if s else UL
                        for off, ecol in ((u0, 0), (u0 + c1 - c0 - 8, 8)):
                            e0 = C_EDGE + 16 * g + ecol
                            v.tensor_tensor(src[:, off:off + 8], src[:, off:off + 8], const[:, e0:e0 + 8],
                                            ALU.mult).then_inc(*dve_tmp.up())
                    dve.wait_ge(*dve_tmp.ago())
                    d = (t3, t2)[g % 2]
                    link(v.scalar_tensor_tensor(out=d[:, b0 + 8:UW - 8], in0=src[:, b0 + 8:UW - 8],
                                                scalar=1.0 / WIN[g], in1=t1[:, b0 + 8:UW - 8], op0=ALU.mult,
                                                op1=ALU.subtract), dve_tmp, "dev", ly, g)
                    dve.wait_ge(*seen("dh", ly, g))
                    for c0, c1, s in cols:
                        u0 = UC if s else UL
                        ins = v.tensor_tensor(dl[:, c0:c1], d[:, u0:u0 + c1 - c0], dh[:, c0:c1], ALU.subtract)
                        ins.then_inc(*(dve_lo.up() if s else dve_lo.up("dl", ly, g)))
                    dve.wait_ge(*dve_lo.ago())

                cy = [ct[:, j, lo:T] for j in range(BR)]
                ca = [cacc[:, j, lo:T] for j in range(BR)]

                def ln_sum():
                    dve.wait_ge(*seen("cy", ly, BR - 1))
                    link(v.tensor_tensor(ca[0], cy[0], cy[1], ALU.add), dve_tmp)
                    link(v.tensor_tensor(ca[0], ca[0], cy[2], ALU.add), dve_tmp)
                    link(v.tensor_tensor(ca[0], ca[0], cy[3], ALU.add), dve_tmp, "cysum", ly)

                def ln_centre():
                    dve.wait_ge(*seen("cmu", ly))
                    link(v.tensor_scalar(ca[1], at(B, lo, T), 1.0 / (BR * P), None, ALU.mult), dve_out,
                         "free", "cmu", ly)
                    for j in range(BR):
                        v.tensor_tensor(cy[j], cy[j], ca[1], ALU.subtract).then_inc(*dve_tmp.up("cc", ly, j))

                def ln_squares():
                    for j in range(BR):
                        dve.wait_ge(*seen("csq", ly, j))
                        ins = (v.tensor_copy(ca[0], ca[2]) if j == 0 else
                               v.tensor_tensor(ca[0], ca[0], ca[2 + j % 2], ALU.add))
                        link(ins, dve_tmp, "cqadd", ly, j)
                    noted[("cqsum", ly)] = noted[("cqadd", ly, BR - 1)]

                def ln_scale():
                    dve.wait_ge(*seen("spread", ly, "conv"))
                    for j in range(BR):
                        v.tensor_tensor(cy[j], cy[j], at(B, lo, T), ALU.mult).then_inc(*dve_tmp.up("cn", ly, j))
                    noted[("free", "spread", ly, "conv")] = noted[("cn", ly, BR - 1)]

                def ln_silu(j):
                    dve.wait_ge(*seen("cth", ly, j))
                    link(v.scalar_tensor_tensor(out=cy[j], in0=ca[2 + j % 2], scalar=1.0, in1=cy[j], op0=ALU.add,
                                                op1=ALU.mult), dve_tmp, "cm", ly, j)
                    dve.wait_ge(*seen("ych", ly, j))
                    v.scalar_tensor_tensor(out=ycl[:, j, lo:T], in0=cy[j], scalar=0.5, in1=ych[:, j, lo:T],
                                           op0=ALU.mult, op1=ALU.subtract).then_inc(*dve_lo.up("ycl", ly, j))

                for j in range(KT):
                    merge(1, j % 2, j)
                    if j == 0:
                        ln_sum()
                    elif j == 1:
                        ln_centre()
                    elif j == 2:
                        ln_squares()
                    elif j == 3:
                        variance("conv", lo // P, (T - lo) // P, BR * P, ly, "conv")
                    elif j == 4:
                        ln_scale()
                    elif j < 7:
                        ln_silu(2 * (j - 5))
                        ln_silu(2 * (j - 5) + 1)
                    ada_step(ly, "p1", j)
                with repeat(dve, KT // 2, ly, "branch", 2) as i:
                    for c in range(2):
                        merge(2, c, i)

                def y_add(st, j):
                    dve.wait_ge(*seen("ysq", ly, st, j))
                    ins = (v.tensor_copy(t3[:, lo:T], t1[:, lo:T]) if j == 0 else
                           v.tensor_tensor(t3[:, lo:T], t3[:, lo:T], (t1, t2)[j % 2][:, lo:T], ALU.add))
                    link(ins, dve_tmp, "yadd", ly, st, j)
                    if j == KT - 1:
                        noted[("ysum", ly, st)] = noted[("yadd", ly, st, j)]

                for j in range(KT):
                    y_add("post1", j)
                    ada_step(ly, "out", j)
                variance("post1", lo // P, (T - lo) // P, D, ly, "post1")
                residual(ly, "post1", lo, 1, 16 * (ly + 2))
                variance("pre2", lo // P, (T - lo) // P, D, ly, "pre2")
                normalise(ly, "pre2", lo, 2, 3 * KT)

                for g, nf in enumerate(GROUPS):
                    s = s0 + FF_IN[g]
                    with repeat(dve, nf // 2, ly, "ffin", g) as i:
                        for c in range(2):
                            f = bass.ds(i * 2 + c, 1)
                            dve.wait_ge(*seen("fth", ly, g, c, i=i))
                            link(v.scalar_tensor_tensor(out=t2[:, lo:T], in0=t1[:, lo:T], scalar=1.0,
                                                        in1=at(A[0], lo, T), op0=ALU.add, op1=ALU.mult),
                                 dve_out, "free", "ffa", ly, g, c)
                            dve.wait_ge(used, i * RING + (s + 2 * c + 2))
                            link(v.scalar_tensor_tensor(out=t3[:, lo:T], in0=t2[:, lo:T], scalar=0.5,
                                                        in1=at(A[1], lo, T), op0=ALU.mult, op1=ALU.mult),
                                 dve_out, "free", "ffb", ly, g, c)
                            dve.wait_ge(*seen("midh", ly, g, c, i=i))
                            v.tensor_tensor(midl[:, f, lo:T].rearrange("p a t -> p (a t)"), t3[:, lo:T],
                                            midh[:, f, lo:T].rearrange("p a t -> p (a t)"), ALU.subtract).then_inc(
                                *dve_lo.up("midl", ly, g, c))
                            dve.wait_ge(*dve_lo.ago())
                    for j in range(KT):
                        if g:
                            dve.wait_ge(used, s0 + FF_OUT[g] + j + 1)
                            link(v.tensor_tensor(acc[:, j, lo:T], acc[:, j, lo:T], at(A[j % 2], lo, T), ALU.add),
                                 dve_out, "free", "ffo", ly, g, j)
                        if g == 2:
                            y_add("post2", j)
                        else:
                            ada_step(ly, f"ffo{g}", j)
                variance("post2", lo // P, (T - lo) // P, D, ly, "post2")
                residual(ly, "post2", lo, 3, None)
                if ly == 0:
                    variance("pre1", 0, TT, D, 1, "pre1")

    return noted, strides


def program(nc, scratch, io):
    known = build(scratch[0], scratch[1], ({}, {}))
    build(nc, io, known)


def slabs_of(l, w_in, w_attn_o, pool_w, w_pool_o, w_conv_o, w_out, w_ffn_in, w_ffn_out, out):
    q_end, v_end = HEADS * HD, HEADS * HD + 2 * KV * HD
    p_end = v_end + BR * P
    g_end = p_end + 2 * BR * P

    def put(s, w, cols, k0=0, k1=KT):
        n = k1 - k0
        out[s, :, 0:n * P] = w[k0 * P:k1 * P, cols:cols + P].reshape(n, P, P).transpose(1, 0, 2).reshape(P, n * P)

    for n, c in ((S_K, q_end), (S_V, q_end + KV * HD)):
        put(n, w_in, c, 0, 4)
        put(n + 1, w_in, c, 4, 8)
    for j in range(BR):
        put(S_Q + j, w_in, j * P)
        put(S_CONV + 2 * j, w_in, p_end + (BR + j) * P)
        put(S_CONV + 2 * j + 1, w_in, p_end + j * P)
    for n, (kind, g) in enumerate(POOL_ORDER):
        if kind == "u":
            put(S_POOL + n, w_in, v_end + g * P)
        else:
            out[S_POOL + n, :, 0:P] = pool_w[g]
    for b, (s, w) in enumerate(((S_P0, w_attn_o), (S_P1, w_pool_o), (S_P2, w_conv_o))):
        for j in range(KT):
            put(s + 2 * j, w_in, g_end + b * D + j * P)
            put(s + 2 * j + 1, w, j * P, 0, BR)
    for j in range(KT):
        put(S_OUT + j, w_out, j * P)
    f0 = 0
    for g, nf in enumerate(GROUPS):
        for f in range(nf):
            put(FF_IN[g] + 2 * f, w_ffn_in, (f0 + f) * P)
            put(FF_IN[g] + 2 * f + 1, w_ffn_in, D_FF + (f0 + f) * P)
        for j in range(KT):
            put(FF_OUT[g] + j, w_ffn_out, j * P, f0, f0 + nf)
        f0 += nf


def constants():
    c = np.zeros((P, NC), np.float32)
    c[:, C_ID:C_ID + P] = np.eye(P)
    c[:, C_ONE:C_ONE + P] = 1
    for h in range(P // HD):
        c[h * HD:(h + 1) * HD, C_BLK + h * HD:C_BLK + (h + 1) * HD] = 1
    for m in range(P):
        if m % 32 < 16:
            c[m + 16, C_ROT + m] = -1
        else:
            c[m - 16, C_ROT + m] = 1
    for g, w in enumerate(WIN):
        for t in range(8):
            c[:, C_EDGE + 16 * g + t] = w / min(w, t + w // 2)
            c[:, C_EDGE + 16 * g + 8 + t] = w / min(w, (8 - t) + w // 2)
    n_freq = HD // 4
    inv = (1.0 / (np.float32(10000.0) ** (np.arange(n_freq, dtype=np.float32) / np.float32(n_freq)))).astype(np.float32)
    pos = np.arange(LAT)
    row, col = (pos // 64).astype(np.float32), (pos % 64).astype(np.float32)
    c[:, C_COS:C_COS + T] = 1
    for p in range(P):
        d = p % HD
        ang = (row if d < HD // 2 else col) * inv[d % n_freq]
        c[p, C_COS + CTX:C_COS + T] = np.cos(ang)
        c[p, C_SIN + CTX:C_SIN + T] = np.sin(ang)
    return c


def kernel(**inputs):
    from concourse.bacc import Bacc
    from concourse.bass_utils import run_bass_kernel_spmd

    a = {k: np.asarray(v) for k, v in inputs.items()}

    def fm(v):
        return v.T.reshape(-1, P, v.shape[0]).transpose(1, 0, 2)

    def fv(v):
        return v.reshape(-1, P).T

    w = np.zeros((LAYERS * SLABS, P, KT * P), np.float32)
    vec = np.zeros((P, LAYERS, NV), np.float32)
    ada = np.empty((LAYERS, ADA, P, KT * P), np.float32)
    for l in range(LAYERS):
        slabs_of(l, *(a[k][l] for k in ("w_in", "w_attn_o", "pool_w", "w_pool_o", "w_conv_o", "w_out",
                                        "w_ffn_in", "w_ffn_out")), w[l * SLABS:(l + 1) * SLABS])
        ada[l] = a["w_ada"][l].T.reshape(ADA, P, D)
        vec[:, l, V_BADA:V_BADA + ADA] = fv(a["b_ada"][l])
        for col, k in ((V_GPRE1, "g_pre1"), (V_GPOST1, "g_post1"), (V_GPRE2, "g_pre2"), (V_GPOST2, "g_post2"),
                       (V_PS, "pool_scale"), (V_CB, "conv_b"), (V_LG, "conv_ln_g"), (V_LB, "conv_ln_b")):
            m = fv(a[k][l])
            vec[:, l, col:col + m.shape[1]] = m
        for col, k in ((V_QN, "q_norm"), (V_KN, "k_norm")):
            for h in range(P // HD):
                vec[h * HD:(h + 1) * HD, l, col] = a[k][l]
        vec[:, l, V_DW:V_DW + BR * TAPS] = a["conv_dw"][l].T.reshape(BR, P, TAPS).transpose(1, 0, 2).reshape(P, -1)
    ada[0, :ADA_PE] = a["w_ada"][0].reshape(KT, P, ADA, P).transpose(2, 1, 0, 3).reshape(ADA, P, KT * P)[:ADA_PE]
    arrays = {
        "x": np.ascontiguousarray(fm(np.concatenate([a["ctx"][0], a["x"][0]], 0))),
        "c": np.ascontiguousarray(fm(np.stack([a["c"][0], a["c_ctx"]], 0))),
        "c_row": np.ascontiguousarray(np.broadcast_to(np.stack([a["c"][0], a["c_ctx"]], 0), (P, 2, D))),
        "w": w, "ada": ada, "vec": vec, "const": constants(),
    }

    def core():
        nc = Bacc("TRN2", target_bir_lowering=False, num_devices=1, dynamic_dma_scratch_size=1024)
        io = {k: nc.dram_tensor(f"in_{k}", v.shape, F32, kind="ExternalInput").ap() for k, v in arrays.items()}
        io["xs"] = nc.dram_tensor("x_between", (P, KT, T), F32).ap()
        io["out"] = nc.dram_tensor("out", (P, KT, LAT), F32, kind="ExternalOutput").ap()
        return nc, io

    nc, io = core()
    program(nc, core(), io)
    r = run_bass_kernel_spmd(nc, [{f"in_{k}": v for k, v in arrays.items()}], core_ids=[0])
    out = r.results[0]["out"]
    return out.transpose(1, 0, 2).reshape(D, LAT).T.reshape(1, LAT, D)
```

```python
from contextlib import ExitStack, contextmanager

import numpy as np
import concourse.bass as bass
from concourse import mybir

F32 = mybir.dt.float32
F32R = mybir.dt.float32r
ACT = mybir.ActivationFunctionType
ALU = mybir.AluOpType
AX = mybir.AxisListType

P = 128
D = 1024
KT = D // P
CTX, LAT = 256, 512
T = CTX + LAT
LAYERS = 2
HD = 64
HEADS = 8
KV = 2
EPS = 1e-6
BR = 4
TAPS = 31
HALF = TAPS // 2
WIN = (2, 4, 8, 16)
D_FF = 2816
FT = D_FF // P
GROUPS = (8, 8, 6)
RING = 4
RAW = 2
ADA = 48

S_KV, S_Q, S_CONV, S_P0, S_POOL, S_P1, S_P2, S_OUT, S_FF = 0, 4, 8, 16, 32, 40, 56, 72, 80
FF_IN, FF_OUT = [], []
_s = S_FF
for _n in GROUPS:
    FF_IN.append(_s)
    FF_OUT.append(_s + 2 * _n)
    _s += 2 * _n + KT
SLABS = _s
POOL_ORDER = (("u", 3), ("u", 2), ("w", 3), ("u", 1), ("w", 2), ("u", 0), ("w", 1), ("w", 0))

ADA_PE, ADA_START = KT, 2 * KT
ADA_SLOTS = 6
ADA_STEPS = {}
for _ly, _phase, _first, _width, _steps in (
        (0, "p1", S_P1, 2, KT), (0, "out", S_OUT, 1, KT - 2), (0, "ffo0", FF_OUT[0], 1, KT),
        (0, "ffo1", FF_OUT[1], 1, KT), (1, "p1", SLABS + S_P1, 2, 4), (1, "out", SLABS + S_OUT, 1, KT - 2)):
    for _j in range(_steps):
        ADA_STEPS[(_ly, _phase, _j)] = (ADA_START + 2 * len(ADA_STEPS), _first + _width * _j)
assert ADA_START + 2 * len(ADA_STEPS) == LAYERS * ADA

V_BADA, V_GPRE1, V_GPOST1, V_GPRE2, V_GPOST2 = 0, 48, 56, 64, 72
V_QN, V_KN, V_PS, V_DW = 80, 81, 82, 86
V_CB = V_DW + BR * TAPS
V_LG, V_LB = V_CB + BR, V_CB + 2 * BR
NV = V_LB + BR
C_ID, C_ONE, C_BLK, C_ROT, C_EDGE, C_COS, C_SIN = 0, 128, 256, 384, 512, 576, 576 + T
NC = C_SIN + T

TT = T // P
TOK = {"post1": 0, "post2": 0, "pre1": TT, "pre2": TT, "conv": 2 * TT, "k": 3 * TT, "q": 5 * TT}
NTOK = 5 * TT + TT * HEADS

GC, GL = HALF, HALF + CTX + HALF
GW = GL + LAT + HALF
CW = GW - 2 * HALF
UC, UL = 8, 8 + CTX + 8
UW = UL + LAT + 8


def slab_blocks(s):
    if S_P0 <= s < S_POOL or S_P1 <= s < S_OUT:
        return 4 if s % 2 else 8
    if S_POOL <= s < S_P1:
        return 1 if POOL_ORDER[s - S_POOL][0] == "w" else 8
    for g, n in enumerate(GROUPS):
        if FF_OUT[g] <= s < FF_OUT[g] + KT:
            return n
    return 8


def build(nc, io, known):
    noted, strides = {}, {}
    old_marks, old_strides = known

    class Tally:

        def __init__(self, name):
            self.name, self.sem, self.n = name, ctx.enter_context(nc.semaphore(name)), 0
            self.start, self.key, self.i = None, None, None
            tallies[name] = self

        def up(self, *name):
            self.n += 1
            if name:
                assert name not in noted, name
                noted[name] = (self.name, self.n, self.key)
            return self.sem, 1

        def ago(self, back=0):
            v = self.n - back
            if self.key is None:
                return self.sem, max(v, 1)
            return self.sem, self.i * old_strides.get((self.key, self.name), 0) + max(v, 1)

    tallies = {}

    def seen(*name, i=None, back=0):
        if name not in old_marks:
            assert not old_marks, name
            return tallies["rounded"].sem, 1
        tally, value, key = old_marks[name]
        if key is None or i is None:
            assert key is None or back == 0, name
            return tallies[tally].sem, value
        stride = old_strides[(key, tally)]
        return tallies[tally].sem, i * stride + (value - back * stride)

    @contextmanager
    def repeat(eng, count, *key):
        with eng.Fori(0, count) as i:
            for t in tallies.values():
                t.start = t.n
            mine = (eng_name[id(eng)],) + key
            for t in tallies.values():
                t.key, t.i = mine, i
            yield i
            for t in tallies.values():
                d = t.n - t.start
                strides[(mine, t.name)] = d
                t.n += d * (count - 1)
                t.key = t.i = None

    eng_name = {}

    ctx = ExitStack()
    with ctx:
        def sb(name, shape, dt=F32):
            return ctx.enter_context(nc.sbuf_tensor(name, [P] + shape, dt))

        def overlay(name, size, *layouts):
            out = []
            for layout in layouts:
                with ExitStack() as open_:
                    for n, shape, dt in layout:
                        out.append(open_.enter_context(nc.sbuf_tensor(n, [P] + shape, dt)))
            sb(name, [size // 4])
            return out

        x, pt0h, pt0l, cg, cacc, ct, ml = overlay(
            "region_x", 4 * BR * (GW + CW) + 32,
            [("x", [KT, T], F32)],
            [("pt0h", [6, LAT], F32R), ("pt0l", [6, LAT], F32R)],
            [("conv_in", [BR, GW], F32), ("conv_acc", [BR, CW], F32)],
            [("conv_norm", [BR, T], F32)],
            [("merged_l", [KT, T], F32R)])
        pt1h, pt1l, acc, ada_first = overlay(
            "region_acc", 4 * KT * T,
            [("pt1h", [6, LAT], F32R), ("pt1l", [6, LAT], F32R)],
            [("acc", [KT, T], F32)],
            [("ada_first", [ADA_SLOTS, KT * P], F32)])
        half = 4 * KT * T
        (qs, kk, vh, vl, pr, o_raw, pad1, oh, ol, yph, ypl, dh, dl, pad2, ych, ycl, mh, midh, midl,
         ns) = overlay(
            "region_m", 2 * half,
            [("q_split", [HEADS, T], F32R), ("k_split", [2 * KV, T], F32R), ("v_h", [6, P], F32R),
             ("v_l", [6, P], F32R), ("probs", [2, T], F32)],
            [("o_raw", [BR, 2 * T], F32)],
            [("pad1", [half // 4], F32), ("o_h", [BR, T], F32R), ("o_l", [BR, T], F32R)],
            [("pool_h", [BR, T], F32R), ("pool_l", [BR, T], F32R), ("dev_h", [T], F32R),
             ("dev_l", [T], F32R)],
            [("pad2", [half // 4], F32), ("conv_h", [BR, T], F32R), ("conv_l", [BR, T], F32R)],
            [("merged_h", [KT, T], F32R)],
            [("mid_h", [KT, T], F32R), ("mid_l", [KT, T], F32R)],
            [("norm_tmp", [7, T], F32)])
        hh, hl = sb("h_h", [KT, T], F32R), sb("h_l", [KT, T], F32R)
        raw = sb("w_raw", [RAW, KT * P])
        wh, wl = sb("w_h", [RING, KT * P], F32R), sb("w_l", [RING, KT * P], F32R)
        ada_raw = sb("ada_raw", [2, KT * P])
        t1, t2, t3 = (sb(n, [800]) for n in ("t1", "t2", "t3"))
        const = sb("const", [NC])
        vec = sb("vec", [LAYERS, NV])
        cvec, silu_c = sb("cvec", [KT, 2]), sb("silu_c", [KT, 2])
        c_row = sb("c_row", [2, D])
        mod = sb("mod", [LAYERS, ADA, 2])
        gain = sb("gain", [LAYERS, 4, KT, 2])
        ust = sb("unit_stats", [4, 16])
        token_rs = sb("token_rs", [NTOK])
        ps = ctx.enter_context(nc.psum_tensor("ps", [P, 8, 512], F32))
        psf = ps[:].rearrange("p b n -> p (b n)")
        A = [psf[:, 0:1024], psf[:, 1024:2048]]
        B = psf[:, 2048:3072]
        O = psf[:, 3072:3584]
        DD = psf[:, 3584:4096]
        OD, ODs = psf[:, 3072:4096], (O, DD)

        def token_sum(kind, c, n):
            c += 2048 if kind in ("post1", "post2", "conv") else 3072
            return psf[:, c:c + n]

        ident, ones = const[:, C_ID:C_ID + P], const[:, C_ONE:C_ONE + P]
        blk, rot = const[:, C_BLK:C_BLK + P], const[:, C_ROT:C_ROT + P]
        cos, sin = const[:, C_COS:C_COS + T], const[:, C_SIN:C_SIN + T]

        def sem(name):
            return ctx.enter_context(nc.semaphore(name))

        w_loaded = [sem(f"w_loaded{k}") for k in range(RAW)]
        ada_loaded = [sem(f"ada_loaded{k}") for k in range(2)]
        ada_first_loaded = [sem(f"ada_first_loaded{k}") for k in range(ADA_SLOTS)]
        const_loaded, c_row_loaded, x_stored, out_stored = (
            sem(n) for n in ("const_loaded", "c_row_loaded", "x_stored", "out_stored"))
        x_loaded = [sem(f"x_loaded{k}") for k in range(KT)]
        rounded, split, used = Tally("rounded"), sem("split"), sem("used")
        ada_sum = Tally("ada_sum")
        ada_dot = Tally("ada_dot")
        pe_done = Tally("pe_done")
        act_tmp = Tally("act_tmp")
        act_hi = Tally("act_hi")
        act_out = Tally("act_out")
        dve_tmp = Tally("dve_tmp")
        dve_lo = Tally("dve_lo")
        dve_out = Tally("dve_out")
        pool_norm = Tally("pool_norm")
        dve_tap = Tally("dve_tap")

        def lo_of(ly):
            return 0 if ly == 0 else CTX

        def chunks(lo):
            return ([(0, CTX, 1)] if lo == 0 else []) + [(CTX, T, 0)]

        def at(w, c0, c1):
            return w[:, 256 + c0:256 + c1]

        def units(ly):
            out, b = [], 0
            for h in range(HEADS):
                for q0, nq, nk in ([(CTX, 2, T), (CTX + 2 * P, 2, T)] + ([(0, 1, CTX)] if ly == 0 else [])):
                    out += [(h, q0, nk, q, nq, b) for q in range(nq)]
                    b += 1
            return out

        def first_tile(n):
            return n // 2 + ADA_PE * (n % 2)

        def value_steps(us):
            todo, out = [], {}
            for u in range(2, len(us) + 2):
                if us[u - 2][3] == us[u - 2][4] - 1:
                    parts = 1 if us[u - 2][2] == CTX else 2
                    todo += [(u - 2, part, parts) for part in range(parts)]
                n = 1 if u < len(us) + 1 else len(todo)
                out[u], todo = todo[:n], todo[n:]
            return out

        def q_tiles(unit):
            return 2 if unit[2] == CTX else 1

        def pt(b):
            h, l = ((pt0h, pt0l), (pt1h, pt1l))[b % 4 // 2]
            c = 2 * P * (b % 2)
            return h[:, :, c:c + 2 * P], l[:, :, c:c + 2 * P]

        def q_scale(unit):
            h, q0, nk, q, nq, b = unit
            c = TOK["q"] + (q0 // P + q) * HEADS + h
            return token_rs[:, c:c + HEADS * (q_tiles(unit) - 1) + 1:HEADS]

        def by_key_tile(ap, unit):
            if q_tiles(unit) == 1:
                return ap.rearrange("p (k q) -> p k q", q=P)
            return ap.rearrange("p (r k q) -> p k r q", k=CTX // P, q=P)

        def key_rows(ap, unit):
            h, q0, nk, q, nq, b = unit
            n = q_tiles(unit) * P
            out = ap[:, 0:nk // P, q * n:(q + 1) * n]
            return out if n == P else out.rearrange("p k (r q) -> p k r q", q=P)

        pool_adds, pool_lows = (1, 4), (1, 3, 5)

        def square(k):
            return ns[:, (0, 1, 4, 5)[k % 4]]

        def norm_tile(n):
            return ns[:, (2, 3, 6)[n % 3]]

        block = ctx.enter_context(nc.Block())

        @block.sync
        def _(sp):
            eng_name[id(sp)] = "sp"
            total = LAYERS * SLABS

            def load(s, blocks, i=None):
                if s >= RAW or i is not None:
                    sp.wait_ge(split, s - RAW + 1 if i is None else i * RING + (s - RAW + 1))
                src = io["w"][s] if i is None else io["w"][bass.ds(i * RING + s, 1)].rearrange(
                    "a p n -> (a p) n")
                sp.dma_start(raw[:, s % RAW, 0:blocks * P], src[:, 0:blocks * P]).then_inc(
                    w_loaded[s % RAW], 16)

            def load_ada(k):
                if k >= ADA_START + 2:
                    sp.wait_ge(*seen("ada", k - 2))
                sp.dma_start(ada_raw[:, k % 2, :], io["ada"][k // ADA, k % ADA]).then_inc(ada_loaded[k % 2], 16)

            def load_run(a, b):
                s = a
                while s < b:
                    pat = [slab_blocks((s + k) % SLABS) for k in range(RING)]
                    n = 0
                    while s % RING == 0 and s + RING * (n + 1) <= b and pat == [
                            slab_blocks((s + RING * n + k) % SLABS) for k in range(RING)]:
                        n += 1
                    if n >= 2 and s >= RAW:
                        with sp.Fori(0, n) as i:
                            for k in range(RING):
                                load(s + k, pat[k], i)
                        s += RING * n
                    else:
                        load(s, pat[0])
                        s += 1

            sp.dma_start(c_row[:], io["c_row"]).then_inc(c_row_loaded, 16)
            load(0, KT)
            load(1, KT)
            for n in range(ADA_START):
                if n == ADA_START // 2:
                    load(2, 4)
                    load(3, 4)
                if n >= ADA_SLOTS:
                    sp.wait_ge(*seen("ada", first_tile(n - ADA_SLOTS)))
                sp.dma_start(ada_first[:, n % ADA_SLOTS, :], io["ada"][0, first_tile(n)]).then_inc(
                    ada_first_loaded[n % ADA_SLOTS], 16)
            at_s = RING
            for k, slab in ADA_STEPS.values():
                stop = min(slab + RING + 1, total)
                load_run(at_s, stop)
                at_s = stop
                load_ada(k)
                load_ada(k + 1)
            load_run(at_s, total)

        @block.gpsimd
        def _(pool):
            eng_name[id(pool)] = "pool"

            def split_slab(s, i=None):
                pool.wait_ge(rounded.sem, s + 1 if i is None else i * RING + (s + 1))
                nc.gpsimd.tensor_tensor(wl[:, s % RING, :], raw[:, s % RAW, :], wh[:, s % RING, :],
                                        ALU.subtract).then_inc(split, 1)

            def split_run(a, b):
                n = (b - a) // RING
                if n:
                    with pool.Fori(0, n) as i:
                        for k in range(RING):
                            split_slab(a + k, i)
                for s in range(a + RING * n, b):
                    split_slab(s)

            def add_squares(ly, st, lo, k):
                pool.wait_ge(*seen("sq", ly, st, k))
                pool.wait_ge(*seen("sq", ly, st, k - 1))
                nc.gpsimd.tensor_tensor(square(k - 1)[:, lo:T], square(k - 1)[:, lo:T], square(k)[:, lo:T],
                                        ALU.add).then_inc(*pool_norm.up("sq2", ly, st, k - 1))

            def residual(ly, st, lo, reload, nxt=None):
                for k in range(KT):
                    if k in pool_adds:
                        if reload:
                            pool.wait_ge(x_loaded[k], reload)
                        pool.wait_ge(*seen("rt", ly, st, k))
                        nc.gpsimd.tensor_tensor(x[:, k, lo:T], x[:, k, lo:T], norm_tile(k)[:, lo:T], ALU.add).then_inc(
                            *pool_norm.up("x", ly, st, k))
                    if k % 2 and nxt:
                        add_squares(*nxt, lo, k)

            def lows(ly, st, lo):
                for k in pool_lows:
                    pool.wait_ge(*seen("hh", ly, st, k))
                    nc.gpsimd.tensor_tensor(hl[:, k, lo:T], norm_tile(k)[:, lo:T], hh[:, k, lo:T],
                                            ALU.subtract).then_inc(*pool_norm.up("hl", ly, st, k))

            split_run(0, 2)
            for k in range(1, KT, 2):
                add_squares(0, "pre1", 0, k)
            split_run(2, RING)
            lows(0, "pre1", 0)
            at_s = RING
            for ly in range(LAYERS):
                lo = lo_of(ly)
                stop = ly * SLABS + S_FF + RING - 1
                split_run(at_s, stop)
                residual(ly, "post1", lo, 16 * (ly + 2), (ly, "pre2"))
                lows(ly, "pre2", lo)
                at_s = min((ly + 1) * SLABS + RING, LAYERS * SLABS)
                split_run(stop, at_s)
                residual(ly, "post2", lo, None, (1, "pre1") if ly == 0 else None)
                if ly == 0:
                    lows(1, "pre1", 0)

        @block.tensor
        def _(pe):
            eng_name[id(pe)] = "pe"
            last_use = {}

            def take(w, *name):
                if w in last_use:
                    pe.wait_ge(*seen("free", *last_use[w]))
                last_use[w] = name

            def gemm(out, slabs, xh, xl, cols, i=None, k_ready=None):
                kt = 0
                n_k = sum(nb for _, nb in slabs)
                for s, nb in slabs:
                    pe.wait_ge(split, s + 1 if i is None else i * RING + (s + 1))
                    for b in range(nb):
                        if k_ready is not None:
                            pe.wait_ge(*k_ready(kt))
                        for n, (w, m) in enumerate(((wh, xh), (wh, xl), (wl, xh))):
                            for c0, c1, _ in cols:
                                ins = nc.tensor.matmul(
                                    at(out, c0, c1), w[:, s % RING, b * P:(b + 1) * P], m[:, kt, c0:c1],
                                    start=(kt == 0 and n == 0), stop=(kt == n_k - 1 and n == 2))
                        kt += 1
                    ins.then_inc(used, 1)

            def gemm_pair(outs, slabs, k_ready, cols, i=None):
                n_k, kt = sum(nb for _, _, nb in slabs), 0
                for sa, sb, nb in slabs:
                    pe.wait_ge(split, sb + 1 if i is None else i * RING + (sb + 1))
                    for b in range(nb):
                        pe.wait_ge(*k_ready(kt))
                        for out, s in zip(outs, (sa, sb)):
                            for n, (w, m) in enumerate(((wh, hh), (wh, hl), (wl, hh))):
                                for c0, c1, _ in cols:
                                    ins = nc.tensor.matmul(
                                        at(out, c0, c1), w[:, s % RING, b * P:(b + 1) * P], m[:, kt, c0:c1],
                                        start=(kt == 0 and n == 0), stop=(kt == n_k - 1 and n == 2))
                            if b == nb - 1:
                                ins.then_inc(used, 1)
                        kt += 1

            def shift_tile(k):
                n = 2 * k
                pe.wait_ge(ada_first_loaded[n % ADA_SLOTS], 16 * (n // ADA_SLOTS + 1))
                for b in range(KT):
                    ins = nc.tensor.matmul(DD[:, 2 * k:2 * k + 2],
                                           ada_first[:, n % ADA_SLOTS, b * P:(b + 1) * P],
                                           silu_c[:, b, :], start=(b == 0), stop=(b == KT - 1))
                ins.then_inc(*ada_sum.up("ada", k))

            def sums(mat, src, cols, need, *name, w="B"):
                take(w, *name)
                pe.wait_ge(*seen(*need))
                for c0, c1, _ in cols:
                    ins = nc.tensor.matmul(at(B if w == "B" else OD, c0, c1), mat, src(c0, c1), start=True, stop=True)
                ins.then_inc(*pe_done.up(*name))

            def token_sums(src, lo, kind, start=True, stop=True):
                for t in range(lo // P, TT):
                    first, last = t == lo // P, t == TT - 1
                    ins = nc.tensor.matmul(token_sum(kind, TOK[kind] + t, 1), src[:, t * P:(t + 1) * P], ones[:, 0:1],
                                           start=start and first, stop=stop and last)
                return ins

            def head_sums(src, lo, col, per_tile):
                for t in range(lo // P, TT):
                    c = col + t * per_tile
                    ins = nc.tensor.matmul(token_sum("q", c, 2), src[:, t * P:(t + 1) * P],
                                           blk[:, 0:P:HD], start=True, stop=True)
                return ins

            def spread(lo, kind, *name, heads=1):
                take("B", "spread", *name)
                pe.wait_ge(*seen("rs", *name))
                rows = P // heads
                for t in range(lo // P, TT):
                    for h in range(heads):
                        c = TOK[kind] + t * heads + h
                        ins = nc.tensor.matmul(at(B, t * P, (t + 1) * P)[h * rows:(h + 1) * rows],
                                               token_rs[:, c:c + 1].to_broadcast([P, rows]), ident,
                                               start=True, stop=True)
                ins.then_inc(*pe_done.up("spread", *name))

            def square_sum(ly, st, lo, k):
                pe.wait_ge(*seen("sq2", ly, st, k))
                ins = token_sums(square(k), lo, st, start=(k == 0), stop=(k == KT - 2))
                ins.then_inc(*pe_done.up("sqsum", ly, st, k))
                noted[("stat", ly, st)] = noted[("sqsum", ly, st, k)]

            def t_cols(t):
                return lambda c0, c1: t[:, c0:c1]

            pe.wait_ge(const_loaded, 16 * 3)
            pe.wait_ge(*seen("silu"))
            for k in range(0, KT, 2):
                shift_tile(k)
                shift_tile(k + 1)
                square_sum(0, "pre1", 0, k)
            pe.wait_ge(*seen("free", "ada", 0, 0))
            for ly in range(LAYERS):
                s0 = ly * SLABS
                lo = lo_of(ly)
                cols, full = chunks(lo), chunks(0)

                def pre_ready(k):
                    return seen("hl", ly, "pre1", k)

                if ly:
                    for k in range(0, KT, 2):
                        square_sum(ly, "pre1", 0, k)
                spread(0, "pre1", ly, "pre1")

                tiles = ["k", "v", "q0", "q1", "q2", "q3"]

                def finish(n):
                    c = full if n in "kv" else cols
                    if n == "v":
                        take("B", "vt", ly)
                        pe.wait_ge(*seen("vcopy", ly))
                        for k in range(6):
                            ins = nc.tensor.transpose(at(B, k * P, (k + 1) * P), t1[:, k * P:(k + 1) * P], ident)
                        ins.then_inc(*pe_done.up("vt", ly))
                    else:
                        pe.wait_ge(*seen("tsq", ly, n))
                        if "OD" in last_use:
                            pe.wait_ge(*seen("free", *last_use["OD"]))
                        col, per = (TOK["k"], 2) if n == "k" else (TOK["q"] + 2 * int(n[1]), HEADS)
                        head_sums(t1, c[0][0], col, per).then_inc(*pe_done.up("stat", ly, n))
                        sums(rot, t_cols(t2), c, ("free", "gemm", ly, n), "rot", ly, n, w="OD")
                        if n == "k":
                            spread(0, "k", ly, "k", heads=KV)

                for n, name in enumerate(tiles):
                    w = n % 2
                    take(w, "gemm", ly, name)
                    if name == "v":
                        s = s0 + S_KV
                        gemm_pair(A, [(s, s + 1, 4), (s + 2, s + 3, 4)], pre_ready, full)
                    elif name != "k":
                        gemm(A[w], [(s0 + S_Q + n - 2, 8)], hh, hl, cols)
                    if n:
                        finish(tiles[n - 1])
                take(0, "cgate", ly, 0)
                gemm(A[0], [(s0 + S_CONV, 8)], hh, hl, cols)
                finish(tiles[-1])
                take(1, "cval", ly, 0)
                gemm(A[1], [(s0 + S_CONV + 1, 8)], hh, hl, cols)

                us = units(ly)

                def scores(u):
                    h, q0, nk, q, nq, b = us[u]
                    take(u % 2, "scores", ly, u)
                    if u == 0:
                        pe.wait_ge(*seen("tile", ly, "k"))
                    if q == 0:
                        pe.wait_ge(*seen("tile", ly, f"q{h // 2}"))
                    pieces = ([(0, 0, CTX, 0), (0, CTX, T, CTX)] if nk == T else
                              [(r, 0, CTX, r * CTX) for r in range(2)])
                    for r, c0, c1, to in pieces:
                        for part in range(2):
                            t0 = q0 + (q + r) * P
                            ins = nc.tensor.matmul(
                                at(A[u % 2], to, to + c1 - c0), qs[:, h, t0:t0 + P],
                                kk[:, 2 * (h // 4) + part, c0:c1], start=(part == 0), stop=(part == 1))
                    ins.then_inc(*pe_done.up("scores", ly, u))

                def transposes(u):
                    h, q0, nk, q, nq, b = us[u]
                    take("B", "pt", ly, u)
                    pe.wait_ge(*seen("normed", ly, u))
                    for k in range(nk * q_tiles(us[u]) // P):
                        ins = nc.tensor.transpose(at(B, k * P, (k + 1) * P), pr[:, u % 2, k * P:(k + 1) * P], ident)
                    ins.then_inc(*pe_done.up("pt", ly, u))

                def values(u, part, parts):
                    h, q0, nk, q, nq, b = us[u]
                    if b == 0 and part == 0:
                        take("OD", "pvs", ly)
                        del last_use["OD"]
                    if part == 0:
                        take(("O", b % 2), "pv", ly, b)
                        if b == 0:
                            pe.wait_ge(*seen("tile", ly, "v"))
                        pe.wait_ge(*seen("free", "pt", ly, u))
                    ph, pl = pt(b)
                    d0 = HD * (h // 4)
                    share = nk // P // parts
                    for k in range(part * share, (part + 1) * share):
                        for n, (v, p) in enumerate(((vh, ph), (vh, pl), (vl, ph))):
                            ins = nc.tensor.matmul(ODs[b % 2][0:HD, 0:2 * P], v[:, k, d0:d0 + HD], p[:, k, :],
                                                   start=(k == 0 and n == 0), stop=(k == nk // P - 1 and n == 2))
                    if part == parts - 1:
                        ins.then_inc(*pe_done.up("pv", ly, b))

                scores(0)
                plan = value_steps(us)
                for u in range(len(us) + 2):
                    if u + 1 < len(us):
                        scores(u + 1)
                    if 1 <= u <= len(us):
                        transposes(u - 1)
                    for step in plan.get(u, ()):
                        values(*step)

                for j in range(1, BR):
                    s = s0 + S_CONV + 2 * j
                    take(0, "cgate", ly, j)
                    gemm(A[0], [(s, 8)], hh, hl, cols)
                    take(1, "cval", ly, j)
                    gemm(A[1], [(s + 1, 8)], hh, hl, cols)

                def branch(b, xh, xl, j, i=None, parity=0, ready=None):
                    s = s0 + (S_P0, S_P1, S_P2)[b] + (2 * j if i is None else 2 * parity)
                    gemm(A[0], [(s, 8)], hh, hl, cols, i)
                    if i is None:
                        take(1, "value", ly, b, j)
                    else:
                        pe.wait_ge(*seen("free", "value", ly, b, 1 - parity, i=i, back=1 - parity))
                    gemm(A[1], [(s + 1, 4)], xh, xl, cols, i, ready)

                def branch_loop(b, xh, xl, ready):
                    take(0, "gate", ly, b, 1)
                    take(1, "value", ly, b, 1)

                    def two(i, ready=None):
                        for c in range(2):
                            pe.wait_ge(*seen("free", "gate", ly, b, 1 - c, i=i, back=1 - c))
                            branch(b, xh, xl, None, i, c, None if c else ready)

                    two(0, ready)
                    with repeat(pe, KT // 2 - 1, ly, "branch", b) as i:
                        two(i + 1)

                branch_loop(0, oh, ol, lambda k: seen("ol", ly, k))
                pe.wait_ge(*seen("free", "gate", ly, 0, 1, i=KT // 2 - 1))
                pe.wait_ge(*seen("free", "value", ly, 0, 1, i=KT // 2 - 1))
                del last_use[0], last_use[1]

                for n, (kind, g) in enumerate(POOL_ORDER):
                    s = s0 + S_POOL + n
                    if kind == "u":
                        take(0, "pin", ly, g)
                        gemm(A[0], [(s, 8)], hh, hl, cols)
                    else:
                        take(1, "pout", ly, g)
                        gemm(A[1], [(s, 1)], dh[:].rearrange("p (a t) -> p a t", a=1),
                             dl[:].rearrange("p (a t) -> p a t", a=1), cols,
                             k_ready=lambda k: seen("dl", ly, g))

                for j in range(KT):
                    if j == 2:
                        sums(ones, lambda c0, c1: cacc[:, 0, c0:c1], cols, ("cysum", ly), "cmu", ly)
                    if j == 4:
                        pe.wait_ge(*seen("cqsum", ly))
                        token_sums(cacc[:, 0, :], lo, "conv").then_inc(*pe_done.up("stat", ly, "conv"))
                    if j == 5:
                        spread(lo, "conv", ly, "conv")
                    take(0, "gate", ly, 1, j)
                    branch(1, yph, ypl, j, ready=(lambda k: seen("ypl", ly, k)) if j == 0 else None)

                branch_loop(2, ych, ycl, lambda k: seen("ycl", ly, k))
                pe.wait_ge(*seen("free", "gate", ly, 2, 1, i=KT // 2 - 1))
                pe.wait_ge(*seen("free", "value", ly, 2, 1, i=KT // 2 - 1))
                del last_use[0], last_use[1]

                for j in range(KT):
                    take(j % 2, "out", ly, j)
                    gemm(A[j % 2], [(s0 + S_OUT + j, 8)], mh, ml, cols,
                         k_ready=(lambda k: seen("ml", ly, k % 2, i=k // 2)) if j == 0 else None)
                pe.wait_ge(*seen("ysum", ly, "post1"))
                token_sums(t3, lo, "post1").then_inc(*pe_done.up("stat", ly, "post1"))
                spread(lo, "post1", ly, "post1")
                for k in range(0, KT, 2):
                    square_sum(ly, "pre2", lo, k)
                spread(lo, "pre2", ly, "pre2")

                for k in range(2):
                    if k in last_use:
                        pe.wait_ge(*seen("free", *last_use.pop(k)))
                for g, nf in enumerate(GROUPS):
                    s = s0 + FF_IN[g]

                    def ff_in(i, ready=None):
                        if ready:
                            for name in ("ffa", "ffb"):
                                pe.wait_ge(*seen("free", name, ly, g, 1, i=i, back=1))
                            gemm_pair(A, [(s, s + 1, 8)], ready, cols, i)
                        for c in range(1 if ready else 0, 2):
                            pe.wait_ge(*seen("free", "ffa", ly, g, 1 - c, i=i, back=1 - c))
                            gemm(A[0], [(s + 2 * c, 8)], hh, hl, cols, i)
                            pe.wait_ge(*seen("free", "ffb", ly, g, 1 - c, i=i, back=1 - c))
                            gemm(A[1], [(s + 2 * c + 1, 8)], hh, hl, cols, i)

                    if g == 0:
                        ff_in(0, lambda k: seen("hl", ly, "pre2", k))
                    with repeat(pe, nf // 2 - (g == 0), ly, "ffin", g) as i:
                        ff_in(i + 1 if g == 0 else i)
                    pe.wait_ge(*seen("free", "ffa", ly, g, 1, i=nf // 2 - 1))
                    pe.wait_ge(*seen("free", "ffb", ly, g, 1, i=nf // 2 - 1))
                    s = s0 + FF_OUT[g]
                    for j in range(KT):
                        take(j % 2, "ffo", ly, g, j)
                        gemm(A[j % 2], [(s + j, nf)], midh, midl, cols,
                             k_ready=(lambda k: seen("midl", ly, g, k % 2, i=k // 2)) if j == 0 else None)
                    for k in range(2):
                        pe.wait_ge(*seen("free", *last_use.pop(k)))
                pe.wait_ge(*seen("ysum", ly, "post2"))
                token_sums(t3, lo, "post2").then_inc(*pe_done.up("stat", ly, "post2"))
                spread(lo, "post2", ly, "post2")

        @block.scalar
        def _(act):
            eng_name[id(act)] = "act"
            nxt = [0]
            total = LAYERS * SLABS

            def round_slab(s, i=None):
                nb = slab_blocks(s % SLABS) if s >= RING else 8
                if i is None:
                    act.wait_ge(w_loaded[s % RAW], 16 * (s // RAW + 1))
                    if s >= RING:
                        act.wait_ge(used, s - RING + 1)
                else:
                    act.wait_ge(w_loaded[s % RAW], i * (16 * RING // RAW) + 16 * (s // RAW + 1))
                    act.wait_ge(used, i * RING + (s - RING + 1))
                nc.scalar.activation(wh[:, s % RING, 0:nb * P], raw[:, s % RAW, 0:nb * P],
                                     ACT.Copy).then_inc(*rounded.up())

            def rounds(s):
                while nxt[0] <= min(s, total - 1):
                    round_slab(nxt[0])
                    nxt[0] += 1

            def result_of(s, i=None):
                if i is None:
                    rounds(s + RING - 1)
                else:
                    round_slab(s + RING - 1, i)
                act.wait_ge(used, s + 1 if i is None else i * RING + (s + 1))

            def sq_in(st, lo, x_ready, store=False):
                for k in range(KT):
                    act.wait_ge(*x_ready(k))
                    if store:
                        act.dma_start(io["xs"][:, k, :], x[:, k, :]).then_inc(x_stored, 16)
                    if k >= 4:
                        act.wait_ge(*seen("sqsum", *st, k // 2 * 2 - 4))
                    nc.scalar.activation(square(k)[:, lo:T], x[:, k, lo:T],
                                         ACT.Square).then_inc(*act_tmp.up("sq", *st, k))

            def root(kind, n, *name, scale=1.0):
                act.wait_ge(*seen("var", *name))
                buf = token_rs[:, TOK[kind]:TOK[kind] + n]
                nc.scalar.activation(buf, buf, ACT.Sqrt, scale=scale).then_inc(*act_tmp.up("rs", *name))

            def h_high(ly, st, lo, shift):
                for k in range(KT):
                    act.wait_ge(*seen("t", ly, st, k))
                    t = norm_tile(k)
                    for c0, c1, s in chunks(lo):
                        ins = nc.scalar.activation(t[:, c0:c1] if k in pool_lows else hh[:, k, c0:c1], t[:, c0:c1],
                                                   ACT.Identity, bias=mod[:, ly, shift + k, s:s + 1])
                        if k in pool_lows:
                            ins.then_inc(*act_tmp.up())
                    if k in pool_lows:
                        act.wait_ge(*act_tmp.ago())
                        ins = nc.scalar.activation(hh[:, k, lo:T], t[:, lo:T], ACT.Copy)
                    ins.then_inc(*act_hi.up("hh", ly, st, k))

            act.dma_start(cvec[:], io["c"]).then_inc(const_loaded, 16)
            act.dma_start(vec[:], io["vec"]).then_inc(const_loaded, 16)
            act.dma_start(const[:], io["const"]).then_inc(const_loaded, 16)
            for k in range(KT):
                act.dma_start(x[:, k, :], io["x"][:, k, :]).then_inc(x_loaded[k], 16)
            act.wait_ge(const_loaded, 16 * 3)
            nc.scalar.activation(silu_c[:], cvec[:], ACT.Tanh, scale=0.5).then_inc(*act_tmp.up("ctanh"))
            act.wait_ge(c_row_loaded, 16)
            for n in range(2):
                nc.scalar.activation(psf[:, 1024 * n:1024 * (n + 1)], c_row[:, n, :], ACT.Tanh, scale=0.5).then_inc(
                    *act_tmp.up("c_tanh", n))

            for ly in range(LAYERS):
                s0 = ly * SLABS
                lo = lo_of(ly)
                cols, full = chunks(lo), chunks(0)

                if ly == 0:
                    rounds(1)
                    sq_in((0, "pre1"), 0, lambda k: (x_loaded[k], 16))
                    rounds(RING - 1)
                root("pre1", TT, ly, "pre1")
                h_high(ly, "pre1", 0, 0)

                prev = None
                for n, name in enumerate(["k", "v", "q0", "q1", "q2", "q3"]):
                    w, l0 = A[n % 2], (0 if name in "kv" else lo)
                    result_of(s0 + (S_KV + 2, S_KV + 3, S_Q, S_Q + 1, S_Q + 2, S_Q + 3)[n])
                    if prev:
                        act.wait_ge(*seen("tile", ly, prev))
                    if name == "v":
                        nc.scalar.activation(t1[:, 0:T], at(w, 0, T), ACT.Copy).then_inc(
                            *act_out.up("free", "gemm", ly, name))
                        noted[("vcopy", ly)] = noted[("free", "gemm", ly, name)]
                        act.wait_ge(*seen("vt", ly))
                        nc.scalar.activation(vh[:].rearrange("p a b -> p (a b)"), at(B, 0, T),
                                             ACT.Copy).then_inc(*act_hi.up("vh", ly))
                    else:
                        nc.scalar.activation(t1[:, l0:T], at(w, l0, T), ACT.Square).then_inc(
                            *act_tmp.up("tsq", ly, name))
                        gcol = V_KN if name == "k" else V_QN
                        nc.scalar.activation(t2[:, l0:T], at(w, l0, T), ACT.Copy,
                                             scale=vec[:, ly, gcol:gcol + 1]).then_inc(
                            *act_out.up("free", "gemm", ly, name))
                        if name == "k":
                            root("k", 2 * TT, ly, "k")
                        act.wait_ge(*seen("roped", ly, name))
                        if name == "k":
                            for kv in range(KV):
                                for p in range(2):
                                    ins = nc.scalar.activation(kk[64 * p:64 * p + 64, 2 * kv, :],
                                                               t2[64 * kv:64 * kv + 64, 0:T], ACT.Copy)
                        else:
                            j = int(name[1])
                            for p in range(2):
                                ins = nc.scalar.activation(qs[64 * p:64 * p + 64, 2 * j + p, l0:T],
                                                           t2[64 * p:64 * p + 64, l0:T], ACT.Copy)
                        ins.then_inc(*act_hi.up("hi", ly, name))
                    prev = name
                root("q", HEADS * TT, ly, "q", scale=1.0 / HD)
                result_of(s0 + S_CONV)
                act.wait_ge(*seen("stat", ly, "q3"))
                nc.scalar.activation(t1[:, lo:T], at(A[0], lo, T), ACT.Tanh, scale=0.5).then_inc(
                    *act_out.up("free", "cgate", ly, 0))
                result_of(s0 + S_CONV + 1)

                us = units(ly)
                act.wait_ge(*seen("tile", ly, "q3"))
                if ly:
                    act.wait_ge(x_stored, 16 * KT)

                def o_out(b, h, q0):
                    act.wait_ge(*seen("pv", ly, b))
                    p = 64 * (h % 2)
                    nc.scalar.activation(o_raw[p:p + 64, h // 2, q0:q0 + 2 * P], ODs[b % 2][0:HD, 0:2 * P],
                                         ACT.Copy).then_inc(*act_out.up("free", "pv", ly, b))

                plan = value_steps(us)
                for u in range(len(us) + 3):
                    if u < len(us):
                        h, q0, nk, q, nq, b = us[u]
                        act.wait_ge(*seen("negmax", ly, u))
                        if u >= 2:
                            act.wait_ge(*seen("pt", ly, u - 2))
                        n, c = q_tiles(us[u]), 2 * (u % 8)
                        for r in range(n):
                            nc.scalar.activation(pr[:, u % 2, r * nk:(r + 1) * nk],
                                                 at(A[u % 2], r * nk, (r + 1) * nk), ACT.Exp,
                                                 bias=ust[:, 1, c + r:c + r + 1], scale=q_scale(us[u])[:, r:r + 1],
                                                 accum_out=ust[:, 2, c + r:c + r + 1]).then_inc(
                                *(act_out.up("free", "scores", ly, u) if r == n - 1 else act_out.up()))
                    if 1 <= u <= len(us):
                        h, q0, nk, q, nq, b = us[u - 1]
                        act.wait_ge(*seen("pt", ly, u - 1))
                        if q == 0 and b >= 4:
                            act.wait_ge(*seen("pv", ly, b - 4))
                        ph = pt(b)[0]
                        nc.scalar.activation(key_rows(ph, us[u - 1]),
                                             by_key_tile(at(B, 0, nk * q_tiles(us[u - 1])), us[u - 1]),
                                             ACT.Copy).then_inc(*act_hi.up("pth", ly, u - 1))
                    for v, part, parts in plan.get(u - 1, ()):
                        if part == parts - 1:
                            h, q0, nk, q, nq, b = us[v]
                            o_out(b, h, q0)
                act.wait_ge(*act_out.ago())
                for j in range(BR):
                    nc.scalar.activation(oh[:, j, lo:T], o_raw[:, j, lo:T], ACT.Copy).then_inc(
                        *act_hi.up("oh", ly, j))

                for j in range(1, BR):
                    result_of(s0 + S_CONV + 2 * j)
                    act.wait_ge(*seen("free", "cval", ly, j - 1))
                    nc.scalar.activation(t1[:, lo:T], at(A[0], lo, T), ACT.Tanh, scale=0.5).then_inc(
                        *act_out.up("free", "cgate", ly, j))
                    result_of(s0 + S_CONV + 2 * j + 1)

                def branch_loop(b):
                    s = s0 + (S_P0, S_P2)[b // 2]
                    with repeat(act, KT // 2, ly, "branch", b) as i:
                        for c in range(2):
                            result_of(s + 2 * c, i)
                            act.wait_ge(*seen("free", "value", ly, b, c, i=i, back=1))
                            tt = (t1, t3)[c]
                            nc.scalar.activation(tt[:, lo:T], at(A[0], lo, T), ACT.Tanh, scale=0.5).then_inc(
                                *act_out.up("free", "gate", ly, b, c))
                            round_slab(s + 2 * c + 1 + RING - 1, i)
                            if b == 2:
                                act.wait_ge(*seen("macc", ly, c, i=i))
                                nc.scalar.activation(mh[:, bass.ds(i * 2 + c, 1), lo:T].rearrange("p a t -> p (a t)"),
                                                     acc[:, bass.ds(i * 2 + c, 1), lo:T].rearrange("p a t -> p (a t)"),
                                                     ACT.Copy).then_inc(*act_hi.up("mh", ly, c))
                    nxt[0] += RING * (KT // 2)

                act.wait_ge(*seen("free", "cval", ly, BR - 1))
                branch_loop(0)

                for n, (kind, g) in enumerate(POOL_ORDER):
                    result_of(s0 + S_POOL + n)
                    if kind == "u":
                        act.wait_ge(*(seen("dev", ly, g + 1) if g < BR - 1 else seen("pads", ly)))
                        for c0, c1, s in cols:
                            u0 = UC if s else UL
                            ins = nc.scalar.activation(t1[:, u0:u0 + c1 - c0], at(A[0], c0, c1), ACT.Copy)
                        ins.then_inc(*act_out.up("free", "pin", ly, g))
                        if g < BR - 1:
                            act.wait_ge(used, s0 + S_POOL + POOL_ORDER.index(("w", g + 1)) + 1)
                        act.wait_ge(*seen("dev", ly, g))
                        d = (t3, t2)[g % 2]
                        for c0, c1, s in cols:
                            u0 = UC if s else UL
                            ins = nc.scalar.activation(dh[:, c0:c1], d[:, u0:u0 + c1 - c0], ACT.Copy)
                        ins.then_inc(*act_hi.up("dh", ly, g))
                    else:
                        nc.scalar.activation(yph[:, g, lo:T], at(A[1], lo, T), ACT.Copy,
                                             scale=vec[:, ly, V_PS + g:V_PS + g + 1]).then_inc(
                            *act_hi.up("yph", ly, g))

                def ln_y():
                    act.wait_ge(*seen("taps", ly))
                    for j in range(BR):
                        for c0, c1, s in cols:
                            src = 0 if s else GL - GC
                            ins = nc.scalar.activation(ct[:, j, c0:c1], cacc[:, j, src:src + c1 - c0],
                                                       ACT.Identity, scale=0.5,
                                                       bias=vec[:, ly, V_CB + j:V_CB + j + 1])
                        ins.then_inc(*act_tmp.up("cy", ly, j))

                def ln_sq():
                    for j in range(BR):
                        act.wait_ge(*seen("cc", ly, j))
                        if j >= 2:
                            act.wait_ge(*seen("cqadd", ly, j - 2))
                        nc.scalar.activation(cacc[:, 2 + j % 2, lo:T], ct[:, j, lo:T], ACT.Square).then_inc(
                            *act_tmp.up("csq", ly, j))

                def ln_act(j):
                    act.wait_ge(*seen("cn", ly, j))
                    if j >= 2:
                        act.wait_ge(*seen("cm", ly, j - 2))
                    nc.scalar.activation(ct[:, j, lo:T], ct[:, j, lo:T], ACT.Identity,
                                         scale=vec[:, ly, V_LG + j:V_LG + j + 1],
                                         bias=vec[:, ly, V_LB + j:V_LB + j + 1]).then_inc(*act_tmp.up())
                    act.wait_ge(*act_tmp.ago())
                    nc.scalar.activation(cacc[:, 2 + j % 2, lo:T], ct[:, j, lo:T], ACT.Tanh,
                                         scale=0.5).then_inc(*act_tmp.up("cth", ly, j))
                    act.wait_ge(*seen("cm", ly, j))
                    nc.scalar.activation(ych[:, j, lo:T], ct[:, j, lo:T], ACT.Copy, scale=0.5).then_inc(
                        *act_hi.up("ych", ly, j))

                for j in range(KT):
                    result_of(s0 + S_P1 + 2 * j)
                    if j >= 2:
                        act.wait_ge(*seen("free", "value", ly, 1, j - 2))
                    tt = (t1, t3)[j % 2]
                    nc.scalar.activation(tt[:, lo:T], at(A[0], lo, T), ACT.Tanh, scale=0.5).then_inc(
                        *act_out.up("free", "gate", ly, 1, j))
                    result_of(s0 + S_P1 + 2 * j + 1)
                    if j == 0:
                        ln_y()
                    elif j == 2:
                        ln_sq()
                    elif j == 3:
                        root("conv", TT, ly, "conv")
                    elif j in (5, 6):
                        ln_act(2 * (j - 5))
                        ln_act(2 * (j - 5) + 1)

                branch_loop(2)

                def y_out(j, w, scale, st):
                    if j >= 2:
                        act.wait_ge(*seen("yadd", ly, st, j - 2))
                    nc.scalar.activation((t1, t2)[j % 2][:, lo:T], at(w, lo, T), ACT.Square,
                                         scale=scale).then_inc(*act_tmp.up("ysq", ly, st, j))
                    nc.scalar.activation(acc[:, j, lo:T], at(w, lo, T), ACT.Copy, scale=scale).then_inc(
                        *act_out.up("free", "out", ly, j))

                for j in range(KT):
                    result_of(s0 + S_OUT + j)
                    if j == 0:
                        act.wait_ge(*seen("ml", ly, 1, i=KT // 2 - 1))
                    y_out(j, A[j % 2], 0.5, "post1")
                for k in range(KT):
                    act.dma_start(x[:, k, lo:T], (io["x"] if ly == 0 else io["xs"])[:, k, lo:T]).then_inc(
                        x_loaded[k], 16)
                root("post1", TT, ly, "post1")
                sq_in((ly, "pre2"), lo, lambda k: seen("x", ly, "post1", k))
                root("pre2", TT, ly, "pre2")
                h_high(ly, "pre2", lo, 3 * KT)

                for g, nf in enumerate(GROUPS):
                    s = s0 + FF_IN[g]
                    with repeat(act, nf // 2, ly, "ffin", g) as i:
                        for c in range(2):
                            f = bass.ds(i * 2 + c, 1)
                            result_of(s + 2 * c, i)
                            act.wait_ge(*seen("free", "ffa", ly, g, 1 - c, i=i, back=1 - c))
                            nc.scalar.activation(t1[:, lo:T], at(A[0], lo, T), ACT.Tanh, scale=0.5).then_inc(
                                *act_tmp.up("fth", ly, g, c))
                            round_slab(s + 2 * c + 1 + RING - 1, i)
                            act.wait_ge(*seen("free", "ffb", ly, g, c, i=i))
                            nc.scalar.activation(midh[:, f, lo:T].rearrange("p a t -> p (a t)"), t3[:, lo:T],
                                                 ACT.Copy).then_inc(*act_hi.up("midh", ly, g, c))
                    nxt[0] += RING * (nf // 2)
                    for j in range(KT):
                        result_of(s0 + FF_OUT[g] + j)
                        if g == 0:
                            nc.scalar.activation(acc[:, j, lo:T], at(A[j % 2], lo, T), ACT.Copy).then_inc(
                                *act_out.up("free", "ffo", ly, g, j))
                        elif g == 2:
                            act.wait_ge(*seen("free", "ffo", ly, g, j))
                            if j >= 2:
                                act.wait_ge(*seen("yadd", ly, "post2", j - 2))
                            nc.scalar.activation((t1, t2)[j % 2][:, lo:T], acc[:, j, lo:T], ACT.Square).then_inc(
                                *act_tmp.up("ysq", ly, "post2", j))
                rounds(s0 + SLABS + RING - 1)
                root("post2", TT, ly, "post2")
                if ly == 0:
                    sq_in((1, "pre1"), 0, lambda k: seen("x", 0, "post2", k), store=True)
                else:
                    for k in range(KT):
                        act.wait_ge(*seen("x", ly, "post2", k))
                        act.dma_start(io["out"][:, k, :], x[:, k, CTX:T]).then_inc(out_stored, 16)
                    act.wait_ge(out_stored, 16 * KT)

        @block.vector
        def _(dve):
            eng_name[id(dve)] = "dve"
            v = nc.vector

            def link(ins, tally, *name):
                ins.then_inc(*tally.up(*name))
                dve.wait_ge(*tally.ago())

            def variance(kind, first, cols, n, *name):
                dve.wait_ge(*seen("stat", *name))
                c = TOK[kind] + first
                buf = token_rs[:, c:c + cols]
                link(v.tensor_scalar(buf, token_sum(kind, c, cols), 1.0 / n, EPS, ALU.mult, ALU.add), dve_tmp)
                link(v.reciprocal(buf, buf), dve_tmp, "var", *name)

            def normalise(ly, st, lo, which, shift):
                dve.wait_ge(*seen("spread", ly, st))

                def low(k):
                    dve.wait_ge(*seen("hh", ly, st, k))
                    for c0, c1, s in chunks(lo):
                        ins = v.scalar_tensor_tensor(out=hl[:, k, c0:c1], in0=norm_tile(k)[:, c0:c1],
                                                     scalar=mod[:, ly, shift + k, s:s + 1], in1=hh[:, k, c0:c1],
                                                     op0=ALU.add, op1=ALU.subtract)
                        ins.then_inc(*(dve_lo.up("hl", ly, st, k) if s == 0 else dve_lo.up()))

                for k in range(KT):
                    if k >= 3:
                        dve.wait_ge(*seen("hl", ly, st, k - 3))
                    for c0, c1, s in chunks(lo):
                        ins = v.scalar_tensor_tensor(
                            out=norm_tile(k)[:, c0:c1], in0=x[:, k, c0:c1],
                            scalar=gain[:, ly, which, k, s:s + 1], in1=at(B, c0, c1),
                            op0=ALU.mult, op1=ALU.mult)
                        ins.then_inc(*(dve_tmp.up("t", ly, st, k) if s == 0 else dve_tmp.up()))
                    if k and k - 1 not in pool_lows:
                        low(k - 1)
                noted[("free", "spread", ly, st)] = noted[("t", ly, st, KT - 1)]
                low(KT - 1)

            def residual(ly, st, lo, which, reload):
                dve.wait_ge(*seen("spread", ly, st))
                for k in range(KT):
                    if k >= 3:
                        dve.wait_ge(*seen("x", ly, st, k - 3))
                    for c0, c1, s in chunks(lo):
                        ins = v.scalar_tensor_tensor(
                            out=norm_tile(k)[:, c0:c1], in0=acc[:, k, c0:c1],
                            scalar=gain[:, ly, which, k, s:s + 1], in1=at(B, c0, c1),
                            op0=ALU.mult, op1=ALU.mult)
                        ins.then_inc(*(dve_tmp.up("rt", ly, st, k) if s == 0 else dve_tmp.up()))
                    if k not in pool_adds:
                        dve.wait_ge(*dve_tmp.ago())
                        if reload:
                            dve.wait_ge(x_loaded[k], reload)
                        v.tensor_tensor(x[:, k, lo:T], x[:, k, lo:T], norm_tile(k)[:, lo:T], ALU.add).then_inc(
                            *dve_tmp.up("x", ly, st, k))
                noted[("free", "spread", ly, st)] = noted[("rt", ly, st, KT - 1)]

            def modulation(ly, g):
                m = mod[:, ly, 8 * g:8 * g + 8, :]
                b = vec[:, ly, V_BADA + 8 * g:V_BADA + 8 * g + 8]
                first = ly == 0 and g == 0
                if first:
                    dve.wait_ge(*seen("ada", 8 * g + 7))
                src = DD[:, 0:16].rearrange("p (t s) -> p t s", s=2) if first else m
                for s in range(2):
                    ins = v.tensor_tensor(m[:, :, s], src[:, :, s], b, ALU.add)
                    ins.then_inc(*(dve_out.up("free", "ada", ly, g) if s else dve_out.up()))
                dve.wait_ge(*dve_out.ago())
                if g in (0, 3):
                    return
                which, col = {1: (0, V_GPRE1), 2: (1, V_GPOST1), 4: (2, V_GPRE2), 5: (3, V_GPOST2)}[g]
                for s in range(2):
                    gv = vec[:, ly, col:col + KT]
                    if g in (1, 4):
                        ins = v.scalar_tensor_tensor(out=gain[:, ly, which, :, s], in0=m[:, :, s], scalar=1.0,
                                                     in1=gv, op0=ALU.add, op1=ALU.mult)
                    else:
                        ins = v.tensor_tensor(gain[:, ly, which, :, s], m[:, :, s], gv, ALU.mult)
                    ins.then_inc(*dve_tmp.up())
                dve.wait_ge(*dve_tmp.ago())

            def ada_dots(k, tile, scratch):
                for s in range(2):
                    link(v.tensor_tensor_reduce(out=scratch, in0=tile, in1=c_row[:, s, :], scale=1.0, scalar=0.0,
                                                op0=ALU.mult, op1=ALU.add,
                                                accum_out=mod[:, k // ADA, k % ADA, s:s + 1]),
                         ada_dot, *(("ada", k) if s else ()))

            def ada_step(*step):
                if step not in ADA_STEPS:
                    return
                for k in (ADA_STEPS[step][0], ADA_STEPS[step][0] + 1):
                    dve.wait_ge(ada_loaded[k % 2], 16 * ((k - ADA_START) // 2 + 1))
                    ada_dots(k, ada_raw[:, k % 2, :], OD)
                    if k % KT == KT - 1:
                        modulation(k // ADA, k % ADA // KT)

            dve.wait_ge(*seen("ctanh"))
            link(v.scalar_tensor_tensor(out=silu_c[:].rearrange("p a b -> p (a b)"),
                                        in0=silu_c[:].rearrange("p a b -> p (a b)"), scalar=1.0,
                                        in1=cvec[:].rearrange("p a b -> p (a b)"), op0=ALU.add, op1=ALU.mult),
                 dve_tmp)
            link(v.tensor_scalar(silu_c[:].rearrange("p a b -> p (a b)"),
                                 silu_c[:].rearrange("p a b -> p (a b)"), 0.5, None, ALU.mult), dve_tmp, "silu")
            for n in range(2):
                dve.wait_ge(*seen("c_tanh", n))
                link(v.scalar_tensor_tensor(out=c_row[:, n, :], in0=psf[:, 1024 * n:1024 * (n + 1)], scalar=1.0,
                                            in1=c_row[:, n, :], op0=ALU.add, op1=ALU.mult), dve_tmp)
                link(v.tensor_scalar(c_row[:, n, :], c_row[:, n, :], 0.5, None, ALU.mult), dve_tmp)
            for k in range(ADA_PE, ADA_START):
                n = 2 * (k - ADA_PE) + 1
                dve.wait_ge(ada_first_loaded[n % ADA_SLOTS], 16 * (n // ADA_SLOTS + 1))
                ada_dots(k, ada_first[:, n % ADA_SLOTS, :], psf[:, 0:1024])
            variance("pre1", 0, TT, D, 0, "pre1")
            modulation(0, 1)
            modulation(0, 0)

            for ly in range(LAYERS):
                s0 = ly * SLABS
                lo = lo_of(ly)
                cols, full = chunks(lo), chunks(0)
                normalise(ly, "pre1", 0, 0, 0)

                for n, name in enumerate(["k", "v", "q0", "q1", "q2", "q3"]):
                    l0 = 0 if name in "kv" else lo
                    if name == "v":
                        dve.wait_ge(*seen("vh", ly))
                        v.tensor_tensor(vl[:].rearrange("p a b -> p (a b)"), at(B, 0, T),
                                        vh[:].rearrange("p a b -> p (a b)"), ALU.subtract).then_inc(
                            *dve_lo.up("free", "vt", ly))
                        noted[("tile", ly, "v")] = noted[("free", "vt", ly)]
                        continue
                    dve.wait_ge(*seen("rot", ly, name))
                    if name == "k":
                        variance("k", 0, 2 * TT, HD, ly, "k")
                    v.tensor_tensor(t3[:, l0:T], at(OD, l0, T), sin[:, l0:T], ALU.mult).then_inc(
                        *dve_out.up("free", "rot", ly, name))
                    link(v.tensor_tensor(t2[:, l0:T], t2[:, l0:T], cos[:, l0:T], ALU.mult), dve_tmp)
                    dve.wait_ge(*dve_out.ago())
                    link(v.tensor_tensor(t2[:, l0:T], t2[:, l0:T], t3[:, l0:T], ALU.add), dve_tmp,
                         *(() if name == "k" else ("roped", ly, name)))
                    if name == "k":
                        dve.wait_ge(*seen("spread", ly, name))
                        link(v.tensor_tensor(t2[:, 0:T], t2[:, 0:T], at(B, 0, T), ALU.mult), dve_tmp,
                             "roped", ly, name)
                        noted[("free", "spread", ly, name)] = noted[("roped", ly, name)]
                    dve.wait_ge(*seen("hi", ly, name))
                    for a in range(2):
                        if name == "k":
                            for p in range(2):
                                ins = v.tensor_tensor(kk[64 * p:64 * p + 64, 2 * a + 1, :], t2[64 * a:64 * a + 64, 0:T],
                                                      kk[64 * a:64 * a + 64, 2 * a, :], ALU.subtract)
                                ins.then_inc(*(dve_lo.up("tile", ly, name) if a and p else dve_lo.up()))
                        else:
                            j = int(name[1])
                            ins = v.tensor_tensor(qs[64 - 64 * a:128 - 64 * a, 2 * j + a, l0:T],
                                                  t2[64 * a:64 * a + 64, l0:T],
                                                  qs[64 * a:64 * a + 64, 2 * j + a, l0:T], ALU.subtract)
                            ins.then_inc(*(dve_lo.up("tile", ly, name) if a else dve_lo.up()))

                noted[("stat", ly, "q")] = noted[("stat", ly, "q3")]
                t0 = lo // P
                variance("q", t0 * HEADS, (TT - t0) * HEADS, HD, ly, "q")
                dve.wait_ge(*seen("free", "cgate", ly, 0))
                dve.wait_ge(used, s0 + S_CONV + 2)
                v.scalar_tensor_tensor(out=t3[:, lo:T], in0=t1[:, lo:T], scalar=1.0, in1=at(A[1], lo, T),
                                       op0=ALU.add, op1=ALU.mult).then_inc(*dve_out.up("free", "cval", ly, 0))

                us = units(ly)
                for u in range(len(us) + 2):
                    if u < len(us):
                        h, q0, nk, q, nq, b = us[u]
                        n, c = q_tiles(us[u]), 2 * (u % 8)
                        dve.wait_ge(*seen("scores", ly, u))
                        link(v.reduce_max(ust[:, 0, c:c + n],
                                          at(A[u % 2], 0, n * nk).rearrange("p (r k) -> p r k", k=nk), AX.X), dve_tmp)
                        if u == 0:
                            dve.wait_ge(*seen("rs", ly, "q"))
                        v.scalar_tensor_tensor(out=ust[:, 1, c:c + n], in0=ust[:, 0, c:c + n], scalar=-1.0,
                                               in1=q_scale(us[u]), op0=ALU.mult, op1=ALU.mult).then_inc(
                            *dve_tmp.up("negmax", ly, u))
                    if 1 <= u <= len(us):
                        h, q0, nk, q, nq, b = us[u - 1]
                        n, c = q_tiles(us[u - 1]), 2 * ((u - 1) % 8)
                        dve.wait_ge(*seen("free", "scores", ly, u - 1))
                        link(v.reciprocal(ust[:, 3, c:c + n], ust[:, 2, c:c + n]), dve_tmp)
                        for r in range(n):
                            p_r = pr[:, (u - 1) % 2, r * nk:(r + 1) * nk]
                            v.tensor_scalar(p_r, p_r, ust[:, 3, c + r:c + r + 1], None, ALU.mult).then_inc(
                                *(dve_tmp.up("normed", ly, u - 1) if r == n - 1 else dve_tmp.up()))
                    if u >= 2:
                        h, q0, nk, q, nq, b = us[u - 2]
                        dve.wait_ge(*seen("pth", ly, u - 2))
                        ph, pl = pt(b)
                        v.tensor_tensor(key_rows(pl, us[u - 2]),
                                        by_key_tile(at(B, 0, nk * q_tiles(us[u - 2])), us[u - 2]),
                                        key_rows(ph, us[u - 2]), ALU.subtract).then_inc(
                            *dve_lo.up("free", "pt", ly, u - 2))
                for j in range(BR):
                    dve.wait_ge(*seen("oh", ly, j))
                    v.tensor_tensor(ol[:, j, lo:T], o_raw[:, j, lo:T], oh[:, j, lo:T], ALU.subtract).then_inc(
                        *dve_lo.up("ol", ly, j))

                a0 = 0 if lo == 0 else GL - HALF
                for p0, p1 in ([(0, GC)] if lo == 0 else []) + [(GL - HALF, GL), (GL + LAT, GW)]:
                    v.memset(cg[:, :, p0:p1], 0.0).then_inc(*dve_tmp.up())
                dve.wait_ge(*dve_tmp.ago())

                def tap(j, t, shift):
                    w = vec[:, ly, bass.ds(V_DW + j * TAPS + t, 1)]
                    src = cg[:, j, bass.ds(shift + a0, CW - a0)]
                    return v.scalar_tensor_tensor(out=cacc[:, j, a0:CW], in0=src, scalar=w,
                                                  in1=cacc[:, j, a0:CW], op0=ALU.mult, op1=ALU.add)

                FIRST = TAPS - 5 * (KT // 2)
                for j in range(BR):
                    if j:
                        dve.wait_ge(*seen("free", "cgate", ly, j))
                        dve.wait_ge(used, s0 + S_CONV + 2 * j + 2)
                    for c0, c1, s in cols:
                        g0 = GC if s else GL
                        if j == 0:
                            v.tensor_copy(cg[:, j, g0:g0 + c1 - c0], t3[:, c0:c1]).then_inc(*dve_out.up())
                            continue
                        ins = v.scalar_tensor_tensor(out=cg[:, j, g0:g0 + c1 - c0], in0=t1[:, c0:c1], scalar=1.0,
                                                     in1=at(A[1], c0, c1), op0=ALU.add, op1=ALU.mult)
                        ins.then_inc(*(dve_out.up() if s else dve_out.up("free", "cval", ly, j)))
                    dve.wait_ge(*dve_out.ago())
                    link(v.tensor_scalar(cacc[:, j, a0:CW], cg[:, j, a0:CW], vec[:, ly, V_DW + j * TAPS:V_DW + j * TAPS + 1],
                                         None, ALU.mult), dve_tap)
                    for t in range(1, FIRST):
                        link(tap(j, t, t), dve_tap)

                def merge(b, c, i):
                    dve.wait_ge(*(seen("free", "gate", ly, b, c, i=i) if b != 1 else seen("free", "gate", ly, b, i)))
                    s = s0 + (S_P0, S_P1, S_P2)[b]
                    dve.wait_ge(used, s + 2 * i + 2 if b == 1 else i * RING + (s + 2 * c + 2))
                    tt = (t1, t3)[c]
                    dst = acc[:, i, lo:T] if b == 1 else acc[:, bass.ds(i * 2 + c, 1), lo:T].rearrange(
                        "p a t -> p (a t)")
                    name = ("free", "value", ly, b) + ((i,) if b == 1 else (c,))
                    if b == 0:
                        v.scalar_tensor_tensor(out=dst, in0=tt[:, lo:T], scalar=1.0, in1=at(A[1], lo, T),
                                               op0=ALU.add, op1=ALU.mult).then_inc(*dve_out.up(*name))
                        return
                    link(v.scalar_tensor_tensor(out=t2[:, lo:T], in0=tt[:, lo:T], scalar=1.0, in1=at(A[1], lo, T),
                                                op0=ALU.add, op1=ALU.mult), dve_out, *name)
                    link(v.tensor_tensor(dst, dst, t2[:, lo:T], ALU.add), dve_tmp,
                         *(("macc", ly, c) if b == 2 else ()))
                    if b == 2:
                        dve.wait_ge(*seen("mh", ly, c, i=i))
                        f = bass.ds(i * 2 + c, 1)
                        v.tensor_tensor(ml[:, f, lo:T].rearrange("p a t -> p (a t)"), dst,
                                        mh[:, f, lo:T].rearrange("p a t -> p (a t)"), ALU.subtract).then_inc(
                            *dve_lo.up("ml", ly, c))

                with repeat(dve, KT // 2, ly, "branch", 0) as i:
                    for c in range(2):
                        merge(0, c, i)
                        for t in range(3 - c):
                            for j in range(BR):
                                dve.wait_ge(*dve_tap.ago(BR - 1))
                                shift = i * 5 + (FIRST + 3 * c + t)
                                tap(j, shift, shift).then_inc(*dve_tap.up())
                dve.wait_ge(*dve_tap.ago())
                dve.wait_ge(*dve_out.ago())
                link(v.memset(t1[:, UC + CTX:UL], 0.0), dve_tmp, "taps", ly)

                if lo == 0:
                    v.memset(t1[:, 0:UC], 0.0).then_inc(*dve_tmp.up())
                link(v.memset(t1[:, UL + LAT:UW], 0.0), dve_tmp, "pads", ly)
                b0 = 0 if lo == 0 else UL - 8
                for n, (kind, g) in enumerate(POOL_ORDER):
                    if kind == "w":
                        dve.wait_ge(*seen("yph", ly, g))
                        v.scalar_tensor_tensor(out=ypl[:, g, lo:T], in0=at(A[1], lo, T),
                                               scalar=vec[:, ly, V_PS + g:V_PS + g + 1], in1=yph[:, g, lo:T],
                                               op0=ALU.mult, op1=ALU.subtract).then_inc(
                            *dve_lo.up("free", "pout", ly, g))
                        noted[("ypl", ly, g)] = noted[("free", "pout", ly, g)]
                        continue
                    dve.wait_ge(*seen("free", "pin", ly, g))
                    link(v.tensor_tensor(t2[:, b0 + 1:UW], t1[:, b0:UW - 1], t1[:, b0 + 1:UW], ALU.add), dve_tmp)
                    src, e = t2, 1
                    for m in range(g):
                        sh = 1 << m
                        dst = (t3, t2)[m % 2]
                        e += sh
                        link(v.tensor_tensor(dst[:, b0 + e:UW - e + 1], src[:, b0 + e - sh:UW - e + 1 - sh],
                                             src[:, b0 + e + sh:UW - e + 1 + sh], ALU.add), dve_tmp)
                        src = dst
                    for c0, c1, s in cols:
                        u0 = UC if s else UL
                        for off, ecol in ((u0, 0), (u0 + c1 - c0 - 8, 8)):
                            e0 = C_EDGE + 16 * g + ecol
                            v.tensor_tensor(src[:, off:off + 8], src[:, off:off + 8], const[:, e0:e0 + 8],
                                            ALU.mult).then_inc(*dve_tmp.up())
                    dve.wait_ge(*dve_tmp.ago())
                    d = (t3, t2)[g % 2]
                    link(v.scalar_tensor_tensor(out=d[:, b0 + 8:UW - 8], in0=src[:, b0 + 8:UW - 8],
                                                scalar=1.0 / WIN[g], in1=t1[:, b0 + 8:UW - 8], op0=ALU.mult,
                                                op1=ALU.subtract), dve_tmp, "dev", ly, g)
                    dve.wait_ge(*seen("dh", ly, g))
                    for c0, c1, s in cols:
                        u0 = UC if s else UL
                        ins = v.tensor_tensor(dl[:, c0:c1], d[:, u0:u0 + c1 - c0], dh[:, c0:c1], ALU.subtract)
                        ins.then_inc(*(dve_lo.up() if s else dve_lo.up("dl", ly, g)))
                    dve.wait_ge(*dve_lo.ago())

                cy = [ct[:, j, lo:T] for j in range(BR)]
                ca = [cacc[:, j, lo:T] for j in range(BR)]

                def ln_sum():
                    dve.wait_ge(*seen("cy", ly, BR - 1))
                    link(v.tensor_tensor(ca[0], cy[0], cy[1], ALU.add), dve_tmp)
                    link(v.tensor_tensor(ca[0], ca[0], cy[2], ALU.add), dve_tmp)
                    link(v.tensor_tensor(ca[0], ca[0], cy[3], ALU.add), dve_tmp, "cysum", ly)

                def ln_centre():
                    dve.wait_ge(*seen("cmu", ly))
                    link(v.tensor_scalar(ca[1], at(B, lo, T), 1.0 / (BR * P), None, ALU.mult), dve_out,
                         "free", "cmu", ly)
                    for j in range(BR):
                        v.tensor_tensor(cy[j], cy[j], ca[1], ALU.subtract).then_inc(*dve_tmp.up("cc", ly, j))

                def ln_squares():
                    for j in range(BR):
                        dve.wait_ge(*seen("csq", ly, j))
                        ins = (v.tensor_copy(ca[0], ca[2]) if j == 0 else
                               v.tensor_tensor(ca[0], ca[0], ca[2 + j % 2], ALU.add))
                        link(ins, dve_tmp, "cqadd", ly, j)
                    noted[("cqsum", ly)] = noted[("cqadd", ly, BR - 1)]

                def ln_scale():
                    dve.wait_ge(*seen("spread", ly, "conv"))
                    for j in range(BR):
                        v.tensor_tensor(cy[j], cy[j], at(B, lo, T), ALU.mult).then_inc(*dve_tmp.up("cn", ly, j))
                    noted[("free", "spread", ly, "conv")] = noted[("cn", ly, BR - 1)]

                def ln_silu(j):
                    dve.wait_ge(*seen("cth", ly, j))
                    link(v.scalar_tensor_tensor(out=cy[j], in0=ca[2 + j % 2], scalar=1.0, in1=cy[j], op0=ALU.add,
                                                op1=ALU.mult), dve_tmp, "cm", ly, j)
                    dve.wait_ge(*seen("ych", ly, j))
                    v.scalar_tensor_tensor(out=ycl[:, j, lo:T], in0=cy[j], scalar=0.5, in1=ych[:, j, lo:T],
                                           op0=ALU.mult, op1=ALU.subtract).then_inc(*dve_lo.up("ycl", ly, j))

                for j in range(KT):
                    merge(1, j % 2, j)
                    if j == 0:
                        ln_sum()
                    elif j == 1:
                        ln_centre()
                    elif j == 2:
                        ln_squares()
                    elif j == 3:
                        variance("conv", lo // P, (T - lo) // P, BR * P, ly, "conv")
                    elif j == 4:
                        ln_scale()
                    elif j < 7:
                        ln_silu(2 * (j - 5))
                        ln_silu(2 * (j - 5) + 1)
                    ada_step(ly, "p1", j)
                with repeat(dve, KT // 2, ly, "branch", 2) as i:
                    for c in range(2):
                        merge(2, c, i)

                def y_add(st, j):
                    dve.wait_ge(*seen("ysq", ly, st, j))
                    ins = (v.tensor_copy(t3[:, lo:T], t1[:, lo:T]) if j == 0 else
                           v.tensor_tensor(t3[:, lo:T], t3[:, lo:T], (t1, t2)[j % 2][:, lo:T], ALU.add))
                    link(ins, dve_tmp, "yadd", ly, st, j)
                    if j == KT - 1:
                        noted[("ysum", ly, st)] = noted[("yadd", ly, st, j)]

                for j in range(KT):
                    y_add("post1", j)
                    ada_step(ly, "out", j)
                variance("post1", lo // P, (T - lo) // P, D, ly, "post1")
                residual(ly, "post1", lo, 1, 16 * (ly + 2))
                variance("pre2", lo // P, (T - lo) // P, D, ly, "pre2")
                normalise(ly, "pre2", lo, 2, 3 * KT)

                for g, nf in enumerate(GROUPS):
                    s = s0 + FF_IN[g]
                    with repeat(dve, nf // 2, ly, "ffin", g) as i:
                        for c in range(2):
                            f = bass.ds(i * 2 + c, 1)
                            dve.wait_ge(*seen("fth", ly, g, c, i=i))
                            link(v.scalar_tensor_tensor(out=t2[:, lo:T], in0=t1[:, lo:T], scalar=1.0,
                                                        in1=at(A[0], lo, T), op0=ALU.add, op1=ALU.mult),
                                 dve_out, "free", "ffa", ly, g, c)
                            dve.wait_ge(used, i * RING + (s + 2 * c + 2))
                            link(v.scalar_tensor_tensor(out=t3[:, lo:T], in0=t2[:, lo:T], scalar=0.5,
                                                        in1=at(A[1], lo, T), op0=ALU.mult, op1=ALU.mult),
                                 dve_out, "free", "ffb", ly, g, c)
                            dve.wait_ge(*seen("midh", ly, g, c, i=i))
                            v.tensor_tensor(midl[:, f, lo:T].rearrange("p a t -> p (a t)"), t3[:, lo:T],
                                            midh[:, f, lo:T].rearrange("p a t -> p (a t)"), ALU.subtract).then_inc(
                                *dve_lo.up("midl", ly, g, c))
                            dve.wait_ge(*dve_lo.ago())
                    for j in range(KT):
                        if g:
                            dve.wait_ge(used, s0 + FF_OUT[g] + j + 1)
                            link(v.tensor_tensor(acc[:, j, lo:T], acc[:, j, lo:T], at(A[j % 2], lo, T), ALU.add),
                                 dve_out, "free", "ffo", ly, g, j)
                        if g == 2:
                            y_add("post2", j)
                        else:
                            ada_step(ly, f"ffo{g}", j)
                variance("post2", lo // P, (T - lo) // P, D, ly, "post2")
                residual(ly, "post2", lo, 3, None)
                if ly == 0:
                    variance("pre1", 0, TT, D, 1, "pre1")

    return noted, strides


def program(nc, scratch, io):
    known = build(scratch[0], scratch[1], ({}, {}))
    build(nc, io, known)


def slabs_of(l, w_in, w_attn_o, pool_w, w_pool_o, w_conv_o, w_out, w_ffn_in, w_ffn_out, out):
    q_end, v_end = HEADS * HD, HEADS * HD + 2 * KV * HD
    p_end = v_end + BR * P
    g_end = p_end + 2 * BR * P

    def put(s, w, cols, k0=0, k1=KT):
        n = k1 - k0
        out[s, :, 0:n * P] = w[k0 * P:k1 * P, cols:cols + P].reshape(n, P, P).transpose(1, 0, 2).reshape(P, n * P)

    for n, c in ((S_KV, q_end), (S_KV + 1, q_end + KV * HD)):
        put(n, w_in, c, 0, 4)
        put(n + 2, w_in, c, 4, 8)
    for j in range(BR):
        put(S_Q + j, w_in, j * P)
        put(S_CONV + 2 * j, w_in, p_end + (BR + j) * P)
        put(S_CONV + 2 * j + 1, w_in, p_end + j * P)
    for n, (kind, g) in enumerate(POOL_ORDER):
        if kind == "u":
            put(S_POOL + n, w_in, v_end + g * P)
        else:
            out[S_POOL + n, :, 0:P] = pool_w[g]
    for b, (s, w) in enumerate(((S_P0, w_attn_o), (S_P1, w_pool_o), (S_P2, w_conv_o))):
        for j in range(KT):
            put(s + 2 * j, w_in, g_end + b * D + j * P)
            put(s + 2 * j + 1, w, j * P, 0, BR)
    for j in range(KT):
        put(S_OUT + j, w_out, j * P)
    f0 = 0
    for g, nf in enumerate(GROUPS):
        for f in range(nf):
            put(FF_IN[g] + 2 * f, w_ffn_in, (f0 + f) * P)
            put(FF_IN[g] + 2 * f + 1, w_ffn_in, D_FF + (f0 + f) * P)
        for j in range(KT):
            put(FF_OUT[g] + j, w_ffn_out, j * P, f0, f0 + nf)
        f0 += nf


def constants():
    c = np.zeros((P, NC), np.float32)
    c[:, C_ID:C_ID + P] = np.eye(P)
    c[:, C_ONE:C_ONE + P] = 1
    for h in range(P // HD):
        c[h * HD:(h + 1) * HD, C_BLK + h * HD:C_BLK + (h + 1) * HD] = 1
    for m in range(P):
        if m % 32 < 16:
            c[m + 16, C_ROT + m] = -1
        else:
            c[m - 16, C_ROT + m] = 1
    for g, w in enumerate(WIN):
        for t in range(8):
            c[:, C_EDGE + 16 * g + t] = w / min(w, t + w // 2)
            c[:, C_EDGE + 16 * g + 8 + t] = w / min(w, (8 - t) + w // 2)
    n_freq = HD // 4
    inv = (1.0 / (np.float32(10000.0) ** (np.arange(n_freq, dtype=np.float32) / np.float32(n_freq)))).astype(np.float32)
    pos = np.arange(LAT)
    row, col = (pos // 64).astype(np.float32), (pos % 64).astype(np.float32)
    c[:, C_COS:C_COS + T] = 1
    for p in range(P):
        d = p % HD
        ang = (row if d < HD // 2 else col) * inv[d % n_freq]
        c[p, C_COS + CTX:C_COS + T] = np.cos(ang)
        c[p, C_SIN + CTX:C_SIN + T] = np.sin(ang)
    return c


def kernel(**inputs):
    from concourse.bacc import Bacc
    from concourse.bass_utils import run_bass_kernel_spmd

    a = {k: np.asarray(v) for k, v in inputs.items()}

    def fm(v):
        return v.T.reshape(-1, P, v.shape[0]).transpose(1, 0, 2)

    def fv(v):
        return v.reshape(-1, P).T

    w = np.zeros((LAYERS * SLABS, P, KT * P), np.float32)
    vec = np.zeros((P, LAYERS, NV), np.float32)
    ada = np.empty((LAYERS, ADA, P, KT * P), np.float32)
    for l in range(LAYERS):
        slabs_of(l, *(a[k][l] for k in ("w_in", "w_attn_o", "pool_w", "w_pool_o", "w_conv_o", "w_out",
                                        "w_ffn_in", "w_ffn_out")), w[l * SLABS:(l + 1) * SLABS])
        ada[l] = a["w_ada"][l].T.reshape(ADA, P, D)
        vec[:, l, V_BADA:V_BADA + ADA] = fv(a["b_ada"][l])
        for col, k in ((V_GPRE1, "g_pre1"), (V_GPOST1, "g_post1"), (V_GPRE2, "g_pre2"), (V_GPOST2, "g_post2"),
                       (V_PS, "pool_scale"), (V_CB, "conv_b"), (V_LG, "conv_ln_g"), (V_LB, "conv_ln_b")):
            m = fv(a[k][l])
            vec[:, l, col:col + m.shape[1]] = m
        for col, k in ((V_QN, "q_norm"), (V_KN, "k_norm")):
            for h in range(P // HD):
                vec[h * HD:(h + 1) * HD, l, col] = a[k][l]
        vec[:, l, V_DW:V_DW + BR * TAPS] = a["conv_dw"][l].T.reshape(BR, P, TAPS).transpose(1, 0, 2).reshape(P, -1)
    ada[0, :ADA_PE] = a["w_ada"][0].reshape(KT, P, ADA, P).transpose(2, 1, 0, 3).reshape(ADA, P, KT * P)[:ADA_PE]
    arrays = {
        "x": np.ascontiguousarray(fm(np.concatenate([a["ctx"][0], a["x"][0]], 0))),
        "c": np.ascontiguousarray(fm(np.stack([a["c"][0], a["c_ctx"]], 0))),
        "c_row": np.ascontiguousarray(np.broadcast_to(np.stack([a["c"][0], a["c_ctx"]], 0), (P, 2, D))),
        "w": w, "ada": ada, "vec": vec, "const": constants(),
    }

    def core():
        nc = Bacc("TRN2", target_bir_lowering=False, num_devices=1, dynamic_dma_scratch_size=1024)
        io = {k: nc.dram_tensor(f"in_{k}", v.shape, F32, kind="ExternalInput").ap() for k, v in arrays.items()}
        io["xs"] = nc.dram_tensor("x_between", (P, KT, T), F32).ap()
        io["out"] = nc.dram_tensor("out", (P, KT, LAT), F32, kind="ExternalOutput").ap()
        return nc, io

    nc, io = core()
    program(nc, core(), io)
    r = run_bass_kernel_spmd(nc, [{f"in_{k}": v for k, v in arrays.items()}], core_ids=[0])
    out = r.results[0]["out"]
    return out.transpose(1, 0, 2).reshape(D, LAT).T.reshape(1, LAT, D)
```
